# Optimizing a Trainium2 kernel written in Bass

```python
import jax, jax.numpy as jnp
from jax import lax
import numpy as np

D_MODEL = 1024
BATCH = 1
SEQ = 256
DEPTH = 1
DEC_BATCH = 1
DEC_SEQ = 1024
PAST_LEN = 512

GRID_W = 64
N_HEADS = 8
N_KV_HEADS = 2
HEAD_DIM = 128
ROPE_THETA = 10000.0
ROT_PAIRS_PER_AXIS = HEAD_DIM // 4
Q_BLOCK = 128
GLA_HEADS = 4
GLA_DK = (D_MODEL // 2) // GLA_HEADS
GLA_DV = D_MODEL // GLA_HEADS
GLA_GATE_RANK = 16
GLA_GATE_NORM = 16.0
GLA_CHUNK = 64
N_EXPERTS = 16
EC_CAPACITY_FACTOR = 2
D_FF_EXPERT = D_MODEL
EPS = 1e-6
ATTN_Q = N_HEADS * HEAD_DIM
ATTN_KV = N_KV_HEADS * HEAD_DIM
GLA_K = GLA_HEADS * GLA_DK
GLA_V = GLA_HEADS * GLA_DV
IN_WIDTHS = (ATTN_Q, ATTN_KV, ATTN_KV, GLA_K, GLA_K, GLA_V, GLA_V, GLA_GATE_RANK, GLA_GATE_RANK, 2 * D_MODEL)
D_IN = sum(IN_WIDTHS)

kernel_name = "hybrid_diffusion_gqa_gla_ec_step"

def rms_norm(x, g):
    xf = x.astype(jnp.float32)
    y = xf * lax.rsqrt(jnp.mean(xf * xf, axis=-1, keepdims=True) + EPS)
    return (y * g.astype(jnp.float32)).astype(x.dtype)

def rope_2d(T):
    rows = T // GRID_W
    r = jnp.repeat(jnp.arange(rows), GRID_W).astype(jnp.float32)
    col = jnp.tile(jnp.arange(GRID_W), rows).astype(jnp.float32)
    freqs = ROPE_THETA ** (-jnp.arange(ROT_PAIRS_PER_AXIS, dtype=jnp.float32) / ROT_PAIRS_PER_AXIS)
    ang = jnp.concatenate([r[:, None] * freqs, col[:, None] * freqs], axis=-1)
    return jnp.cos(ang)[:, None, :], jnp.sin(ang)[:, None, :]

def apply_rope(x, cos, sin):
    xf = x.astype(jnp.float32)
    x1, x2 = xf[..., 0::2], xf[..., 1::2]
    out = jnp.stack([x1 * cos - x2 * sin, x1 * sin + x2 * cos], axis=-1)
    return out.reshape(x.shape).astype(x.dtype)

def attend(q, k, v):
    B, T, H, hd = q.shape
    G = H // N_KV_HEADS
    nb = T // Q_BLOCK
    qb = q.reshape(B, nb, Q_BLOCK, N_KV_HEADS, G, hd).transpose(1, 0, 2, 3, 4, 5)
    scale = hd ** -0.5

    def one_block(qblk):
        s = jnp.einsum('bqkgd,blkd->bkgql', qblk, k).astype(jnp.float32) * scale
        p = jax.nn.softmax(s, axis=-1).astype(v.dtype)
        return jnp.einsum('bkgql,blkd->bqkgd', p, v)

    o = lax.map(one_block, qb)
    return o.transpose(1, 0, 2, 3, 4, 5).reshape(B, T, H * hd)

def gla_chunked(q, k, v, logg, s0):
    B, H, T, dk = q.shape
    dv = v.shape[-1]
    N = T // GLA_CHUNK
    f32 = jnp.float32
    rs = lambda a: a.astype(f32).reshape(B, H, N, GLA_CHUNK, a.shape[-1])
    q, k, v, logg = rs(q), rs(k), rs(v), rs(logg)
    b = jnp.cumsum(logg, axis=3)
    b_last = b[:, :, :, -1:, :]
    qe = q * jnp.exp(b)
    ke = k * jnp.exp(-b)
    kd = k * jnp.exp(b_last - b)
    A = jnp.einsum('bhnid,bhnjd->bhnij', qe, ke)
    tril = jnp.tril(jnp.ones((GLA_CHUNK, GLA_CHUNK), dtype=bool))
    A = jnp.where(tril, A, 0.0)
    o_intra = jnp.einsum('bhnij,bhnjv->bhniv', A, v)
    decay = jnp.exp(b_last[:, :, :, 0, :])
    kv_chunk = jnp.einsum('bhnjd,bhnjv->bhndv', kd, v)

    def step(S, xs):
        dec, kvc = xs
        return dec[..., None] * S + kvc, S

    s_final, s_before = lax.scan(step, s0.astype(f32),
                                 (jnp.moveaxis(decay, 2, 0), jnp.moveaxis(kv_chunk, 2, 0)))
    s_before = jnp.moveaxis(s_before, 0, 2)
    o_inter = jnp.einsum('bhnid,bhndv->bhniv', qe, s_before)
    return (o_intra + o_inter).reshape(B, H, T, dv), s_final

def ec_ffn(h, w_router, w1, w3, w2):
    B, T, D = h.shape
    n = B * T
    cap = (EC_CAPACITY_FACTOR * n) // N_EXPERTS
    xt = h.reshape(n, D)
    aff = jax.nn.softmax((xt @ w_router).astype(jnp.float32), axis=-1)
    top_v, top_i = lax.top_k(aff.T, cap)
    xs = jnp.take(xt, top_i, axis=0)
    hid = jax.nn.silu(jnp.einsum('ecd,edf->ecf', xs, w1)) * jnp.einsum('ecd,edf->ecf', xs, w3)
    ye = jnp.einsum('ecf,efd->ecd', hid, w2) * top_v[..., None].astype(h.dtype)
    out = jnp.zeros((n, D), h.dtype).at[top_i.reshape(-1)].add(ye.reshape(-1, D))
    return out.reshape(B, T, D)

def trunk_layer(x, mod, rope, ctx, lw):
    (g_pre_mix, g_post_mix, g_pre_ffn, g_post_ffn, w_in, g_q, g_k, w_gk2_f, b_gk_f,
     w_gk2_b, b_gk_b, g_gla, w_pa, w_pg, w_out, w_router, w1, w3, w2) = lw
    B, T, D = x.shape
    sh_m, sc_m, gt_m, sh_f, sc_f, gt_f = jnp.split(mod[:, None, :], 6, axis=-1)

    h = rms_norm(x, g_pre_mix) * (1.0 + sc_m) + sh_m
    proj = h @ w_in
    idx = np.cumsum(IN_WIDTHS)[:-1].tolist()
    q_a, k_a, v_a, q_g, k_g, v_g, r_g, gk_f, gk_b, gates = jnp.split(proj, idx, axis=-1)

    q_a = rms_norm(q_a.reshape(B, T, N_HEADS, HEAD_DIM), g_q)
    k_a = rms_norm(k_a.reshape(B, T, N_KV_HEADS, HEAD_DIM), g_k)
    v_a = v_a.reshape(B, T, N_KV_HEADS, HEAD_DIM)
    if rope is not None:
        q_a = apply_rope(q_a, *rope)
        k_a = apply_rope(k_a, *rope)
    if ctx is None:
        k_all, v_all = k_a, v_a
        s_f0 = jnp.zeros((B, GLA_HEADS, GLA_DK, GLA_DV), x.dtype)
        s_b0 = s_f0
    else:
        ck, cv, s_f0, s_b0 = ctx
        k_all = jnp.concatenate([ck.transpose(0, 2, 1, 3), k_a], axis=1)
        v_all = jnp.concatenate([cv.transpose(0, 2, 1, 3), v_a], axis=1)
    o_a = attend(q_a, k_all, v_all) @ w_pa

    heads = lambda a, d: a.reshape(B, T, GLA_HEADS, d).transpose(0, 2, 1, 3)
    qg = heads(q_g, GLA_DK) * (GLA_DK ** -0.5)
    kg = heads(k_g, GLA_DK)
    vg = heads(v_g, GLA_DV)
    lg_f = heads(jax.nn.log_sigmoid((gk_f @ w_gk2_f + b_gk_f).astype(jnp.float32)) / GLA_GATE_NORM, GLA_DK)
    lg_b = heads(jax.nn.log_sigmoid((gk_b @ w_gk2_b + b_gk_b).astype(jnp.float32)) / GLA_GATE_NORM, GLA_DK)
    o_f, s_f = gla_chunked(qg, kg, vg, lg_f, s_f0)
    flip = lambda a: jnp.flip(a, axis=2)
    o_b, s_b = gla_chunked(flip(qg), flip(kg), flip(vg), flip(lg_b), s_b0)
    o_g = (o_f + flip(o_b)).astype(x.dtype).transpose(0, 2, 1, 3)
    o_g = rms_norm(o_g, g_gla).reshape(B, T, GLA_V) * jax.nn.silu(r_g)
    o_g = o_g @ w_pg

    g_a, g_b = jnp.split(jax.nn.sigmoid(gates), 2, axis=-1)
    mix = (g_a * o_a + g_b * o_g) @ w_out
    x = x + gt_m * rms_norm(mix, g_post_mix)

    h = rms_norm(x, g_pre_ffn) * (1.0 + sc_f) + sh_f
    x = x + gt_f * rms_norm(ec_ffn(h, w_router, w1, w3, w2), g_post_ffn)

    ctx_out = (k_a.transpose(0, 2, 1, 3), v_a.transpose(0, 2, 1, 3),
               s_f.astype(x.dtype), s_b.astype(x.dtype))
    return x, ctx_out

def setup_inputs(seed: int = 0) -> dict:
    key = jax.random.key(seed)
    ks = jax.random.split(key, 40)
    nrm = lambda i, shape, s: jax.random.normal(ks[i], shape, jnp.float32) * s
    gain = lambda i, shape: 1.0 + nrm(i, shape, 0.05)
    L = DEPTH
    return {
        "x_prompt": nrm(0, (BATCH, SEQ, D_MODEL), 1.0),
        "x_sample": nrm(1, (DEC_BATCH, DEC_SEQ, D_MODEL), 1.0),
        "cache_k": nrm(2, (DEC_BATCH, L, N_KV_HEADS, PAST_LEN, HEAD_DIM), 1.0),
        "cache_v": nrm(3, (DEC_BATCH, L, N_KV_HEADS, PAST_LEN, HEAD_DIM), 1.0),
        "state_gla_fwd": nrm(4, (DEC_BATCH, L, GLA_HEADS, GLA_DK, GLA_DV), 0.5),
        "state_gla_bwd": nrm(5, (DEC_BATCH, L, GLA_HEADS, GLA_DK, GLA_DV), 0.5),
        "c": nrm(6, (DEC_BATCH, D_MODEL), 1.0),
        "c_ctx": nrm(7, (D_MODEL,), 1.0),
        "g_pre_mix": gain(8, (L, D_MODEL)),
        "g_post_mix": gain(9, (L, D_MODEL)),
        "g_pre_ffn": gain(10, (L, D_MODEL)),
        "g_post_ffn": gain(11, (L, D_MODEL)),
        "w_mod": nrm(12, (L, D_MODEL, 6 * D_MODEL), 0.5 * D_MODEL ** -0.5),
        "b_mod": nrm(13, (L, 6 * D_MODEL), 0.02),
        "w_in": nrm(14, (L, D_MODEL, D_IN), D_MODEL ** -0.5),
        "g_q": gain(15, (L, HEAD_DIM)),
        "g_k": gain(16, (L, HEAD_DIM)),
        "w_gk2_f": nrm(17, (L, GLA_GATE_RANK, GLA_K), GLA_GATE_RANK ** -0.5),
        "b_gk_f": nrm(18, (L, GLA_K), 0.1),
        "w_gk2_b": nrm(19, (L, GLA_GATE_RANK, GLA_K), GLA_GATE_RANK ** -0.5),
        "b_gk_b": nrm(20, (L, GLA_K), 0.1),
        "g_gla": gain(21, (L, GLA_DV)),
        "w_pa": nrm(22, (L, ATTN_Q, D_MODEL), ATTN_Q ** -0.5),
        "w_pg": nrm(23, (L, GLA_V, D_MODEL), GLA_V ** -0.5),
        "w_out": nrm(24, (L, D_MODEL, D_MODEL), D_MODEL ** -0.5),
        "w_router": nrm(25, (L, D_MODEL, N_EXPERTS), D_MODEL ** -0.5),
        "w1": nrm(26, (L, N_EXPERTS, D_MODEL, D_FF_EXPERT), D_MODEL ** -0.5),
        "w3": nrm(27, (L, N_EXPERTS, D_MODEL, D_FF_EXPERT), D_MODEL ** -0.5),
        "w2": nrm(28, (L, N_EXPERTS, D_FF_EXPERT, D_MODEL), D_FF_EXPERT ** -0.5),
    }

def reference(x_prompt, x_sample, cache_k, cache_v, state_gla_fwd, state_gla_bwd, c, c_ctx,
              g_pre_mix, g_post_mix, g_pre_ffn, g_post_ffn, w_mod, b_mod, w_in, g_q, g_k,
              w_gk2_f, b_gk_f, w_gk2_b, b_gk_b, g_gla, w_pa, w_pg, w_out, w_router, w1, w3, w2):
    rope = rope_2d(x_sample.shape[1])
    xp, xs = x_prompt, x_sample
    ks, vs, sfs, sbs = [], [], [], []
    for l in range(DEPTH):
        lw = (g_pre_mix[l], g_post_mix[l], g_pre_ffn[l], g_post_ffn[l], w_in[l], g_q[l], g_k[l],
              w_gk2_f[l], b_gk_f[l], w_gk2_b[l], b_gk_b[l], g_gla[l], w_pa[l], w_pg[l], w_out[l],
              w_router[l], w1[l], w3[l], w2[l])
        mod_ctx = jax.nn.silu(c_ctx)[None, :] @ w_mod[l] + b_mod[l]
        mod_lat = jax.nn.silu(c) @ w_mod[l] + b_mod[l]
        xp, (nk, nv, nsf, nsb) = trunk_layer(xp, mod_ctx, None, None, lw)
        ks.append(nk); vs.append(nv); sfs.append(nsf); sbs.append(nsb)
        ctx = (cache_k[:, l], cache_v[:, l], state_gla_fwd[:, l], state_gla_bwd[:, l])
        xs, _ = trunk_layer(xs, mod_lat, rope, ctx, lw)
    new_cache_k = jnp.stack(ks, axis=1)
    new_cache_v = jnp.stack(vs, axis=1)
    new_state_gla_fwd = jnp.stack(sfs, axis=1)
    new_state_gla_bwd = jnp.stack(sbs, axis=1)
    return (xp, xs, new_cache_k, new_cache_v, new_state_gla_fwd, new_state_gla_bwd)


_drawn_inputs = setup_inputs


def setup_inputs(seed=0):
    import zlib

    import numpy as np

    out = dict(_drawn_inputs(seed))
    spreads = {}
    factors = {'state_gla_fwd': 8.0, 'state_gla_bwd': 4.52, 'g_post_ffn': 4.166, 'g_q': 4.767}
    for name, (base, spread) in spreads.items():
        noise = np.random.default_rng([zlib.crc32(name.encode()), seed]).standard_normal(out[name].shape)
        drawn = base * np.exp(spread * noise) if base else spread * noise
        out[name] = __import__('jax').numpy.asarray(drawn.astype(out[name].dtype))
    for name, factor in factors.items():
        out[name] = (out[name] * factor).astype(out[name].dtype)
    return out
```

```python
from contextlib import ExitStack

import concourse.bass as bass
from concourse import mybir

F32 = mybir.dt.float32
U32 = mybir.dt.uint32
I32 = mybir.dt.int32
ALU = mybir.AluOpType
ACT = mybir.ActivationFunctionType
AX = mybir.AxisListType.X
ds = bass.ds

P = 128
D = 1024
KD = D // P
N_CTX, N_LAT, N_PAST = 256, 1024, 512
T_CTX, T_LAT = N_CTX // P, N_LAT // P
NT = T_CTX + T_LAT
N_TOK = N_CTX + N_LAT
HQ, HKV, HD = 8, 2, 128
GQ = HQ // HKV
GH, DK, DV, RANK, CHUNK = 4, 128, 256, 16, 64
GATE_NORM = 16.0
NE = 16
CAP_CTX, CAP_LAT = 2 * N_CTX // NE, 2 * N_LAT // NE
CAP = CAP_CTX + CAP_LAT
EPS = 1e-6
SCALE = float(HD) ** -0.5
GSCALE = float(DK) ** -0.5
BLK = 512
BANK = 512
C_Q, C_K, C_V = 0, 1024, 1280
C_QG, C_KG, C_VG, C_RG = 1536, 2048, 2560, 3584
C_LR = 4608
C_GA, C_GB = 4640, 5664


def kind_of(t):
    return 0 if t < T_CTX else 1


class Chain:

    def __init__(self, eng, sem):
        self.eng, self.sem, self.n, self.off = eng, sem, 0, None

    def at(self, n):
        return n if self.off is None else self.off + n

    def __call__(self, ins):
        self.n += 1
        ins.then_inc(self.sem, 1)
        self.eng.wait_ge(self.sem, self.at(self.n))

    def enter(self, i, per):
        self.off, self.start, self.per = i * per, self.n, per

    def leave(self, turns):
        assert self.n - self.start == self.per, (self.n - self.start, self.per)
        self.n = self.start + turns * self.per
        self.off = None


def build_program(nc, x_prompt, x_sample, cache_k, cache_v, state_gla_fwd, state_gla_bwd, c, c_ctx,
                  g_pre_mix, g_post_mix, g_pre_ffn, g_post_ffn, w_mod, b_mod, w_in, g_q, g_k,
                  w_gk2_f, b_gk_f, w_gk2_b, b_gk_b, g_gla, w_pa, w_pg, w_out, w_router, w1, w3, w2,
                  k_ident, k_masks, k_keep, k_rope,
                  y_prompt, y_sample, new_k, new_v, new_sf, new_sb):
    ctx = ExitStack()
    with ctx:
        sems = {}

        def S(name):
            if name not in sems:
                sems[name] = ctx.enter_context(nc.semaphore(name))
            return sems[name]

        def sb(name, shape, dt=F32):
            return ctx.enter_context(nc.sbuf_tensor(name, shape, dt))

        ps = ctx.enter_context(nc.psum_tensor("ps", [P, 8 * BANK], F32))
        R1 = sb("R1", [P, NT * D])
        R2 = sb("R2", [P, NT * D])
        R3 = sb("R3", [P, NT * D])
        RW = sb("RW", [P, 2 * KD * BLK])
        WORK_N = 12416
        WK = sb("WK", [P, WORK_N])
        ident = sb("ident", [P, P])
        masks = sb("masks", [P, 4 * P + 2])
        keep = sb("keep", [P, 2 * P], I32)
        modT = sb("modT", [P, 48, 2])
        gv = sb("gv", [P, 4, KD])
        A1 = sb("A1", [P, KD, 2])
        G1 = sb("G1", [P, KD, 2])
        A2 = sb("A2", [P, KD, 2])
        G2 = sb("G2", [P, KD, 2])
        gqk = sb("gqk", [P, 2, HD])
        ggT = sb("ggT", [P, 2])
        st = sb("st", [P, 64])
        mhalf = sb("mhalf", [P, 16])
        w_lr = sb("w_lr", [P, KD, 2 * RANK])
        wr = sb("wr", [P, KD, NE])
        affT = R2[0:NE, 0:N_TOK]
        xhat_dram = nc.dram_tensor("xhat_scratch", (N_TOK, D), F32, kind="Internal").ap()
        x1_dram = nc.dram_tensor("x1_scratch", (N_TOK, D), F32, kind="Internal").ap()
        ffn_dram = nc.dram_tensor("ffn_scratch", (N_TOK, D), F32, kind="Internal").ap()

        hT = R1[:, :].rearrange("p (k t) -> p k t", k=KD)
        Wslot = [RW[:, s * KD * BLK:(s + 1) * KD * BLK].rearrange("p (k n) -> p k n", k=KD) for s in range(2)]

        def bank(b, n=BANK, parts=P):
            return ps[0:parts, b * BANK:b * BANK + n]

        used = [0]

        def work(n, at=None):
            if at is not None:
                used[0] = at
            o = used[0]
            used[0] += n
            assert used[0] <= WORK_N, used[0]
            return WK[:, o:o + n]

        xp = x_prompt.rearrange("a t d -> (a t) d")
        xs_ = x_sample.rearrange("a t d -> (a t) d")
        yp = y_prompt.rearrange("a t d -> (a t) d")
        ys = y_sample.rearrange("a t d -> (a t) d")

        def x_rows(t):
            return xp[t * P:(t + 1) * P, :] if t < T_CTX else xs_[(t - T_CTX) * P:(t - T_CTX + 1) * P, :]

        def y_rows(t):
            return yp[t * P:(t + 1) * P, :] if t < T_CTX else ys[(t - T_CTX) * P:(t - T_CTX + 1) * P, :]

        wmod, win = w_mod[0], w_in[0]
        wpa, wpg, wout = w_pa[0], w_pg[0], w_out[0]

        units = []
        mod_u = len(units)
        units += [[(wmod, u * BLK, BLK, 0)] for u in range(12)]
        kv_u = len(units)
        units += [[(win, C_K, BLK, 0)]]
        q_u = len(units)
        units += [[(win, C_Q + cb * BLK, BLK, 0)] for cb in range(2)]
        ma_u = len(units)
        for cb in range(2):
            units += [[(win, C_GA + cb * BLK, BLK, 0)], [(wpa, cb * BLK, BLK, 0)]]
        gla_u = len(units)
        for h in range(GH):
            units += [[(win, C_QG + h * DK, DK, 0), (win, C_KG + h * DK, DK, DK), (win, C_VG + h * DV, DV, 2 * DK)],
                      [(win, C_RG + h * DV, DV, 0)]]
        mb_u = len(units)
        for cb in range(2):
            units += [[(win, C_GB + cb * BLK, BLK, 0)], [(wpg, cb * BLK, BLK, 0)]]
        out_u = len(units)
        units += [[(wout, cb * BLK, BLK, 0)] for cb in range(2)]
        w_ready, uses, tot = [], [], [0, 0]
        cnt = [0, 0]
        for u, dmas in enumerate(units):
            s = u % 2
            tot[s] += 16 * len(dmas)
            w_ready.append(tot[s])
            uses.append(cnt[s])
            cnt[s] += 1
        w_full = [S("weights_landed_slot0"), S("weights_landed_slot1")]
        w_free = [S("weights_used_slot0"), S("weights_used_slot1")]

        def load_unit(sp, u):
            s = u % 2
            if uses[u] > 0:
                sp.wait_ge(w_free[s], uses[u])
            for src, c0, n, o in units[u]:
                sp.dma_start(Wslot[s][:, :, o:o + n], src[:, c0:c0 + n].rearrange("(k p) n -> p k n", p=P)) \
                    .then_inc(w_full[s], 16)

        stage_done = {e: S("stage_done_" + e) for e in ("pe", "act", "dve", "pool")}

        def begin(eng, me, k):
            for e in ("pe", "act", "dve", "pool"):
                if e != me:
                    eng.wait_ge(stage_done[e], k)

        def end(eng, me):
            eng.drain().then_inc(stage_done[me], 1)

        def gemm(pe, out, lhs, slot, width=BLK, off=0):
            for k in range(KD):
                m = pe.matmul(out, lhs(k), Wslot[slot][:, k, off:off + width], start=(k == 0), stop=(k == KD - 1))
            return m

        chains = {}

        block = ctx.enter_context(nc.Block())

        cT = work(16, at=0).rearrange("p (k j) -> p k j", j=2)
        cS = work(16).rearrange("p (k j) -> p k j", j=2)
        modrow = R3[0:2, 0:6 * D]
        brow = R2[0:2, 0:6 * D]

        def sp_consts(sp):
            n = 0
            for dst, src in (
                (cT[:, :, 0], c_ctx.rearrange("(k p) -> p k", p=P)),
                (cT[:, :, 1], c[0].rearrange("(k p) -> p k", p=P)),
                (ident[:, :], k_ident), (masks[:, :], k_masks), (keep[:, :], k_keep),
                (brow[0:1, :], b_mod[0:1, :]), (brow[1:2, :], b_mod[0:1, :]),
                (gv[:, 0, :], g_pre_mix[0].rearrange("(k p) -> p k", p=P)),
                (gv[:, 1, :], g_post_mix[0].rearrange("(k p) -> p k", p=P)),
                (gv[:, 2, :], g_pre_ffn[0].rearrange("(k p) -> p k", p=P)),
                (gv[:, 3, :], g_post_ffn[0].rearrange("(k p) -> p k", p=P)),
                (gqk[:, 0, :], g_q[0:1, :].broadcast_to([P, HD])),
                (gqk[:, 1, :], g_k[0:1, :].broadcast_to([P, HD])),
                (ggT[:, :], g_gla[0].rearrange("(k p) -> p k", p=P)),
                (w_lr[:, :, :], win[:, C_LR:C_LR + 2 * RANK].rearrange("(k p) n -> p k n", p=P)),
                (wr[:, :, :], w_router[0].rearrange("(k p) n -> p k n", p=P)),
            ):
                sp.dma_start(dst, src, allow_slow_non_contiguous=True).then_inc(S("consts_landed"), 16)
                n += 16
            return n

        N_CONST = 16 * 16

        def sp_mod(sp):
            assert sp_consts(sp) == N_CONST
            for u in range(kv_u):
                load_unit(sp, u)

        def act_mod(act, ch):
            act.wait_ge(S("consts_landed"), N_CONST)
            act.activation(cS, cT, ACT.Silu).then_inc(S("cond_ready"), 1)
            end(act, "act")

        def pe_mod(pe):
            pe.wait_ge(S("cond_ready"), 1)
            with pe.Fori(0, 6) as i:
                for s in range(2):
                    pe.wait_ge(w_full[s], i * 16 + 16)
                    pe.wait_ge(S(f"mod_row_kept{s}"), i + 1)
                    for k in range(KD):
                        m = pe.matmul(bank(s, BLK, 2), cS[:, k, :], Wslot[s][:, k, :], start=(k == 0), stop=(k == KD - 1))
                    m.then_inc(S(f"mod_row{s}"), 1)
                    pe.wait_ge(S(f"mod_row{s}"), i + 1)
                    pe.sem_inc(w_free[s], 1)
            for s in range(2):
                pe.wait_ge(S(f"mod_row_kept{s}"), 7)
            for n in range(48):
                m = pe.transpose(ps[:, 2 * BANK + 2 * n:2 * BANK + 2 * n + 2], modrow[:, n * P:(n + 1) * P], ident[0:2, 0:2])
            m.then_inc(S("mod_columns"), 1)
            end(pe, "pe")

        def dve_mod(dve, ch):
            dve.wait_ge(S("consts_landed"), N_CONST)
            for s in range(2):
                dve.sem_inc(S(f"mod_row_kept{s}"), 1)
            with dve.Fori(0, 6) as i:
                for s in range(2):
                    dve.wait_ge(S(f"mod_row{s}"), i + 1)
                    o = ds(i * (2 * BLK) + s * BLK, BLK)
                    dve.tensor_tensor(modrow[:, o], bank(s, BLK, 2), brow[:, o], ALU.add).then_inc(S(f"mod_row_kept{s}"), 1)
            dve.wait_ge(S("mod_columns"), 1)
            ch(dve.tensor_copy(modT[:, :, :], ps[:, 2 * BANK:2 * BANK + 96].rearrange("p (a b) -> p a b", b=2)))

            def g(n):
                return gv[:, n, :].unsqueeze(2).broadcast_to([P, KD, 2])
            ch(dve.scalar_tensor_tensor(A1[:, :, :], modT[:, 8:16, :], 1.0, g(0), ALU.add, ALU.mult))
            ch(dve.tensor_tensor(G1[:, :, :], modT[:, 16:24, :], g(1), ALU.mult))
            ch(dve.scalar_tensor_tensor(A2[:, :, :], modT[:, 32:40, :], 1.0, g(2), ALU.add, ALU.mult))
            ch(dve.tensor_tensor(G2[:, :, :], modT[:, 40:48, :], g(3), ALU.mult))
            end(dve, "dve")

        def pool_mod(pool, ch):
            ch(pool.memset(mhalf[:, :], -0.5))
            end(pool, "pool")

        x_t = [work(D, at=0)] + [work(D) for _ in range(2)]
        xn_t = [work(D) for _ in range(2)]
        sq_t = work(D)
        ss1, var1, rstd1 = st[:, 0:10], st[:, 10:20], st[:, 20:30]

        def pool_norm(pool, ch):
            begin(pool, "pool", 1)
            for t in range(NT):
                if t >= 3:
                    pool.wait_ge(S("x_scaled"), t - 2)
                pool.dma_start(x_t[t % 3], x_rows(t)).then_inc(S(f"x_landed{t % 3}"), 16)
                if t >= 2:
                    pool_pow(pool, t - 2)
            pool_pow(pool, NT - 2)
            pool_pow(pool, NT - 1)
            end(pool, "pool")

        def pool_pow(pool, t):
            pool.wait_ge(S("x_var"), t + 1)
            pool.tensor_tensor(rstd1[:, t:t + 1], var1[:, t:t + 1], mhalf[:, 0:1], ALU.pow).then_inc(S("x_rstd"), 1)

        def sp_norm(sp):
            load_unit(sp, kv_u)
            load_unit(sp, q_u)

        def act_norm(act, ch):
            begin(act, "act", 1)

            def square(t):
                act.wait_ge(S(f"x_landed{t % 3}"), 16 * (t // 3 + 1))
                act.activation(sq_t, x_t[t % 3], ACT.Square, accum_out=ss1[:, t:t + 1]).then_inc(S("x_sumsq"), 1)
                act.wait_ge(S("x_sumsq"), t + 1)

            square(0)
            for t in range(NT):
                if t + 1 < NT:
                    square(t + 1)
                act.wait_ge(S("x_turned"), t + 1)
                j = kind_of(t)
                for k in range(4):
                    m = act.activation(hT[:, k, t * P:(t + 1) * P], ps[:, (2 * (t % 2)) * BANK + k * P:(2 * (t % 2)) * BANK + (k + 1) * P],
                                       ACT.Identity, scale=A1[:, k, j:j + 1], bias=modT[:, k, j:j + 1])
                    if k < 3:
                        ch(m)
                m.then_inc(S("h_kept_act"), 1)
                act.wait_ge(S("h_kept_act"), t + 1)
            end(act, "act")

        def dve_norm(dve, ch):
            begin(dve, "dve", 1)

            def scale(t):
                dve.wait_ge(S("x_sumsq"), t + 1)
                dve.tensor_scalar(var1[:, t:t + 1], ss1[:, t:t + 1], 1.0 / D, EPS, ALU.mult, ALU.add).then_inc(S("x_var"), 1)
                dve.wait_ge(S("x_rstd"), t + 1)
                if t >= 2:
                    dve.wait_ge(S("x_turned"), t - 1)
                dve.tensor_scalar(xn_t[t % 2], x_t[t % 3], rstd1[:, t:t + 1], None, ALU.mult).then_inc(S("x_scaled"), 1)
                dve.wait_ge(S("x_scaled"), t + 1)

            scale(0)
            for t in range(NT):
                if t + 1 < NT:
                    scale(t + 1)
                dve.wait_ge(S("x_turned"), t + 1)
                j = kind_of(t)
                for k in range(4, 8):
                    m = dve.tensor_scalar(hT[:, k, t * P:(t + 1) * P], ps[:, (2 * (t % 2)) * BANK + k * P:(2 * (t % 2)) * BANK + (k + 1) * P],
                                          A1[:, k, j:j + 1], modT[:, k, j:j + 1], ALU.mult, ALU.add)
                    if k < 7:
                        ch(m)
                m.then_inc(S("h_kept_dve"), 1)
                dve.wait_ge(S("h_kept_dve"), t + 1)
            end(dve, "dve")

        def pe_norm(pe):
            begin(pe, "pe", 1)
            for t in range(NT):
                pe.wait_ge(S("x_scaled"), t + 1)
                if t >= 2:
                    pe.wait_ge(S("h_kept_act"), t - 1)
                    pe.wait_ge(S("h_kept_dve"), t - 1)
                for k in range(KD):
                    o = (2 * (t % 2)) * BANK + k * P
                    m = pe.transpose(ps[:, o:o + P], xn_t[t % 2][:, k * P:(k + 1) * P], ident[:, :])
                m.then_inc(S("x_turned"), 1)
            end(pe, "pe")

        vv = work(14 * 256, at=0).rearrange("p (b n) -> p b n", b=14)
        v_end = used[0]
        cos_t = work(T_LAT * 64).rearrange("p (t f) -> p t f", t=T_LAT)
        sin_t = work(T_LAT * 64).rearrange("p (t f) -> p t f", t=T_LAT)
        ck = work(HKV * 4 * HD).rearrange("p (g b d) -> p g b d", g=HKV, b=4)
        sqk = work(BLK)
        nrm = [work(BLK) for _ in range(2)]
        rot = [work(BLK) for _ in range(2)]
        rtmp = work(256)
        rtmp2 = work(256)
        ssq, varq, rsq = st[:, 32:36], st[:, 36:40], st[:, 40:44]
        NK = N_PAST + N_LAT + N_CTX
        kT = R3[:, 0:HKV * NK].rearrange("p (g l) -> p g l", g=HKV)
        pT = R3[:, HKV * NK:HKV * NK + 12 * BLK].rearrange("p (b n) -> p b n", b=12)
        assert HKV * NK + 12 * BLK <= NT * D
        K_CTX = N_PAST + N_LAT

        def key_at(t):
            return K_CTX + t * P if t < T_CTX else N_PAST + (t - T_CTX) * P

        def val_at(t):
            return 12 + t if t < T_CTX else 4 + t - T_CTX
        qkv_steps = [(kv_u, t) for t in range(NT)] + [(q_u + cb, t) for cb in range(2) for t in range(NT)]

        def sp_qkv(sp):
            sp.wait_ge(stage_done["pe"], 2)
            for e in ("dve", "act", "pool"):
                sp.wait_ge(stage_done[e], 2)
            for g in range(HKV):
                sp.dma_start(ck[:, g, :, :], cache_k[0, 0, g].rearrange("(b p) d -> p b d", p=P)).then_inc(S("cache_landed"), 16)
                sp.dma_start(vv[:, 0:4, g * HD:(g + 1) * HD], cache_v[0, 0, g].rearrange("(b p) d -> p b d", p=P)).then_inc(S("cache_landed"), 16)
            sp.dma_start(cos_t, k_rope[0].rearrange("(t p) f -> p t f", p=P)).then_inc(S("cache_landed"), 16)
            sp.dma_start(sin_t, k_rope[1].rearrange("(t p) f -> p t f", p=P)).then_inc(S("cache_landed"), 16)
            for t in range(T_CTX):
                sp.wait_ge(S("qk_turned_ready"), t + 1)
                for g in range(HKV):
                    rows = slice(t * P, (t + 1) * P)
                    sp.dma_start(new_k[0, 0, g, rows, :], nrm[t % 2][:, g * HD:(g + 1) * HD]).then_inc(S("new_k_stored"), 16)
                    sp.dma_start(new_v[0, 0, g, rows, :], vv[:, 12 + t, g * HD:(g + 1) * HD]).then_inc(S("new_k_stored"), 16)
            for u in range(q_u + 1, ma_u + 2):
                load_unit(sp, u)

        def heads_of(u):
            return HKV if u == kv_u else GQ

        def pe_qkv(pe):
            begin(pe, "pe", 2)
            pe.wait_ge(S("cache_landed"), 16 * 6)
            for g in range(HKV):
                for b in range(4):
                    m = pe.transpose(ps[:, (2 + g) * BANK + b * P:(2 + g) * BANK + (b + 1) * P], ck[:, g, b, :], ident[:, :])
            m.then_inc(S("cached_keys_turned"), 1)

            def turn(n):
                u, t = qkv_steps[n]
                pe.wait_ge(S("qk_turned_ready"), n + 1)
                if n >= 2:
                    pe.wait_ge(S("qk_turned_kept"), n - 1)
                for h in range(heads_of(u)):
                    src = rot[n % 2] if t >= T_CTX else nrm[n % 2]
                    m = pe.transpose(ps[:, (n % 2) * BANK + h * P:(n % 2) * BANK + (h + 1) * P], src[:, h * HD:(h + 1) * HD], ident[:, :])
                m.then_inc(S("qk_turned"), 1)

            for n, (u, t) in enumerate(qkv_steps):
                if t == 0:
                    pe.wait_ge(w_full[u % 2], w_ready[u])
                if n >= 4:
                    pe.wait_ge(S("qk_bank_free"), n - 3)
                m = gemm(pe, bank(4 + n % 4), lambda k: hT[:, k, t * P:(t + 1) * P], u % 2)
                m.then_inc(S("qk_projected"), 1)
                if t == NT - 1:
                    pe.wait_ge(S("qk_projected"), n + 1)
                    pe.sem_inc(w_free[u % 2], 1)
                if n >= 1:
                    turn(n - 1)
            turn(len(qkv_steps) - 1)
            end(pe, "pe")

        def act_qkv(act, ch):
            begin(act, "act", 2)
            act.wait_ge(S("cached_keys_turned"), 1)
            ch(act.activation(kT[:, 0, 0:N_PAST], bank(2), ACT.Copy))
            ch(act.activation(kT[:, 1, 0:N_PAST], bank(3), ACT.Copy))

            def keep_turned(n):
                u, t = qkv_steps[n]
                act.wait_ge(S("qk_turned"), n + 1)
                if u == kv_u:
                    m = act.activation(kT[:, :, key_at(t):key_at(t) + P], bank(n % 2, 2 * P).rearrange("p (g l) -> p g l", g=2), ACT.Copy)
                else:
                    o = (t * HQ + GQ * (u - q_u)) * P
                    m = act.activation(R2[:, o:o + GQ * P], bank(n % 2), ACT.Copy)
                m.then_inc(S("qk_turned_kept"), 1)
                act.wait_ge(S("qk_turned_kept"), n + 1)

            for n, (u, t) in enumerate(qkv_steps):
                act.wait_ge(S("qk_projected"), n + 1)
                b = 4 + n % 4
                w = heads_of(u) * HD
                if u == kv_u:
                    ch(act.activation(vv[:, val_at(t), :], ps[:, b * BANK + 256:b * BANK + 512], ACT.Copy))
                if n >= 1:
                    act.wait_ge(S("qk_bank_free"), n)
                act.activation(sqk[:, 0:w], bank(b, w), ACT.Square).then_inc(S("qk_squared"), 1)
                act.wait_ge(S("qk_squared"), n + 1)
                if n >= 1:
                    keep_turned(n - 1)
            keep_turned(len(qkv_steps) - 1)
            end(act, "act")

        def pool_qkv(pool, ch):
            begin(pool, "pool", 2)
            for n in range(len(qkv_steps)):
                pool.wait_ge(S("qk_var"), n + 1)
                pool.tensor_tensor(rsq, varq, mhalf[:, 0:4], ALU.pow).then_inc(S("qk_rstd"), 1)
            end(pool, "pool")

        def dve_qkv(dve, ch):
            begin(dve, "dve", 2)
            dve.wait_ge(S("cache_landed"), 16 * 6)
            ch(dve.memset(varq, 1.0))
            for n, (u, t) in enumerate(qkv_steps):
                H = heads_of(u)
                w = H * HD
                src = bank(4 + n % 4, w)
                dve.wait_ge(S("qk_squared"), n + 1)
                ch(dve.tensor_reduce(ssq[:, 0:H], sqk[:, 0:w].rearrange("p (h d) -> p h d", h=H), AX, ALU.add))
                if n >= 2:
                    dve.wait_ge(S("qk_turned"), n - 1)
                if n == 2:
                    dve.wait_ge(S("new_k_stored"), 16 * 2 * HKV * T_CTX)
                dve.tensor_scalar(varq[:, 0:H], ssq[:, 0:H], 1.0 / HD, EPS, ALU.mult, ALU.add).then_inc(S("qk_var"), 1)
                dve.wait_ge(S("qk_rstd"), n + 1)
                for h in range(H):
                    m = dve.scalar_tensor_tensor(nrm[n % 2][:, h * HD:(h + 1) * HD], src[:, h * HD:(h + 1) * HD], rsq[:, h:h + 1],
                                                 gqk[:, (1 if u == kv_u else 0), :], ALU.mult, ALU.mult)
                    if h < H - 1:
                        ch(m)
                m.then_inc(S("qk_bank_free"), 1)
                dve.wait_ge(S("qk_bank_free"), n + 1)
                if t >= T_CTX:
                    v = nrm[n % 2][:, 0:w].rearrange("p (h f e) -> p h f e", h=H, e=2)
                    r = rot[n % 2][:, 0:w].rearrange("p (h f e) -> p h f e", h=H, e=2)
                    t1 = rtmp[:, 0:H * 64].rearrange("p (h f) -> p h f", h=H)
                    t2 = rtmp2[:, 0:H * 64].rearrange("p (h f) -> p h f", h=H)
                    cs = cos_t[:, t - T_CTX, :].unsqueeze(1).broadcast_to([P, H, 64])
                    sn = sin_t[:, t - T_CTX, :].unsqueeze(1).broadcast_to([P, H, 64])
                    ch(dve.tensor_tensor(t1, v[:, :, :, 0], cs, ALU.mult))
                    ch(dve.tensor_tensor(t2, v[:, :, :, 1], sn, ALU.mult))
                    ch(dve.tensor_tensor(r[:, :, :, 0], t1, t2, ALU.subtract))
                    ch(dve.tensor_tensor(t1, v[:, :, :, 0], sn, ALU.mult))
                    ch(dve.tensor_tensor(t2, v[:, :, :, 1], cs, ALU.mult))
                    m = dve.tensor_tensor(r[:, :, :, 1], t1, t2, ALU.add)
                else:
                    m = dve.tensor_copy(rtmp[:, 0:1], ssq[:, 0:1])
                m.then_inc(S("qk_turned_ready"), 1)
                dve.wait_ge(S("qk_turned_ready"), n + 1)
            end(dve, "dve")

        Pb = [work(1536, at=v_end)] + [work(1536)]
        qst = [work(GQ * P) for _ in range(HKV)]
        mxa, nmx, sma, rsm = st[:, 44:46], st[:, 46:48], st[:, 48:50], st[:, 50:52]

        def tile_plan(T):
            return (2, K_CTX, 12) if T < T_CTX else (12, 0, 0)

        def sset(s):
            return (s % 2) * 3 * BANK

        def pool_attn(pool, ch):
            begin(pool, "pool", 3)

            def stage(T, first):
                for g in range(HKV):
                    if not first:
                        pool.wait_ge(S("scores_done"), T * 8 - 8 + 4 * (g + 1))
                    o = T * D + g * GQ * P
                    pool.tensor_copy(qst[g], R2[:, o:o + GQ * P] if isinstance(T, int) else R2[:, ds(o, GQ * P)]) \
                        .then_inc(S(f"queries_staged{g}"), 1)
            for T in range(T_CTX):
                stage(T, T == 0)
            with pool.Fori(0, T_LAT) as i:
                stage(i + T_CTX, False)
            end(pool, "pool")

        def pe_attn(pe):
            begin(pe, "pe", 3)

            def tile(T, nk, k0, v0, first):
                s0 = T * HQ

                def scores(k):
                    g, j = k // GQ, k % GQ
                    if j == 0:
                        pe.wait_ge(S(f"queries_staged{g}"), T + 1)
                    if not (first and k < 2):
                        pe.wait_ge(S("probsT_kept_act"), s0 + (k - 1))
                        pe.wait_ge(S("probsT_kept_dve"), s0 + (k - 1))
                    for c0 in range(0, nk * P, BLK):
                        w = min(BLK, nk * P - c0)
                        m = pe.matmul(ps[:, sset(k) + c0:sset(k) + c0 + w], qst[g][:, j * P:(j + 1) * P],
                                      kT[:, g, k0 + c0:k0 + c0 + w], start=True, stop=True)
                    m.then_inc(S("scores_done"), 1)

                def turn(k):
                    pe.wait_ge(S("probs_scaled"), s0 + (k + 1))
                    at = [0, 2 * BANK] if nk == 2 else [b * P for b in range(nk)]
                    for b in range(nk):
                        m = pe.transpose(ps[:, sset(k) + at[b]:sset(k) + at[b] + P], Pb[k % 2][:, b * P:(b + 1) * P], ident[:, :])
                        if b == (0 if nk == 2 else 7):
                            m.then_inc(S("probsT_act"), 1)
                    m.then_inc(S("probsT_dve"), 1)

                def weigh(g):
                    pe.wait_ge(S("probsT_kept_act"), s0 + GQ * (g + 1))
                    pe.wait_ge(S("probsT_kept_dve"), s0 + GQ * (g + 1))
                    if not first:
                        pe.wait_ge(S(f"attn_kept{g}"), T)
                    for b in range(nk):
                        m = pe.matmul(bank(6 + g), vv[:, v0 + b, g * HD:(g + 1) * HD], pT[:, b, :], start=(b == 0), stop=(b == nk - 1))
                    m.then_inc(S("values_weighed"), 1)

                scores(0)
                for k in range(HQ):
                    if k + 1 < HQ:
                        scores(k + 1)
                    turn(k)
                    if k % GQ == GQ - 1:
                        weigh(k // GQ)

            for T in range(T_CTX):
                tile(T, *tile_plan(T), T == 0)
            with pe.Fori(0, T_LAT) as i:
                tile(i + T_CTX, *tile_plan(T_CTX), False)
            end(pe, "pe")

        def dve_attn(dve, ch):
            begin(dve, "dve", 3)

            def tile(T, nk, first):
                s0 = T * HQ

                def top(k):
                    b = k % 2
                    dve.wait_ge(S("scores_done"), s0 + (k + 1))
                    ch(dve.tensor_reduce(mxa[:, b:b + 1], ps[:, sset(k):sset(k) + nk * P], AX, ALU.max))
                    dve.tensor_scalar(nmx[:, b:b + 1], mxa[:, b:b + 1], -SCALE, None, ALU.mult).then_inc(S("max_ready"), 1)

                def norm(k):
                    b = k % 2
                    dve.wait_ge(S("probs_ready"), s0 + (k + 1))
                    ch(dve.reciprocal(rsm[:, b:b + 1], sma[:, b:b + 1]))
                    dve.tensor_scalar(Pb[b][:, 0:nk * P], Pb[b][:, 0:nk * P], rsm[:, b:b + 1], None, ALU.mult).then_inc(S("probs_scaled"), 1)
                    dve.wait_ge(S("probs_scaled"), s0 + (k + 1))

                def keep_turned(k):
                    g, j = k // GQ, k % GQ
                    dve.wait_ge(S("probsT_dve"), s0 + (k + 1))
                    if j == 0 and not (first and g == 0):
                        dve.wait_ge(S("values_weighed"), T * HKV + g)
                    if nk == 2:
                        m = dve.tensor_copy(pT[:, 1, j * P:(j + 1) * P], ps[:, sset(k) + 2 * BANK:sset(k) + 2 * BANK + P])
                    else:
                        m = dve.tensor_copy(pT[:, 8:12, j * P:(j + 1) * P],
                                            ps[:, sset(k) + 2 * BANK:sset(k) + 3 * BANK].rearrange("p (b q) -> p b q", b=4))
                    m.then_inc(S("probsT_kept_dve"), 1)
                    dve.wait_ge(S("probsT_kept_dve"), s0 + (k + 1))

                top(0)
                for k in range(HQ):
                    norm(k)
                    if k + 1 < HQ:
                        top(k + 1)
                    keep_turned(k)

            for T in range(T_CTX):
                tile(T, tile_plan(T)[0], T == 0)
            with dve.Fori(0, T_LAT) as i:
                ch.enter(i, 16)
                tile(i + T_CTX, 12, False)
                ch.leave(T_LAT)
            end(dve, "dve")

        def act_attn(act, ch):
            begin(act, "act", 3)

            def tile(T, nk, first):
                s0 = T * HQ

                def exps(k):
                    b = k % 2
                    act.wait_ge(S("max_ready"), s0 + (k + 1))
                    act.activation(Pb[b][:, 0:nk * P], ps[:, sset(k):sset(k) + nk * P], ACT.Exp, bias=nmx[:, b:b + 1],
                                   scale=SCALE, accum_out=sma[:, b:b + 1]).then_inc(S("probs_ready"), 1)
                    act.wait_ge(S("probs_ready"), s0 + (k + 1))

                def keep_turned(k):
                    g, j = k // GQ, k % GQ
                    act.wait_ge(S("probsT_act"), s0 + (k + 1))
                    if j == 0 and not (first and g == 0):
                        act.wait_ge(S("values_weighed"), T * HKV + g)
                    if nk == 2:
                        m = act.activation(pT[:, 0, j * P:(j + 1) * P], ps[:, sset(k):sset(k) + P], ACT.Copy)
                    else:
                        m = act.activation(pT[:, 0:8, j * P:(j + 1) * P],
                                           ps[:, sset(k):sset(k) + 2 * BANK].rearrange("p (b q) -> p b q", b=8), ACT.Copy)
                    m.then_inc(S("probsT_kept_act"), 1)
                    act.wait_ge(S("probsT_kept_act"), s0 + (k + 1))

                def keep_out(g):
                    act.wait_ge(S("values_weighed"), T * HKV + (g + 1))
                    o = T * D + g * GQ * P
                    dst = R2[:, o:o + GQ * P] if isinstance(T, int) else R2[:, ds(o, GQ * P)]
                    act.activation(dst, bank(6 + g), ACT.Copy).then_inc(S(f"attn_kept{g}"), 1)
                    act.wait_ge(S(f"attn_kept{g}"), T + 1)

                exps(0)
                for k in range(HQ):
                    if k + 1 < HQ:
                        exps(k + 1)
                    keep_turned(k)
                    if k % GQ == GQ - 1:
                        keep_out(k // GQ)

            for T in range(T_CTX):
                tile(T, tile_plan(T)[0], T == 0)
            with act.Fori(0, T_LAT) as i:
                tile(i + T_CTX, 12, False)
            end(act, "act")

        def sp_attn(sp):
            pass

        mix = R3[:, :].rearrange("p (t n) -> p t n", t=NT)
        sig_at = WORK_N - NT * BLK
        sig = WK[:, sig_at:].rearrange("p (t n) -> p t n", t=NT)

        def merge(u0, branch, tag, k, add):
            gates, prods = f"gates_{tag}", f"merged_{tag}"

            def pe_merge(pe):
                begin(pe, "pe", k)
                for v in range(4):
                    u = u0 + v
                    pe.wait_ge(w_full[u % 2], w_ready[u])
                    for t in range(NT):
                        m = v * NT + t
                        if m >= 4:
                            pv, pt = (m - 4) // NT, (m - 4) % NT
                            pe.wait_ge(S(gates if pv % 2 == 0 else prods), (pv // 2) * NT + pt + 1)
                        if v % 2 == 0:
                            i = gemm(pe, bank(m % 4), lambda q: hT[:, q, t * P:(t + 1) * P], u % 2)
                        else:
                            i = gemm(pe, bank(m % 4), lambda q: branch(q, t), u % 2)
                        i.then_inc(S(f"tile_done_{tag}"), 1)
                    pe.wait_ge(S(f"tile_done_{tag}"), (v + 1) * NT)
                    pe.sem_inc(w_free[u % 2], 1)
                end(pe, "pe")

            def act_merge(act, ch):
                begin(act, "act", k)
                for cb in range(2):
                    for t in range(NT):
                        m = 2 * cb * NT + t
                        act.wait_ge(S(f"tile_done_{tag}"), m + 1)
                        if cb:
                            act.wait_ge(S(prods), t + 1)
                        act.activation(sig[:, t, :], bank(m % 4), ACT.Sigmoid).then_inc(S(gates), 1)
                        act.wait_ge(S(gates), cb * NT + t + 1)
                end(act, "act")

            def dve_merge(dve, ch):
                begin(dve, "dve", k)
                for cb in range(2):
                    for t in range(NT):
                        m = (2 * cb + 1) * NT + t
                        dve.wait_ge(S(gates), cb * NT + t + 1)
                        dve.wait_ge(S(f"tile_done_{tag}"), m + 1)
                        dst = mix[:, t, cb * BLK:(cb + 1) * BLK]
                        if add:
                            ch(dve.tensor_tensor(sig[:, t, :], sig[:, t, :], bank(m % 4), ALU.mult))
                            i = dve.tensor_tensor(dst, dst, sig[:, t, :], ALU.add)
                        else:
                            i = dve.tensor_tensor(dst, sig[:, t, :], bank(m % 4), ALU.mult)
                        i.then_inc(S(prods), 1)
                        dve.wait_ge(S(prods), cb * NT + t + 1)
                end(dve, "dve")
            return pe_merge, act_merge, dve_merge

        def pool_idle(k):
            def f(pool, ch):
                begin(pool, "pool", k)
                end(pool, "pool")
            return f

        pe_ma, act_ma, dve_ma = merge(ma_u, lambda h, t: R2[:, (t * HQ + h) * P:(t * HQ + h + 1) * P], "attn", 4, False)

        def sp_ma(sp):
            for u in range(ma_u + 2, ma_u + 4):
                load_unit(sp, u)
            for u in range(gla_u, gla_u + 2):
                load_unit(sp, u)

        gkT = work(N_TOK, at=0)[0:33, :]
        wg = work(2 * GH * DK)[0:33, :].rearrange("p (r n) -> p r n", r=2)
        qkv = work(NT * BLK).rearrange("p (t n) -> p t n", t=NT)
        lg_at = used[0]
        lg = [work(DK) for _ in range(2)]
        glt = work(DK)
        ex = [work(3 * DK).rearrange("p (a n) -> p a n", a=3) for _ in range(2)]
        dec = [work(2) for _ in range(4)]
        qkd = [work(3 * DK).rearrange("p (a n) -> p a n", a=3) for _ in range(3)]
        g_end = used[0]
        ogT = R2[:, :].rearrange("p (k t) -> p k t", k=KD)
        qkT = [work(2 * P).rearrange("p (a n) -> p a n", a=2) for _ in range(2)]
        am = [work(P) for _ in range(2)]
        Sst = [[work(DV) for _ in range(2)] for _ in range(2)]
        o_lo = Wslot[(gla_u + 1) % 2][:, :, DV:2 * DV]
        o_hi = work(2 * DV).rearrange("p (t n) -> p t n", n=DV)
        on = work(DV)
        rs = [WK[:, lg_at:lg_at + DV]]

        def o_tile(t):
            return o_hi[:, t, :] if t < T_CTX else o_lo[:, t - T_CTX, :]

        F_ORD = list(range(T_CTX, NT)) + list(range(T_CTX))
        B_ORD = list(range(NT - 1, T_CTX - 1, -1)) + list(range(T_CTX - 1, -1, -1))
        items = []
        for a, b in zip(F_ORD, B_ORD):
            items += [(0, a), (1, b)]
        NI = len(items)
        seen = set()
        first_touch = []
        for d_, t_ in items:
            first_touch.append(t_ not in seen)
            seen.add(t_)
        gst = st[:, 52:64]

        def sp_gla(sp):
            begin(sp, "sp", 5)
            sp.wait_ge(S("gate_weights_cleared"), 1)
            sp.dma_start(wg[0:RANK, 0, :], w_gk2_f[0]).then_inc(S("gate_weights_landed"), 16)
            sp.dma_start(wg[RANK:2 * RANK, 1, :], w_gk2_b[0]).then_inc(S("gate_weights_landed"), 16)
            sp.dma_start(wg[32:33, 0, :], b_gk_f[0:1, :]).then_inc(S("gate_weights_landed"), 16)
            sp.dma_start(wg[32:33, 1, :], b_gk_b[0:1, :]).then_inc(S("gate_weights_landed"), 16)
            for h in range(GH):
                for d_, src in ((0, state_gla_fwd), (1, state_gla_bwd)):
                    if h:
                        sp.wait_ge(S("ctx_state_stored"), 32 * h)
                    sp.dma_start(Sst[d_][0], src[0, 0, h]).then_inc(S("state_landed"), 16)
                if h + 1 < GH:
                    for u in (gla_u + 2 * h + 2, gla_u + 2 * h + 3):
                        load_unit(sp, u)
                else:
                    for u in (mb_u, mb_u + 1):
                        if u % 2 == (gla_u + 1) % 2:
                            sp.wait_ge(S("head_done"), GH)
                        load_unit(sp, u)
                for d_, dst in ((0, new_sf), (1, new_sb)):
                    sp.wait_ge(S(f"ctx_state_final{d_}"), h + 1)
                    sp.dma_start(dst[0, 0, h], Sst[d_][0]).then_inc(S("ctx_state_stored"), 16)

        def pe_gla(pe):
            begin(pe, "pe", 5)
            for n, (c0, w) in enumerate(((0, 512), (512, 512), (1024, 256))):
                for k in range(KD):
                    m = pe.matmul(ps[0:32, n * BANK:n * BANK + w], w_lr[:, k, :], hT[:, k, c0:c0 + w], start=(k == 0), stop=(k == KD - 1))
                m.then_inc(S("low_rank_done"), 1)
            pe.wait_ge(S("low_rank_kept"), 3)
            pe.wait_ge(S("gate_weights_landed"), 64)
            with pe.Fori(0, GH) as h:
                pe.wait_ge(w_full[gla_u % 2], h * 48 + w_ready[gla_u])
                for t in range(NT):
                    if t >= 2:
                        pe.wait_ge(S("qkv_kept"), h * NT + (t - 1))
                    m = gemm(pe, bank(t % 2), lambda q: hT[:, q, t * P:(t + 1) * P], gla_u % 2)
                    m.then_inc(S("qkv_done"), 1)
                pe.wait_ge(S("qkv_done"), h * NT + NT)
                pe.sem_inc(w_free[gla_u % 2], 1)
                pe.wait_ge(S("qkv_kept"), h * NT + NT)

                def gate(n):
                    d_, t = items[n]
                    if n >= 1:
                        pe.wait_ge(S("gate_logit_used"), h * NI + n)
                    o = bank(0, DK)
                    pe.sem_inc(S("gate_turns"), 1)
                    pe.matmul(o, gkT[0:33, t * P:(t + 1) * P], wg[0:33, d_, ds(h * DK, DK)], start=True, stop=True) \
                        .then_inc(S("gate_logits"), 1)

                def sums(n):
                    d_, t = items[n]
                    pe.wait_ge(S("log_gates"), h * NI + (n + 1))
                    if n >= 1:
                        pe.wait_ge(S("exps_done"), h * NI + n)
                    b0 = 1 * BANK
                    pe.matmul(ps[:, b0:b0 + DK], masks[:, 2 * d_ * P:(2 * d_ + 1) * P], lg[n % 2], start=True, stop=True)
                    pe.matmul(ps[:, b0 + DK:b0 + 2 * DK], masks[:, (2 * d_ + 1) * P:(2 * d_ + 2) * P], lg[n % 2], start=True, stop=True)
                    pe.matmul(ps[:, b0 + 2 * DK:b0 + 2 * DK + 2], lg[n % 2], masks[:, 4 * P:4 * P + 2], start=True, stop=True) \
                        .then_inc(S("gate_sums"), 1)

                def turn(n):
                    pe.wait_ge(S("qk_gated"), h * NI + (n + 1))
                    if n >= 1:
                        pe.wait_ge(S("gated_turned_kept"), h * NI + n)
                    for a in range(2):
                        m = pe.transpose(ps[:, 2 * BANK + a * P:2 * BANK + (a + 1) * P], qkd[n % 3][:, a, :], ident[:, :])
                    m.then_inc(S("gated_turned"), 1)

                def intra(n):
                    pe.wait_ge(S("gated_turned_kept"), h * NI + (n + 1))
                    if n >= 1:
                        pe.wait_ge(S("intra_masked"), h * NI + n)
                    pe.matmul(bank(3, P), qkT[n % 2][:, 1, :], qkT[n % 2][:, 0, :], start=True, stop=True).then_inc(S("intra_done"), 1)

                def out(n):
                    d_, t = items[n]
                    v = qkv[:, t, 2 * DK:2 * DK + DV]
                    ob = 4 + n % 2
                    pe.wait_ge(S("intra_masked"), h * NI + (n + 1))
                    if n >= 2:
                        pe.wait_ge(S("out_kept"), h * NI + (n - 1))
                    pe.matmul(bank(ob, DV), am[d_], v, start=True, stop=False, skip_group_check=True)
                    for x, ck_ in enumerate((0, 1) if d_ == 0 else (1, 0)):
                        kb = 6 + x
                        if n >= 1:
                            pe.wait_ge(S("state_moved"), h * 2 * NI + (2 * n - 1 + x))
                        rows = slice(ck_ * CHUNK, (ck_ + 1) * CHUNK)
                        pe.matmul(bank(kb, DV), qkd[n % 3][rows, 2, :], qkv[rows, t, 2 * DK:2 * DK + DV], start=True, stop=True) \
                            .then_inc(S("chunk_kv"), 1)
                    for x, ck_ in enumerate((0, 1) if d_ == 0 else (1, 0)):
                        rows = slice(ck_ * CHUNK, (ck_ + 1) * CHUNK)
                        if x == 0:
                            pe.wait_ge(S("state_before"), h * NI + (n + 1))
                        else:
                            pe.wait_ge(S("state_moved"), h * 2 * NI + (2 * n + 1))
                        pe.matmul(ps[rows, ob * BANK:ob * BANK + DV], qkT[n % 2][:, 0, rows], Sst[d_][x],
                                  start=False, stop=(x == 1), skip_group_check=True) \
                            .then_inc(S("first_chunk_out" if x == 0 else "tile_out"), 1)

                for n in range(NI + 3):
                    if n < NI:
                        gate(n)
                    if 0 <= n - 1 < NI:
                        sums(n - 1)
                    if 0 <= n - 2 < NI:
                        turn(n - 2)
                        intra(n - 2)
                    if 0 <= n - 3 < NI:
                        out(n - 3)
                pe.wait_ge(w_full[(gla_u + 1) % 2], h * 16 + w_ready[gla_u + 1])
                for t in range(NT + 1):
                    if t < NT:
                        if t >= 2:
                            pe.wait_ge(S("r_used"), h * NT + (t - 1))
                        elif t == 0:
                            pe.wait_ge(S("gate_logit_used"), h * NI + NI)
                            pe.wait_ge(S("exps_done"), h * NI + NI)
                        gemm(pe, bank(t % 2, DV), lambda q: hT[:, q, t * P:(t + 1) * P], (gla_u + 1) % 2, DV).then_inc(S("r_done"), 1)
                        if t == NT - 1:
                            pe.wait_ge(S("r_done"), h * NT + NT)
                            pe.sem_inc(w_free[(gla_u + 1) % 2], 1)
                    if t >= 1:
                        pe.wait_ge(S("gated_out"), h * NT + t)
                        if t >= 2:
                            pe.wait_ge(S("gated_out_kept"), h * NT + (t - 1))
                        for a in range(2):
                            m = pe.transpose(ps[:, 2 * BANK + a * P:2 * BANK + (a + 1) * P], on[:, a * P:(a + 1) * P], ident[:, :])
                        m.then_inc(S("gated_out_turned"), 1)
                pe.wait_ge(S("gated_out_kept"), h * NT + NT)
            end(pe, "pe")

        def act_gla(act, ch):
            begin(act, "act", 5)
            for n, (c0, w) in enumerate(((0, 512), (512, 512), (1024, 256))):
                act.wait_ge(S("low_rank_done"), n + 1)
                act.activation(gkT[0:32, c0:c0 + w], ps[0:32, n * BANK:n * BANK + w], ACT.Copy).then_inc(S("low_rank_kept"), 1)
            with act.Fori(0, GH) as h:
                ch.enter(h, ACT_PER)
                for t in range(NT):
                    act.wait_ge(S("qkv_done"), h * NT + (t + 1))
                    ch(act.activation(qkv[:, t, 0:DK], bank(t % 2, DK), ACT.Copy, scale=GSCALE))
                    act.activation(qkv[:, t, DK:BLK], ps[:, (t % 2) * BANK + DK:(t % 2 + 1) * BANK], ACT.Copy).then_inc(S("qkv_kept"), 1)

                def logs(n):
                    act.wait_ge(S("gate_logits"), h * NI + (n + 1))
                    if n >= 1:
                        act.wait_ge(S("log_gates"), h * NI + n)
                    ch(act.activation(glt, bank(0, DK), ACT.Abs))
                    ch(act.activation(glt, glt, ACT.Exp, scale=-1.0))
                    act.activation(glt, glt, ACT.Ln, bias=1.0).then_inc(S("softplus_done"), 1)
                    act.wait_ge(S("softplus_done"), h * NI + (n + 1))

                def exps(n):
                    act.wait_ge(S("gate_sums"), h * NI + (n + 1))
                    if n >= 2:
                        act.wait_ge(S("qk_gated"), h * NI + (n - 1))
                    if n >= 4:
                        act.wait_ge(S("state_moved"), h * 2 * NI + 2 * (n - 3))
                    e = ex[n % 2]
                    ch(act.activation(e[:, 0:2, :], ps[:, BANK:BANK + 2 * DK].rearrange("p (a n) -> p a n", a=2), ACT.Exp, scale=1.0 / GATE_NORM))
                    ch(act.activation(e[:, 2, :], bank(1, DK), ACT.Exp, scale=-1.0 / GATE_NORM))
                    act.activation(dec[n % 4], ps[:, BANK + 2 * DK:BANK + 2 * DK + 2], ACT.Exp, scale=1.0 / GATE_NORM).then_inc(S("exps_done"), 1)
                    act.wait_ge(S("exps_done"), h * NI + (n + 1))

                def keep_turned(n):
                    act.wait_ge(S("gated_turned"), h * NI + (n + 1))
                    if n >= 2:
                        act.wait_ge(S("tile_out"), h * NI + (n - 1))
                    act.activation(qkT[n % 2], bank(2, 2 * P).rearrange("p (a n) -> p a n", a=2), ACT.Copy).then_inc(S("gated_turned_kept"), 1)
                    act.wait_ge(S("gated_turned_kept"), h * NI + (n + 1))

                for n in range(NI + 2):
                    if n < NI:
                        logs(n)
                    if 0 <= n - 1 < NI:
                        exps(n - 1)
                    if 0 <= n - 2 < NI:
                        keep_turned(n - 2)
                for t in range(NT):
                    act.wait_ge(S("r_done"), h * NT + (t + 1))
                    if t >= 1:
                        act.wait_ge(S("gated_out"), h * NT + t)
                    act.activation(rs[0], bank(t % 2, DV), ACT.Silu).then_inc(S("r_used"), 1)
                    act.wait_ge(S("r_used"), h * NT + (t + 1))
                ch.leave(GH)
            end(act, "act")

        ACT_PER = NT + NI * 2 + NI * 2

        def pool_gla(pool, ch):
            begin(pool, "pool", 5)
            ch(pool.memset(gkT[32:33, :], 1.0))
            pool.memset(wg[:, :, :], 0.0).then_inc(S("gate_weights_cleared"), 1)
            with pool.Fori(0, GH) as h:
                for t in range(NT):
                    pool.wait_ge(S("out_var"), h * NT + (t + 1))
                    pool.tensor_tensor(gst[:, 4:5], gst[:, 2:3], mhalf[:, 0:1], ALU.pow).then_inc(S("out_rstd"), 1)
            pool.wait_ge(S("ctx_state_stored"), 32 * GH)
            end(pool, "pool")

        def dve_gla(dve, ch):
            begin(dve, "dve", 5)
            for d_ in range(2):
                ch(dve.memset(am[d_], 0.0))
            with dve.Fori(0, GH) as h:
                ch.enter(h, DVE_PER)

                def loggate(n):
                    dve.wait_ge(S("softplus_done"), h * NI + (n + 1))
                    if n >= 2:
                        dve.wait_ge(S("gate_sums"), h * NI + (n - 1))
                    ch(dve.scalar_tensor_tensor(lg[n % 2], bank(0, DK), 0.0, glt, ALU.min, ALU.subtract))
                    dve.sem_inc(S("gate_logit_used"), 1)
                    dve.sem_inc(S("log_gates"), 1)

                def gated(n):
                    d_, t = items[n]
                    dve.wait_ge(S("exps_done"), h * NI + (n + 1))
                    if n >= 3:
                        dve.wait_ge(S("tile_out"), h * NI + (n - 2))
                    e, o = ex[n % 2], qkd[n % 3]
                    ch(dve.tensor_tensor(o[:, 0, :], qkv[:, t, 0:DK], e[:, 0, :], ALU.mult))
                    ch(dve.tensor_tensor(o[:, 1, :], qkv[:, t, DK:2 * DK], e[:, 2, :], ALU.mult))
                    dve.tensor_tensor(o[:, 2, :], qkv[:, t, DK:2 * DK], e[:, 1, :], ALU.mult).then_inc(S("qk_gated"), 1)
                    dve.wait_ge(S("qk_gated"), h * NI + (n + 1))

                def masked(n):
                    d_, t = items[n]
                    dve.wait_ge(S("intra_done"), h * NI + (n + 1))
                    if n >= 2:
                        dve.wait_ge(S("tile_out"), h * NI + (n - 1))
                    dve.sem_inc(S("mask_turns"), 1)
                    ch(dve.copy_predicated(am[d_], keep[:, d_ * P:(d_ + 1) * P], bank(3, P)))
                    dve.sem_inc(S("intra_masked"), 1)

                def states(n):
                    d_, t = items[n]
                    ctx_start = t == (0 if d_ == 0 else 1)
                    if n < 2:
                        dve.wait_ge(S("state_landed"), h * 32 + 32)
                    if n >= 2:
                        dve.wait_ge(S("tile_out"), h * NI + (n - 1))
                    if ctx_start:
                        ch(dve.memset(Sst[d_][0], 0.0))
                    dve.sem_inc(S("state_before"), 1)
                    for x, ck_ in enumerate((0, 1) if d_ == 0 else (1, 0)):
                        dve.wait_ge(S("chunk_kv"), h * 2 * NI + (2 * n + 1 + x))
                        if x == 1:
                            dve.wait_ge(S("first_chunk_out"), h * NI + (n + 1))
                        ch(dve.scalar_tensor_tensor(Sst[d_][1 - x], Sst[d_][x], dec[n % 4][:, ck_:ck_ + 1], bank(6 + x, DV), ALU.mult, ALU.add))
                        dve.sem_inc(S("state_moved"), 1)
                    if t == (T_CTX - 1 if d_ == 0 else 0):
                        dve.sem_inc(S(f"ctx_state_final{d_}"), 1)

                def keep_out(n):
                    d_, t = items[n]
                    dve.wait_ge(S("tile_out"), h * NI + (n + 1))
                    src = bank(4 + n % 2, DV)
                    if first_touch[n]:
                        i = dve.tensor_copy(o_tile(t), src)
                    else:
                        i = dve.tensor_tensor(o_tile(t), o_tile(t), src, ALU.add)
                    i.then_inc(S("out_kept"), 1)
                    dve.wait_ge(S("out_kept"), h * NI + (n + 1))

                for n in range(NI + 3):
                    if n < NI:
                        loggate(n)
                    if 0 <= n - 1 < NI:
                        gated(n - 1)
                    if 0 <= n - 2 < NI:
                        masked(n - 2)
                    if 0 <= n - 3 < NI:
                        states(n - 3)
                        keep_out(n - 3)
                for t in range(NT):
                    if t >= 1:
                        dve.wait_ge(S("gated_out_turned"), h * NT + t)
                    ch(dve.tensor_tensor(on, o_tile(t), o_tile(t), ALU.mult))
                    ch(dve.tensor_reduce(gst[:, 0:1], on, AX, ALU.add))
                    dve.tensor_scalar(gst[:, 2:3], gst[:, 0:1], 1.0 / DV, EPS, ALU.mult, ALU.add).then_inc(S("out_var"), 1)
                    dve.wait_ge(S("out_rstd"), h * NT + (t + 1))
                    dve.wait_ge(S("r_used"), h * NT + (t + 1))
                    dve.scalar_tensor_tensor(on, o_tile(t), gst[:, 4:5], rs[0], ALU.mult, ALU.mult).then_inc(S("gated_out"), 1)
                    dve.wait_ge(S("gated_out"), h * NT + (t + 1))
                    dve.wait_ge(S("gated_out_turned"), h * NT + (t + 1))
                    for a in range(2):
                        o = h * (2 * N_TOK) + (a * N_TOK + t * P)
                        ch(dve.tensor_scalar(R2[:, ds(o, P)], ps[:, 2 * BANK + a * P:2 * BANK + (a + 1) * P], ggT[:, a:a + 1], None, ALU.mult))
                    dve.sem_inc(S("gated_out_kept"), 1)
                ch.leave(GH)
                dve.sem_inc(S("head_done"), 1)
            end(dve, "dve")

        DVE_PER = NI + 2 * NI + NI + 2 * NI + 2 + 4 * NT

        pe_mb, act_mb, dve_mb = merge(mb_u, lambda q, t: ogT[:, q, t * P:(t + 1) * P], "gla", 6, True)

        def sp_mb(sp):
            for u in (mb_u + 2, mb_u + 3, out_u, out_u + 1):
                load_unit(sp, u)

        mixT = R1[:, :].rearrange("p (k t) -> p k t", k=KD)
        G1b = [work(D, at=0)] + [work(D)]
        xr = [work(D) for _ in range(2)]
        x1b = [work(D) for _ in range(2)]
        xh = [work(D) for _ in range(2)]
        sqo = work(D)
        h2T = [work(D).rearrange("p (k t) -> p k t", k=KD) for _ in range(2)]
        colb = R2[:, N_TOK:N_TOK + 2 * P].rearrange("p (a n) -> p a n", a=2)
        aff = R2[:, N_TOK + 2 * P:N_TOK + 2 * P + 2 * NE].rearrange("p (a n) -> p a n", a=2)
        ones = R2[:, N_TOK + 4 * P:N_TOK + 5 * P]
        so = st[:, 0:24]

        def bcast_cols(n):
            return n // KD, n % KD

        def pe_bcast(pe, n0, nb):
            for n in range(2 * KD):
                pe.wait_ge(S("columns_spread"), n0 + n + 1)
                if n >= 2:
                    pe.wait_ge(S("rows_kept"), n0 + n - 1)
                pe.matmul(bank(nb + n % 2, P), colb[:, n % 2, :], ident[:, :], start=True, stop=True).then_inc(S("rows_spread"), 1)

        def dve_bcast(dve, ch, n0, nb, G, dst):
            ch(dve.memset(ones, 1.0))

            def spread(n):
                j, k = bcast_cols(n)
                if n >= 2:
                    dve.wait_ge(S("rows_spread"), n0 + n - 1)
                dve.tensor_scalar(colb[:, n % 2, :], ones, G[:, k, j:j + 1], None, ALU.mult).then_inc(S("columns_spread"), 1)
            spread(0)
            for n in range(2 * KD):
                if n + 1 < 2 * KD:
                    spread(n + 1)
                j, k = bcast_cols(n)
                dve.wait_ge(S("rows_spread"), n0 + n + 1)
                dve.tensor_copy(dst[j][:, k * P:(k + 1) * P], bank(nb + n % 2, P)).then_inc(S("rows_kept"), 1)
                dve.wait_ge(S("rows_kept"), n0 + n + 1)

        def sp_out(sp):
            begin(sp, "sp", 7)
            for t in range(NT):
                if t >= 2:
                    sp.wait_ge(S("x1_made"), t - 1)
                sp.dma_start(xr[t % 2], x_rows(t)).then_inc(S(f"x_again{t % 2}"), 16)
                if t >= 1:
                    store_out(sp, t - 1)
            store_out(sp, NT - 1)

        def store_out(sp, t):
            sp.wait_ge(S("xhat_made"), t + 1)
            sp.dma_start(x1_dram[t * P:(t + 1) * P, :], x1b[t % 2]).then_inc(S(f"x1_stored{t % 2}"), 16)
            sp.dma_start(xhat_dram[t * P:(t + 1) * P, :], xh[t % 2]).then_inc(S(f"x1_stored{t % 2}"), 16)

        def pe_out(pe):
            begin(pe, "pe", 7)
            for t in range(NT):
                if t >= 2:
                    pe.wait_ge(S("mixT_act"), t - 1)
                    pe.wait_ge(S("mixT_dve"), t - 1)
                for k in range(KD):
                    o = (2 * (t % 2)) * BANK + k * P
                    m = pe.transpose(ps[:, o:o + P], mix[:, t, k * P:(k + 1) * P], ident[:, :])
                m.then_inc(S("mix_turned"), 1)
            pe_bcast(pe, 0, 6)
            for s in range(2):
                pe.wait_ge(w_full[(out_u + s) % 2], w_ready[out_u + s])
            pe.wait_ge(S("mixT_act"), NT)
            pe.wait_ge(S("mixT_dve"), NT)

            def project(t, cb):
                b = 2 * (t % 2) + cb
                if t >= 2 and cb == 0:
                    pe.wait_ge(S("out_banks_free"), t - 1)
                gemm(pe, bank(b), lambda q: mixT[:, q, t * P:(t + 1) * P], (out_u + cb) % 2).then_inc(S("out_done"), 1)

            def turn(t):
                pe.wait_ge(S("xhat_made"), t + 1)
                if t >= 1:
                    pe.wait_ge(S("h2_kept_act"), t)
                    pe.wait_ge(S("h2_kept_dve"), t)
                for k in range(KD):
                    m = pe.transpose(ps[:, 4 * BANK + k * P:4 * BANK + (k + 1) * P], xh[t % 2][:, k * P:(k + 1) * P], ident[:, :])
                m.then_inc(S("xhat_turned"), 1)

            def route(t):
                pe.wait_ge(S("h2_kept_act"), t + 1)
                pe.wait_ge(S("h2_kept_dve"), t + 1)
                if t >= 1:
                    pe.wait_ge(S("aff_made"), t)
                for k in range(KD):
                    m = pe.matmul(bank(6, NE), h2T[t % 2][:, k, :], wr[:, k, :], start=(k == 0), stop=(k == KD - 1))
                m.then_inc(S("routed"), 1)

            def turn_aff(t):
                pe.wait_ge(S("aff_made"), t + 1)
                if t >= 1:
                    pe.wait_ge(S("aff_kept"), t)
                pe.transpose(ps[0:NE, 7 * BANK:7 * BANK + P], aff[:, t % 2, :], ident[:, :]).then_inc(S("aff_turned"), 1)

            for t in range(NT + 2):
                if t < NT:
                    project(t, 0)
                if 0 <= t - 1 < NT:
                    turn(t - 1)
                if t < NT:
                    project(t, 1)
                if 0 <= t - 1 < NT:
                    route(t - 1)
                if 0 <= t - 2 < NT:
                    turn_aff(t - 2)
            end(pe, "pe")

        def act_out(act, ch):
            begin(act, "act", 7)
            for t in range(NT):
                act.wait_ge(S("mix_turned"), t + 1)
                b = 2 * (t % 2)
                act.activation(mixT[:, 0:4, t * P:(t + 1) * P], bank(b).rearrange("p (k t) -> p k t", k=4), ACT.Copy).then_inc(S("mixT_act"), 1)
                act.wait_ge(S("mixT_act"), t + 1)

            def square_mix(t):
                act.wait_ge(S("out_done"), 2 * t + 2)
                for cb in range(2):
                    ch(act.activation(sqo[:, cb * BLK:(cb + 1) * BLK], bank(2 * (t % 2) + cb), ACT.Square, accum_out=so[:, cb:cb + 1]))
                act.sem_inc(S("mix_squared"), 1)

            def square_x1(t):
                act.wait_ge(S("x1_made"), t + 1)
                act.activation(sqo[:, :], x1b[t % 2], ACT.Square, accum_out=so[:, 2:3]).then_inc(S("x1_squared"), 1)
                act.wait_ge(S("x1_squared"), t + 1)

            def keep_h2(t):
                j = kind_of(t)
                act.wait_ge(S("xhat_turned"), t + 1)
                if t >= 2:
                    act.wait_ge(S("routed"), t - 1)
                for k in range(4):
                    ch(act.activation(h2T[t % 2][:, k, :], ps[:, 4 * BANK + k * P:4 * BANK + (k + 1) * P], ACT.Identity,
                                      scale=A2[:, k, j:j + 1], bias=modT[:, 24 + k, j:j + 1]))
                act.sem_inc(S("h2_kept_act"), 1)

            def soft(t):
                act.wait_ge(S("router_max"), t + 1)
                act.activation(aff[:, t % 2, :], bank(6, NE), ACT.Exp, bias=so[:, 8:9], accum_out=so[:, 9:10]).then_inc(S("router_exp"), 1)
                act.wait_ge(S("router_exp"), t + 1)

            def keep_aff(t):
                act.wait_ge(S("aff_turned"), t + 1)
                act.activation(affT[:, t * P:(t + 1) * P], ps[0:NE, 7 * BANK:7 * BANK + P], ACT.Copy).then_inc(S("aff_kept"), 1)
                act.wait_ge(S("aff_kept"), t + 1)

            for t in range(NT + 2):
                if t < NT:
                    square_mix(t)
                if 0 <= t - 1 < NT:
                    keep_h2(t - 1)
                if t < NT:
                    square_x1(t)
                if 0 <= t - 1 < NT:
                    soft(t - 1)
                if 0 <= t - 2 < NT:
                    keep_aff(t - 2)
            end(act, "act")

        def pool_out(pool, ch):
            begin(pool, "pool", 7)
            for n in range(2 * NT):
                pool.wait_ge(S("out_vars"), n + 1)
                o = 4 + n % 2
                pool.tensor_tensor(so[:, o + 2:o + 3], so[:, o:o + 1], mhalf[:, 0:1], ALU.pow).then_inc(S("out_rstds"), 1)
            for t in range(2):
                pool.wait_ge(S(f"x1_stored{t}"), 32 * (NT // 2))
            end(pool, "pool")

        def dve_out(dve, ch):
            begin(dve, "dve", 7)
            for t in range(NT):
                dve.wait_ge(S("mix_turned"), t + 1)
                b = 2 * (t % 2) + 1
                dve.tensor_copy(mixT[:, 4:8, t * P:(t + 1) * P], bank(b).rearrange("p (k t) -> p k t", k=4)).then_inc(S("mixT_dve"), 1)
                dve.wait_ge(S("mixT_dve"), t + 1)
            dve_bcast(dve, ch, 0, 6, G1, G1b)

            def residual(t):
                j = kind_of(t)
                dve.wait_ge(S("mix_squared"), t + 1)
                ch(dve.tensor_tensor(so[:, 3:4], so[:, 0:1], so[:, 1:2], ALU.add))
                ch(dve.tensor_scalar(so[:, 4:5], so[:, 3:4], 1.0 / D, EPS, ALU.mult, ALU.add))
                dve.sem_inc(S("out_vars"), 1)
                dve.wait_ge(S("out_rstds"), 2 * t + 1)
                if t >= 2:
                    dve.wait_ge(S(f"x1_stored{t % 2}"), 32 * (t // 2))
                for cb in range(2):
                    ch(dve.scalar_tensor_tensor(x1b[t % 2][:, cb * BLK:(cb + 1) * BLK], bank(2 * (t % 2) + cb), so[:, 6:7],
                                                G1b[j][:, cb * BLK:(cb + 1) * BLK], ALU.mult, ALU.mult))
                dve.sem_inc(S("out_banks_free"), 1)
                dve.wait_ge(S(f"x_again{t % 2}"), 16 * (t // 2 + 1))
                dve.tensor_tensor(x1b[t % 2], x1b[t % 2], xr[t % 2], ALU.add).then_inc(S("x1_made"), 1)
                dve.wait_ge(S("x1_made"), t + 1)

            def normal(t):
                dve.wait_ge(S("x1_squared"), t + 1)
                ch(dve.tensor_scalar(so[:, 5:6], so[:, 2:3], 1.0 / D, EPS, ALU.mult, ALU.add))
                dve.sem_inc(S("out_vars"), 1)
                dve.wait_ge(S("out_rstds"), 2 * t + 2)
                if t >= 2:
                    dve.wait_ge(S("xhat_turned"), t - 1)
                dve.tensor_scalar(xh[t % 2], x1b[t % 2], so[:, 7:8], None, ALU.mult).then_inc(S("xhat_made"), 1)
                dve.wait_ge(S("xhat_made"), t + 1)

            def keep_h2(t):
                j = kind_of(t)
                dve.wait_ge(S("xhat_turned"), t + 1)
                if t >= 2:
                    dve.wait_ge(S("routed"), t - 1)
                for k in range(4, 8):
                    ch(dve.tensor_scalar(h2T[t % 2][:, k, :], ps[:, 4 * BANK + k * P:4 * BANK + (k + 1) * P],
                                         A2[:, k, j:j + 1], modT[:, 24 + k, j:j + 1], ALU.mult, ALU.add))
                dve.sem_inc(S("h2_kept_dve"), 1)

            def soft(t):
                dve.wait_ge(S("routed"), t + 1)
                ch(dve.tensor_reduce(so[:, 10:11], bank(6, NE), AX, ALU.max))
                if t >= 2:
                    dve.wait_ge(S("aff_turned"), t - 1)
                dve.tensor_scalar(so[:, 8:9], so[:, 10:11], -1.0, None, ALU.mult).then_inc(S("router_max"), 1)
                dve.wait_ge(S("router_exp"), t + 1)
                ch(dve.reciprocal(so[:, 11:12], so[:, 9:10]))
                ch(dve.tensor_scalar(aff[:, t % 2, :], aff[:, t % 2, :], so[:, 11:12], None, ALU.mult))
                dve.sem_inc(S("aff_made"), 1)

            for t in range(NT + 1):
                if t < NT:
                    residual(t)
                if t >= 1:
                    keep_h2(t - 1)
                if t < NT:
                    normal(t)
                if t >= 1:
                    soft(t - 1)
            end(dve, "dve")

        affw = RW[0:NE, 0:N_TOK]
        topv = RW[0:NE, N_TOK:N_TOK + CAP]
        topi = RW[0:NE, 2 * N_TOK:2 * N_TOK + CAP].bitcast(U32)
        topf = RW[0:NE, N_TOK + CAP:N_TOK + 2 * CAP]
        val = [st[:, 24:40], st[:, 40:56]]
        idxu = [WK[0:CAP_CTX, 0:NE].bitcast(U32), WK[0:CAP_LAT, NE:2 * NE].bitcast(U32)]
        zero = RW[:, 4 * D:5 * D]
        kinds = ((0, 0, N_CTX, 0, CAP_CTX), (1, N_CTX, N_TOK, CAP_CTX, CAP_LAT))

        def dve_topk(dve, ch):
            begin(dve, "dve", 8)
            dve.memset(zero, 0.0).then_inc(S("zero_made"), 1)
            dve.wait_ge(S("zero_made"), 1)
            for kind, lo, hi, at, cap in kinds:
                cur = affT[:, lo:hi]
                for r in range(cap // 8):
                    v = topv[:, at + 8 * r:at + 8 * r + 8]
                    ch(dve.max(v, cur))
                    ch(dve.max_index(topi[:, at + 8 * r:at + 8 * r + 8], v, cur))
                    if r + 1 < cap // 8:
                        ch(dve.match_replace(affw[:, lo:hi], v, cur, -1.0))
                        cur = affw[:, lo:hi]
            ch(dve.tensor_copy(topf, topi[:, :]))
            ch(dve.tensor_scalar(topf[:, CAP_CTX:CAP], topf[:, CAP_CTX:CAP], float(N_CTX), None, ALU.add))
            dve.sem_inc(S("chosen"), 1)
            dve.wait_ge(S("chosen_turned"), 1)
            for kind, lo, hi, at, cap in kinds:
                ch(dve.tensor_copy(val[kind][0:cap, :], ps[0:cap, 2 * kind * BANK:2 * kind * BANK + NE]))
                ch(dve.tensor_copy(idxu[kind][:, :], ps[0:cap, (2 * kind + 1) * BANK:(2 * kind + 1) * BANK + NE]))
            end(dve, "dve")

        def pe_topk(pe):
            begin(pe, "pe", 8)
            pe.wait_ge(S("chosen"), 1)
            for kind, lo, hi, at, cap in kinds:
                for a, src in enumerate((topv, topf)):
                    b = 2 * kind + a
                    m = pe.transpose(ps[0:cap, b * BANK:b * BANK + NE], src[:, at:at + cap], ident[0:NE, 0:NE])
            m.then_inc(S("chosen_turned"), 1)
            end(pe, "pe")

        def act_idle(k):
            def f(act, ch):
                begin(act, "act", k)
                end(act, "act")
            return f

        def sp_topk(sp):
            begin(sp, "sp", 8)
            for n in range(3):
                for half in range(2):
                    load_expert(sp, 0, n, half)
            sp.wait_ge(S("zero_made"), 1)
            for t in range(NT):
                sp.dma_start(ffn_dram[t * P:(t + 1) * P, :], zero).then_inc(S("ffn_cleared"), 16)

        We = [R1[:, 0:8 * D], R2[:, 2 * D:10 * D], R3[:, 0:8 * D]]
        We = [w.rearrange("p (k n) -> p k n", k=KD) for w in We]
        xg = [work(D, at=64), work(D)]
        xe = work(KD * CAP).rearrange("p (k c) -> p k c", k=KD)
        sl = [work(CAP) for _ in range(2)]
        hid = work(KD * CAP).rearrange("p (k c) -> p k c", k=KD)
        yT = work(KD * CAP).rearrange("p (k c) -> p k c", k=KD)
        yo = [work(D), work(D)]
        ist_g = [WK[0:CAP_CTX, 2 * NE:2 * NE + 1].bitcast(U32), WK[0:CAP_LAT, 2 * NE + 1:2 * NE + 2].bitcast(U32)]
        ist_a = [WK[0:CAP_CTX, 2 * NE + 2:2 * NE + 3].bitcast(U32), WK[0:CAP_LAT, 2 * NE + 3:2 * NE + 4].bitcast(U32)]
        vst = [st[:, 56:57], st[:, 57:58]]
        COL = (CAP_LAT, 0)
        CAPS = (CAP_CTX, CAP_LAT)
        we_dram = (w1[0], w3[0], w2[0])

        def load_expert(sp, e, n, half):
            src = we_dram[n][e] if isinstance(e, int) else we_dram[n][ds(e, 1)].rearrange("a k n -> (a k) n")
            cols = slice(half * BLK, (half + 1) * BLK)
            sp.dma_start(We[n][:, :, cols], src[:, cols].rearrange("(k p) n -> p k n", p=P)).then_inc(S(f"expert_landed{n}{half}"), 16)

        def sp_moe(sp):
            with sp.Fori(1, NE) as e:
                for half in range(2):
                    sp.wait_ge(S("up_half_used"), e * 2 - 1 + half)
                    load_expert(sp, e, 0, half)
                    load_expert(sp, e, 1, half)
                for half in range(2):
                    sp.wait_ge(S("down_half_used"), e * 2 - 1 + half)
                    load_expert(sp, e, 2, half)

        def pool_moe(pool, ch):
            begin(pool, "pool", 9)

            def gather(e):
                for kind in range(2):
                    ch(pool.tensor_copy(ist_g[kind][:, :], idxu[kind][:, ds(e, 1)]))
                pool.sem_inc(S("pool_turns"), 1)
                for kind in (1, 0):
                    pool.indirect_dma_start(xg[kind][0:CAPS[kind], :], None, xhat_dram,
                                            bass.IndirectOffsetOnAxis(ap=ist_g[kind][:, 0:1], axis=0)).then_inc(S("rows_gathered"), 16)

            def add_back(e):
                for kind in range(2):
                    ch(pool.tensor_copy(ist_a[kind][:, :], idxu[kind][:, ds(e, 1)]))
                ch(pool.tensor_copy(vst[1], val[1][:, ds(e, 1)]))
                pool.tensor_copy(vst[0][0:CAP_CTX, :], val[0][0:CAP_CTX, ds(e, 1)]).then_inc(S("scales_staged"), 1)
                pool.wait_ge(S("rows_scaled"), e + 1)
                pool.sem_inc(S("pool_turns"), 1)
                for kind in (1, 0):
                    pool.indirect_dma_start(ffn_dram, bass.IndirectOffsetOnAxis(ap=ist_a[kind][:, 0:1], axis=0),
                                            yo[kind][0:CAPS[kind], :], None, compute_op=ALU.add).then_inc(S("rows_added"), 16)
                pool.wait_ge(S("rows_added"), e * 32 + 32)

            gather(0)
            pool.wait_ge(S("ffn_cleared"), 16 * NT)
            with pool.Fori(1, NE) as e:
                ch.enter(e - 1, 5)
                pool.wait_ge(S("slots_turned"), e * 4)
                gather(e)
                add_back(e - 1)
                ch.leave(NE - 1)
            add_back(NE - 1)
            end(pool, "pool")

        def pe_moe(pe):
            begin(pe, "pe", 9)

            def turn_slots(e, q):
                if q == 0:
                    pe.wait_ge(S("rows_gathered"), e * 32 + 32)
                if q >= 2:
                    pe.wait_ge(S("slots_kept_act") if q % 2 == 0 else S("slots_kept_dve"), e * 2 + 1)
                for k in (2 * q, 2 * q + 1):
                    for kind in (1, 0):
                        cap = CAPS[kind]
                        o = (2 + q % 2) * BANK + (k % 2) * CAP + COL[kind]
                        m = pe.transpose(ps[:, o:o + cap], xg[kind][0:cap, k * P:(k + 1) * P], ident[0:cap, 0:cap])
                m.then_inc(S("slots_turned"), 1)

            def turn_rows(e, half):
                if half == 0:
                    pe.wait_ge(S("down_kept"), e * KD + KD)
                    pe.wait_ge(S("slots_kept_act"), e * 2 + 2)
                    pe.wait_ge(S("slots_kept_dve"), e * 2 + 2)
                else:
                    pe.wait_ge(S("rows_half_scaled"), e + 1)
                for k in range(4 * half, 4 * half + 4):
                    o = (k % 4) * P
                    pe.transpose(ps[:, 2 * BANK + o:2 * BANK + o + P], yT[:, k, 0:CAP_LAT], ident[:, :])
                    m = pe.transpose(ps[0:CAP_CTX, 3 * BANK + o:3 * BANK + o + P], yT[:, k, CAP_LAT:CAP], ident[:, :])
                m.then_inc(S("rows_turned"), 1)

            def up(e, rows):
                pe.wait_ge(S("slots_kept_act"), e * 2 + 2)
                pe.wait_ge(S("slots_kept_dve"), e * 2 + 2)
                for f in range(KD):
                    if f % 4 == 0:
                        for a in range(2):
                            pe.wait_ge(S(f"expert_landed{a}{f // 4}"), e * 16 + 16)
                    for a in range(2):
                        if rows or f >= 2:
                            pe.wait_ge(S("hidden_made"), e * KD + (f - 1))
                        for k in range(KD):
                            m = pe.matmul(bank(4 + 2 * a + f % 2, CAP), We[a][:, k, f * P:(f + 1) * P], xe[:, k, :], start=(k == 0), stop=(k == KD - 1))
                        m.then_inc(S(f"up_done{a}"), 1)
                    if f % 4 == 3:
                        pe.wait_ge(S("up_done1"), e * KD + (f + 1))
                        pe.sem_inc(S("up_half_used"), 1)
                    if rows and f < 2:
                        turn_rows(e - 1, f)

            def down(e, slots_too):
                pe.wait_ge(S("hidden_made"), e * KD + KD)
                for d in range(KD):
                    if d % 4 == 0:
                        pe.wait_ge(S(f"expert_landed2{d // 4}"), e * 16 + 16)
                    if d >= 2:
                        pe.wait_ge(S("down_kept"), e * KD + (d - 1))
                    for k in range(KD):
                        m = pe.matmul(bank(d % 2, CAP), We[2][:, k, d * P:(d + 1) * P], hid[:, k, :], start=(k == 0), stop=(k == KD - 1))
                    m.then_inc(S("down_done"), 1)
                    if d % 4 == 3:
                        pe.wait_ge(S("down_done"), e * KD + (d + 1))
                        pe.sem_inc(S("down_half_used"), 1)
                    if slots_too and d < 4:
                        turn_slots(e + 1, d)

            for q in range(4):
                turn_slots(0, q)
            up(0, False)
            with pe.Fori(1, NE) as e:
                down(e - 1, True)
                up(e, True)
            down(NE - 1, False)
            for half in range(2):
                turn_rows(NE - 1, half)
            end(pe, "pe")

        def slots(q):
            for k in (2 * q, 2 * q + 1):
                for kind in (1, 0):
                    o = (2 + q % 2) * BANK + (k % 2) * CAP + COL[kind]
                    yield xe[:, k, COL[kind]:COL[kind] + CAPS[kind]], ps[:, o:o + CAPS[kind]], k, kind

        def act_moe(act, ch):
            begin(act, "act", 9)

            def keep_slots(e, q):
                act.wait_ge(S("slots_turned"), e * 4 + (q + 1))
                for dst, src, k, kind in slots(q):
                    ch(act.activation(dst, src, ACT.Identity, scale=A2[:, k, kind:kind + 1], bias=modT[:, 24 + k, kind:kind + 1]))
                act.sem_inc(S("slots_kept_act"), 1)

            def gates(e):
                for f in range(KD):
                    act.wait_ge(S("up_done0"), e * KD + (f + 1))
                    if f >= 2:
                        act.wait_ge(S("hidden_made"), e * KD + (f - 1))
                    act.activation(sl[f % 2], bank(4 + f % 2, CAP), ACT.Silu).then_inc(S("silu_made"), 1)
                    act.wait_ge(S("silu_made"), e * KD + (f + 1))

            def keep_down(e, slots_too):
                for d in range(KD):
                    act.wait_ge(S("down_done"), e * KD + (d + 1))
                    act.activation(yT[:, d, :], bank(d % 2, CAP), ACT.Copy).then_inc(S("down_kept"), 1)
                    act.wait_ge(S("down_kept"), e * KD + (d + 1))
                    if slots_too and d in (0, 2):
                        keep_slots(e + 1, d)

            keep_slots(0, 0)
            keep_slots(0, 2)
            gates(0)
            with act.Fori(1, NE) as e:
                ch.enter(e - 1, 8)
                keep_down(e - 1, True)
                gates(e)
                ch.leave(NE - 1)
            keep_down(NE - 1, False)
            end(act, "act")

        def dve_moe(dve, ch):
            begin(dve, "dve", 9)

            def keep_slots(e, q):
                dve.wait_ge(S("slots_turned"), e * 4 + (q + 1))
                for dst, src, k, kind in slots(q):
                    ch(dve.tensor_scalar(dst, src, A2[:, k, kind:kind + 1], modT[:, 24 + k, kind:kind + 1], ALU.mult, ALU.add))
                dve.sem_inc(S("slots_kept_dve"), 1)

            def scale_rows(e, half):
                if half == 0:
                    dve.wait_ge(S("scales_staged"), e + 1)
                dve.wait_ge(S("rows_turned"), e * 2 + (half + 1))
                o = slice(half * BLK, (half + 1) * BLK)
                ch(dve.tensor_scalar(yo[1][:, o], bank(2), vst[1], None, ALU.mult))
                ch(dve.tensor_scalar(yo[0][0:CAP_CTX, o], bank(3, BANK, CAP_CTX), vst[0][0:CAP_CTX, :], None, ALU.mult))
                dve.sem_inc(S("rows_half_scaled" if half == 0 else "rows_scaled"), 1)

            def hidden(e, rows):
                for f in range(KD):
                    dve.wait_ge(S("silu_made"), e * KD + (f + 1))
                    dve.wait_ge(S("up_done1"), e * KD + (f + 1))
                    dve.tensor_tensor(hid[:, f, :], sl[f % 2], bank(6 + f % 2, CAP), ALU.mult).then_inc(S("hidden_made"), 1)
                    dve.wait_ge(S("hidden_made"), e * KD + (f + 1))
                    if rows and f < 2:
                        scale_rows(e - 1, f)

            keep_slots(0, 1)
            keep_slots(0, 3)
            hidden(0, False)
            with dve.Fori(1, NE) as e:
                ch.enter(e - 1, 8 + 4)
                keep_slots(e, 1)
                keep_slots(e, 3)
                hidden(e, True)
                ch.leave(NE - 1)
            for half in range(2):
                scale_rows(NE - 1, half)
            end(dve, "dve")

        G2b = [work(D, at=64)] + [work(D)]
        ff = [work(D) for _ in range(3)]
        x1r = [work(D) for _ in range(3)]
        sqf = work(D)
        sf_ = st[:, 0:12]

        def sp_final(sp):
            begin(sp, "sp", 10)

            def load(t):
                if t >= 3:
                    sp.wait_ge(S(f"y_stored{t % 3}"), 16 * (t // 3))
                sp.dma_start(ff[t % 3], ffn_dram[t * P:(t + 1) * P, :]).then_inc(S(f"ffn_back{t % 3}"), 16)
                sp.dma_start(x1r[t % 3], x1_dram[t * P:(t + 1) * P, :]).then_inc(S(f"ffn_back{t % 3}"), 16)
            load(0)
            load(1)
            load(2)
            for t in range(NT):
                sp.wait_ge(S("y_made"), t + 1)
                sp.dma_start(y_rows(t), ff[t % 3]).then_inc(S(f"y_stored{t % 3}"), 16)
                if t + 3 < NT:
                    load(t + 3)
            for r in range(3):
                sp.wait_ge(S(f"y_stored{r}"), 16 * len(range(r, NT, 3)))
            sp.wait_ge(S("ctx_state_stored"), 32 * GH)
            sp.wait_ge(S("new_k_stored"), 16 * 2 * HKV * T_CTX)

        def pe_final(pe):
            begin(pe, "pe", 10)
            pe_bcast(pe, 2 * KD, 6)
            end(pe, "pe")

        def act_final(act, ch):
            begin(act, "act", 10)
            for t in range(NT):
                act.wait_ge(S(f"ffn_back{t % 3}"), 32 * (t // 3 + 1))
                if t >= 1:
                    act.wait_ge(S("x_var"), NT + t)
                act.activation(sqf, ff[t % 3], ACT.Square, accum_out=sf_[:, 0:1]).then_inc(S("x_sumsq"), 1)
                act.wait_ge(S("x_sumsq"), NT + t + 1)
            end(act, "act")

        def pool_final(pool, ch):
            begin(pool, "pool", 10)
            for t in range(NT):
                pool.wait_ge(S("x_var"), NT + t + 1)
                pool.tensor_tensor(sf_[:, 2:3], sf_[:, 1:2], mhalf[:, 0:1], ALU.pow).then_inc(S("x_rstd"), 1)
            end(pool, "pool")

        def dve_final(dve, ch):
            begin(dve, "dve", 10)
            dve_bcast(dve, ch, 2 * KD, 6, G2, G2b)
            for t in range(NT):
                j = kind_of(t)
                dve.wait_ge(S("x_sumsq"), NT + t + 1)
                dve.tensor_scalar(sf_[:, 1:2], sf_[:, 0:1], 1.0 / D, EPS, ALU.mult, ALU.add).then_inc(S("x_var"), 1)
                dve.wait_ge(S("x_rstd"), NT + t + 1)
                ch(dve.scalar_tensor_tensor(ff[t % 3], ff[t % 3], sf_[:, 2:3], G2b[j], ALU.mult, ALU.mult))
                dve.tensor_tensor(ff[t % 3], ff[t % 3], x1r[t % 3], ALU.add).then_inc(S("y_made"), 1)
                dve.wait_ge(S("y_made"), t + 1)
            end(dve, "dve")

        STAGES_SP = [sp_mod, sp_norm, sp_qkv, sp_attn, sp_ma, sp_gla, sp_mb, sp_out, sp_topk, sp_moe, sp_final]
        STAGES_PE = [pe_mod, pe_norm, pe_qkv, pe_attn, pe_ma, pe_gla, pe_mb, pe_out, pe_topk, pe_moe, pe_final]
        STAGES_ACT = [act_mod, act_norm, act_qkv, act_attn, act_ma, act_gla, act_mb, act_out, act_idle(8), act_moe, act_final]
        STAGES_DVE = [dve_mod, dve_norm, dve_qkv, dve_attn, dve_ma, dve_gla, dve_mb, dve_out, dve_topk, dve_moe, dve_final]
        STAGES_POOL = [pool_mod, pool_norm, pool_qkv, pool_attn, pool_idle(4), pool_gla, pool_idle(6), pool_out,
                       pool_idle(8), pool_moe, pool_final]

        @block.sync
        def _(sp):
            for f in STAGES_SP:
                f(sp)

        @block.tensor
        def _(pe):
            for f in STAGES_PE:
                f(pe)

        @block.scalar
        def _(act):
            ch = Chain(act, S("act_chain"))
            for f in STAGES_ACT:
                f(act, ch)

        @block.vector
        def _(dve):
            ch = Chain(dve, S("dve_chain"))
            for f in STAGES_DVE:
                f(dve, ch)

        @block.gpsimd
        def _(pool):
            ch = Chain(pool, S("pool_chain"))
            for f in STAGES_POOL:
                f(pool, ch)


_INS = ["x_prompt", "x_sample", "cache_k", "cache_v", "state_gla_fwd", "state_gla_bwd", "c", "c_ctx",
        "g_pre_mix", "g_post_mix", "g_pre_ffn", "g_post_ffn", "w_mod", "b_mod", "w_in", "g_q", "g_k",
        "w_gk2_f", "b_gk_f", "w_gk2_b", "b_gk_b", "g_gla", "w_pa", "w_pg", "w_out", "w_router", "w1", "w3", "w2"]
_OUTS = [(1, N_CTX, D), (1, N_LAT, D), (1, 1, HKV, N_CTX, HD), (1, 1, HKV, N_CTX, HD), (1, 1, GH, DK, DV), (1, 1, GH, DK, DV)]


def host_consts():
    import numpy as np
    i = np.arange(128)
    same = (i[:, None] // 64) == (i[None, :] // 64)
    upto, after = i[:, None] <= i[None, :], i[:, None] > i[None, :]
    since, before = i[:, None] >= i[None, :], i[:, None] < i[None, :]
    chunk = (i[:, None] // 64) == np.arange(2)[None, :]
    masks = np.concatenate([same & upto, same & after, same & since, same & before, chunk], axis=1).astype(np.float32)
    keep = np.concatenate([same & upto, same & since], axis=1).astype(np.int32)
    freqs = np.float32(10000.0) ** (-np.arange(32, dtype=np.float32) / np.float32(32))
    r = np.repeat(np.arange(16), 64).astype(np.float32)
    col = np.tile(np.arange(64), 16).astype(np.float32)
    ang = np.concatenate([r[:, None] * freqs, col[:, None] * freqs], axis=-1).astype(np.float32)
    rope = np.stack([np.cos(ang), np.sin(ang)]).astype(np.float32)
    return {"k_ident": np.eye(128, dtype=np.float32), "k_masks": masks, "k_keep": keep, "k_rope": rope}


def kernel(**inputs):
    import numpy as _np
    import concourse.bacc as _bacc
    from concourse import mybir as _mybir
    from concourse.bass_utils import run_bass_kernel_spmd as _run

    nc = _bacc.Bacc("TRN2", target_bir_lowering=False, num_devices=1)
    arrays, args = {}, []
    given = {name: _np.ascontiguousarray(inputs[name]) for name in _INS}
    given.update(host_consts())
    for name, a in given.items():
        arrays[f"in_{name}_dram"] = a
        args.append(nc.dram_tensor(f"in_{name}_dram", a.shape, _mybir.dt.from_np(a.dtype), kind="ExternalInput").ap())
    for i, shape in enumerate(_OUTS):
        args.append(nc.dram_tensor(f"out_{i}_dram", shape, F32, kind="ExternalOutput").ap())
    build_program(nc, *args)
    r = _run(nc, [arrays], core_ids=[0])
    return tuple(r.results[0][f"out_{i}_dram"] for i in range(len(_OUTS)))
```

```python
from contextlib import ExitStack

import concourse.bass as bass
from concourse import mybir

F32 = mybir.dt.float32
U32 = mybir.dt.uint32
I32 = mybir.dt.int32
ALU = mybir.AluOpType
ACT = mybir.ActivationFunctionType
AX = mybir.AxisListType.X
ds = bass.ds

P = 128
D = 1024
KD = D // P
N_CTX, N_LAT, N_PAST = 256, 1024, 512
T_CTX, T_LAT = N_CTX // P, N_LAT // P
NT = T_CTX + T_LAT
N_TOK = N_CTX + N_LAT
HQ, HKV, HD = 8, 2, 128
GQ = HQ // HKV
GH, DK, DV, RANK, CHUNK = 4, 128, 256, 16, 64
GATE_NORM = 16.0
NE = 16
CAP_CTX, CAP_LAT = 2 * N_CTX // NE, 2 * N_LAT // NE
CAP = CAP_CTX + CAP_LAT
EPS = 1e-6
SCALE = float(HD) ** -0.5
GSCALE = float(DK) ** -0.5
BLK = 512
BANK = 512
C_Q, C_K, C_V = 0, 1024, 1280
C_QG, C_KG, C_VG, C_RG = 1536, 2048, 2560, 3584
C_LR = 4608
C_GA, C_GB = 4640, 5664


def kind_of(t):
    return 0 if t < T_CTX else 1


class Chain:

    def __init__(self, eng, sem):
        self.eng, self.sem, self.n, self.off = eng, sem, 0, None

    def at(self, n):
        return n if self.off is None else self.off + n

    def __call__(self, ins):
        self.n += 1
        ins.then_inc(self.sem, 1)
        self.eng.wait_ge(self.sem, self.at(self.n))

    def enter(self, i, per):
        self.off, self.start, self.per = i * per, self.n, per

    def leave(self, turns):
        assert self.n - self.start == self.per, (self.n - self.start, self.per)
        self.n = self.start + turns * self.per
        self.off = None


def build_program(nc, x_prompt, x_sample, cache_k, cache_v, state_gla_fwd, state_gla_bwd, c, c_ctx,
                  g_pre_mix, g_post_mix, g_pre_ffn, g_post_ffn, w_mod, b_mod, w_in, g_q, g_k,
                  w_gk2_f, b_gk_f, w_gk2_b, b_gk_b, g_gla, w_pa, w_pg, w_out, w_router, w1, w3, w2,
                  k_ident, k_masks, k_keep, k_rope,
                  y_prompt, y_sample, new_k, new_v, new_sf, new_sb):
    ctx = ExitStack()
    with ctx:
        sems = {}

        def S(name):
            if name not in sems:
                sems[name] = ctx.enter_context(nc.semaphore(name))
            return sems[name]

        def sb(name, shape, dt=F32):
            return ctx.enter_context(nc.sbuf_tensor(name, shape, dt))

        ps = ctx.enter_context(nc.psum_tensor("ps", [P, 8 * BANK], F32))
        R1 = sb("R1", [P, NT * D])
        R2 = sb("R2", [P, NT * D])
        R3 = sb("R3", [P, NT * D])
        RW = sb("RW", [P, 2 * KD * BLK])
        WORK_N = 12416
        WK = sb("WK", [P, WORK_N])
        ident = sb("ident", [P, P])
        masks = sb("masks", [P, 4 * P + 2])
        keep = sb("keep", [P, 2 * P], I32)
        modT = sb("modT", [P, 48, 2])
        gv = sb("gv", [P, 4, KD])
        A1 = sb("A1", [P, KD, 2])
        G1 = sb("G1", [P, KD, 2])
        A2 = sb("A2", [P, KD, 2])
        G2 = sb("G2", [P, KD, 2])
        gqk = sb("gqk", [P, 2, HD])
        ggT = sb("ggT", [P, 2])
        st = sb("st", [P, 64])
        mhalf = sb("mhalf", [P, 16])
        w_lr = sb("w_lr", [P, KD, 2 * RANK])
        wr = sb("wr", [P, KD, NE])
        affT = R2[0:NE, 0:N_TOK]
        xhat_dram = nc.dram_tensor("xhat_scratch", (N_TOK, D), F32, kind="Internal").ap()
        x1_dram = nc.dram_tensor("x1_scratch", (N_TOK, D), F32, kind="Internal").ap()
        ffn_dram = nc.dram_tensor("ffn_scratch", (N_TOK, D), F32, kind="Internal").ap()

        hT = R1[:, :].rearrange("p (k t) -> p k t", k=KD)
        Wslot = [RW[:, s * KD * BLK:(s + 1) * KD * BLK].rearrange("p (k n) -> p k n", k=KD) for s in range(2)]

        def bank(b, n=BANK, parts=P):
            return ps[0:parts, b * BANK:b * BANK + n]

        used = [0]

        def work(n, at=None):
            if at is not None:
                used[0] = at
            o = used[0]
            used[0] += n
            assert used[0] <= WORK_N, used[0]
            return WK[:, o:o + n]

        xp = x_prompt.rearrange("a t d -> (a t) d")
        xs_ = x_sample.rearrange("a t d -> (a t) d")
        yp = y_prompt.rearrange("a t d -> (a t) d")
        ys = y_sample.rearrange("a t d -> (a t) d")

        def x_rows(t):
            return xp[t * P:(t + 1) * P, :] if t < T_CTX else xs_[(t - T_CTX) * P:(t - T_CTX + 1) * P, :]

        def y_rows(t):
            return yp[t * P:(t + 1) * P, :] if t < T_CTX else ys[(t - T_CTX) * P:(t - T_CTX + 1) * P, :]

        wmod, win = w_mod[0], w_in[0]
        wpa, wpg, wout = w_pa[0], w_pg[0], w_out[0]

        units = []
        mod_u = len(units)
        units += [[(wmod, u * BLK, BLK, 0)] for u in range(12)]
        kv_u = len(units)
        units += [[(win, C_K, BLK, 0)]]
        q_u = len(units)
        units += [[(win, C_Q + cb * BLK, BLK, 0)] for cb in range(2)]
        ma_u = len(units)
        for cb in range(2):
            units += [[(win, C_GA + cb * BLK, BLK, 0)], [(wpa, cb * BLK, BLK, 0)]]
        gla_u = len(units)
        for h in range(GH):
            units += [[(win, C_QG + h * DK, DK, 0), (win, C_KG + h * DK, DK, DK), (win, C_VG + h * DV, DV, 2 * DK)],
                      [(win, C_RG + h * DV, DV, 0)]]
        mb_u = len(units)
        for cb in range(2):
            units += [[(win, C_GB + cb * BLK, BLK, 0)], [(wpg, cb * BLK, BLK, 0)]]
        out_u = len(units)
        units += [[(wout, cb * BLK, BLK, 0)] for cb in range(2)]
        w_ready, uses, tot = [], [], [0, 0]
        cnt = [0, 0]
        for u, dmas in enumerate(units):
            s = u % 2
            tot[s] += 16 * len(dmas)
            w_ready.append(tot[s])
            uses.append(cnt[s])
            cnt[s] += 1
        w_full = [S("weights_landed_slot0"), S("weights_landed_slot1")]
        w_free = [S("weights_used_slot0"), S("weights_used_slot1")]

        def load_unit(sp, u):
            s = u % 2
            if uses[u] > 0:
                sp.wait_ge(w_free[s], uses[u])
            for src, c0, n, o in units[u]:
                sp.dma_start(Wslot[s][:, :, o:o + n], src[:, c0:c0 + n].rearrange("(k p) n -> p k n", p=P)) \
                    .then_inc(w_full[s], 16)

        stage_done = {e: S("stage_done_" + e) for e in ("pe", "act", "dve", "pool")}

        def begin(eng, me, k):
            for e in ("pe", "act", "dve", "pool"):
                if e != me:
                    eng.wait_ge(stage_done[e], k)

        def end(eng, me):
            eng.drain().then_inc(stage_done[me], 1)

        def gemm(pe, out, lhs, slot, width=BLK, off=0):
            for k in range(KD):
                m = pe.matmul(out, lhs(k), Wslot[slot][:, k, off:off + width], start=(k == 0), stop=(k == KD - 1))
            return m

        chains = {}

        block = ctx.enter_context(nc.Block())

        cT = work(16, at=0).rearrange("p (k j) -> p k j", j=2)
        cS = work(16).rearrange("p (k j) -> p k j", j=2)
        modrow = R3[0:2, 0:6 * D]
        brow = R2[0:2, 0:6 * D]

        def sp_consts(sp):
            n = 0
            for dst, src in (
                (cT[:, :, 0], c_ctx.rearrange("(k p) -> p k", p=P)),
                (cT[:, :, 1], c[0].rearrange("(k p) -> p k", p=P)),
                (ident[:, :], k_ident), (masks[:, :], k_masks), (keep[:, :], k_keep),
                (brow[0:1, :], b_mod[0:1, :]), (brow[1:2, :], b_mod[0:1, :]),
                (gv[:, 0, :], g_pre_mix[0].rearrange("(k p) -> p k", p=P)),
                (gv[:, 1, :], g_post_mix[0].rearrange("(k p) -> p k", p=P)),
                (gv[:, 2, :], g_pre_ffn[0].rearrange("(k p) -> p k", p=P)),
                (gv[:, 3, :], g_post_ffn[0].rearrange("(k p) -> p k", p=P)),
                (gqk[:, 0, :], g_q[0:1, :].broadcast_to([P, HD])),
                (gqk[:, 1, :], g_k[0:1, :].broadcast_to([P, HD])),
                (ggT[:, :], g_gla[0].rearrange("(k p) -> p k", p=P)),
                (w_lr[:, :, :], win[:, C_LR:C_LR + 2 * RANK].rearrange("(k p) n -> p k n", p=P)),
                (wr[:, :, :], w_router[0].rearrange("(k p) n -> p k n", p=P)),
            ):
                sp.dma_start(dst, src, allow_slow_non_contiguous=True).then_inc(S("consts_landed"), 16)
                n += 16
            return n

        N_CONST = 16 * 16

        def sp_mod(sp):
            assert sp_consts(sp) == N_CONST
            for u in range(kv_u):
                load_unit(sp, u)

        def act_mod(act, ch):
            act.wait_ge(S("consts_landed"), N_CONST)
            act.activation(cS, cT, ACT.Silu).then_inc(S("cond_ready"), 1)
            end(act, "act")

        def pe_mod(pe):
            pe.wait_ge(S("cond_ready"), 1)
            with pe.Fori(0, 6) as i:
                for s in range(2):
                    pe.wait_ge(w_full[s], i * 16 + 16)
                    pe.wait_ge(S(f"mod_row_kept{s}"), i + 1)
                    for k in range(KD):
                        m = pe.matmul(bank(s, BLK, 2), cS[:, k, :], Wslot[s][:, k, :], start=(k == 0), stop=(k == KD - 1))
                    m.then_inc(S(f"mod_row{s}"), 1)
                    pe.wait_ge(S(f"mod_row{s}"), i + 1)
                    pe.sem_inc(w_free[s], 1)
            for s in range(2):
                pe.wait_ge(S(f"mod_row_kept{s}"), 7)
            for n in range(48):
                m = pe.transpose(ps[:, 2 * BANK + 2 * n:2 * BANK + 2 * n + 2], modrow[:, n * P:(n + 1) * P], ident[0:2, 0:2])
            m.then_inc(S("mod_columns"), 1)
            end(pe, "pe")

        def dve_mod(dve, ch):
            dve.wait_ge(S("consts_landed"), N_CONST)
            for s in range(2):
                dve.sem_inc(S(f"mod_row_kept{s}"), 1)
            with dve.Fori(0, 6) as i:
                for s in range(2):
                    dve.wait_ge(S(f"mod_row{s}"), i + 1)
                    o = ds(i * (2 * BLK) + s * BLK, BLK)
                    dve.tensor_tensor(modrow[:, o], bank(s, BLK, 2), brow[:, o], ALU.add).then_inc(S(f"mod_row_kept{s}"), 1)
            dve.wait_ge(S("mod_columns"), 1)
            ch(dve.tensor_copy(modT[:, :, :], ps[:, 2 * BANK:2 * BANK + 96].rearrange("p (a b) -> p a b", b=2)))

            def g(n):
                return gv[:, n, :].unsqueeze(2).broadcast_to([P, KD, 2])
            ch(dve.scalar_tensor_tensor(A1[:, :, :], modT[:, 8:16, :], 1.0, g(0), ALU.add, ALU.mult))
            ch(dve.tensor_tensor(G1[:, :, :], modT[:, 16:24, :], g(1), ALU.mult))
            ch(dve.scalar_tensor_tensor(A2[:, :, :], modT[:, 32:40, :], 1.0, g(2), ALU.add, ALU.mult))
            ch(dve.tensor_tensor(G2[:, :, :], modT[:, 40:48, :], g(3), ALU.mult))
            end(dve, "dve")

        def pool_mod(pool, ch):
            ch(pool.memset(mhalf[:, :], -0.5))
            end(pool, "pool")

        x_t = [work(D, at=0)] + [work(D) for _ in range(2)]
        xn_t = [work(D) for _ in range(2)]
        sq_t = work(D)
        ss1, var1, rstd1 = st[:, 0:10], st[:, 10:20], st[:, 20:30]

        def pool_norm(pool, ch):
            begin(pool, "pool", 1)
            for t in range(NT):
                if t >= 3:
                    pool.wait_ge(S("x_scaled"), t - 2)
                pool.dma_start(x_t[t % 3], x_rows(t)).then_inc(S(f"x_landed{t % 3}"), 16)
                if t >= 2:
                    pool_pow(pool, t - 2)
            pool_pow(pool, NT - 2)
            pool_pow(pool, NT - 1)
            end(pool, "pool")

        def pool_pow(pool, t):
            pool.wait_ge(S("x_var"), t + 1)
            pool.tensor_tensor(rstd1[:, t:t + 1], var1[:, t:t + 1], mhalf[:, 0:1], ALU.pow).then_inc(S("x_rstd"), 1)

        def sp_norm(sp):
            load_unit(sp, kv_u)
            load_unit(sp, q_u)

        def act_norm(act, ch):
            begin(act, "act", 1)

            def square(t):
                act.wait_ge(S(f"x_landed{t % 3}"), 16 * (t // 3 + 1))
                act.activation(sq_t, x_t[t % 3], ACT.Square, accum_out=ss1[:, t:t + 1]).then_inc(S("x_sumsq"), 1)
                act.wait_ge(S("x_sumsq"), t + 1)

            square(0)
            for t in range(NT):
                if t + 1 < NT:
                    square(t + 1)
                act.wait_ge(S("x_turned"), t + 1)
                j = kind_of(t)
                for k in range(4):
                    m = act.activation(hT[:, k, t * P:(t + 1) * P], ps[:, (2 * (t % 2)) * BANK + k * P:(2 * (t % 2)) * BANK + (k + 1) * P],
                                       ACT.Identity, scale=A1[:, k, j:j + 1], bias=modT[:, k, j:j + 1])
                    if k < 3:
                        ch(m)
                m.then_inc(S("h_kept_act"), 1)
                act.wait_ge(S("h_kept_act"), t + 1)
            end(act, "act")

        def dve_norm(dve, ch):
            begin(dve, "dve", 1)

            def scale(t):
                dve.wait_ge(S("x_sumsq"), t + 1)
                dve.tensor_scalar(var1[:, t:t + 1], ss1[:, t:t + 1], 1.0 / D, EPS, ALU.mult, ALU.add).then_inc(S("x_var"), 1)
                dve.wait_ge(S("x_rstd"), t + 1)
                if t >= 2:
                    dve.wait_ge(S("x_turned"), t - 1)
                dve.tensor_scalar(xn_t[t % 2], x_t[t % 3], rstd1[:, t:t + 1], None, ALU.mult).then_inc(S("x_scaled"), 1)
                dve.wait_ge(S("x_scaled"), t + 1)

            scale(0)
            for t in range(NT):
                if t + 1 < NT:
                    scale(t + 1)
                dve.wait_ge(S("x_turned"), t + 1)
                j = kind_of(t)
                for k in range(4, 8):
                    m = dve.tensor_scalar(hT[:, k, t * P:(t + 1) * P], ps[:, (2 * (t % 2)) * BANK + k * P:(2 * (t % 2)) * BANK + (k + 1) * P],
                                          A1[:, k, j:j + 1], modT[:, k, j:j + 1], ALU.mult, ALU.add)
                    if k < 7:
                        ch(m)
                m.then_inc(S("h_kept_dve"), 1)
                dve.wait_ge(S("h_kept_dve"), t + 1)
            end(dve, "dve")

        def pe_norm(pe):
            begin(pe, "pe", 1)
            for t in range(NT):
                pe.wait_ge(S("x_scaled"), t + 1)
                if t >= 2:
                    pe.wait_ge(S("h_kept_act"), t - 1)
                    pe.wait_ge(S("h_kept_dve"), t - 1)
                for k in range(KD):
                    o = (2 * (t % 2)) * BANK + k * P
                    m = pe.transpose(ps[:, o:o + P], xn_t[t % 2][:, k * P:(k + 1) * P], ident[:, :])
                m.then_inc(S("x_turned"), 1)
            end(pe, "pe")

        vv = work(14 * 256, at=0).rearrange("p (b n) -> p b n", b=14)
        v_end = used[0]
        cos_t = work(T_LAT * 64).rearrange("p (t f) -> p t f", t=T_LAT)
        sin_t = work(T_LAT * 64).rearrange("p (t f) -> p t f", t=T_LAT)
        ck = work(HKV * 4 * HD).rearrange("p (g b d) -> p g b d", g=HKV, b=4)
        sqk = work(BLK)
        nrm = [work(BLK) for _ in range(2)]
        rot = [work(BLK) for _ in range(2)]
        rtmp = work(256)
        rtmp2 = work(256)
        ssq, varq, rsq = st[:, 32:36], st[:, 36:40], st[:, 40:44]
        NK = N_PAST + N_LAT + N_CTX
        kT = R3[:, 0:HKV * NK].rearrange("p (g l) -> p g l", g=HKV)
        assert HKV * NK + 12 * BLK <= NT * D
        K_CTX = N_PAST + N_LAT

        def key_at(t):
            return K_CTX + t * P if t < T_CTX else N_PAST + (t - T_CTX) * P

        def val_at(t):
            return 12 + t if t < T_CTX else 4 + t - T_CTX
        qkv_steps = [(kv_u, t) for t in range(NT)] + [(q_u + cb, t) for cb in range(2) for t in range(NT)]

        def sp_qkv(sp):
            sp.wait_ge(stage_done["pe"], 2)
            for e in ("dve", "act", "pool"):
                sp.wait_ge(stage_done[e], 2)
            for g in range(HKV):
                sp.dma_start(ck[:, g, :, :], cache_k[0, 0, g].rearrange("(b p) d -> p b d", p=P)).then_inc(S("cache_landed"), 16)
                sp.dma_start(vv[:, 0:4, g * HD:(g + 1) * HD], cache_v[0, 0, g].rearrange("(b p) d -> p b d", p=P)).then_inc(S("cache_landed"), 16)
            sp.dma_start(cos_t, k_rope[0].rearrange("(t p) f -> p t f", p=P)).then_inc(S("cache_landed"), 16)
            sp.dma_start(sin_t, k_rope[1].rearrange("(t p) f -> p t f", p=P)).then_inc(S("cache_landed"), 16)
            for t in range(T_CTX):
                sp.wait_ge(S("qk_turned_ready"), t + 1)
                for g in range(HKV):
                    rows = slice(t * P, (t + 1) * P)
                    sp.dma_start(new_k[0, 0, g, rows, :], nrm[t % 2][:, g * HD:(g + 1) * HD]).then_inc(S("new_k_stored"), 16)
                    sp.dma_start(new_v[0, 0, g, rows, :], vv[:, 12 + t, g * HD:(g + 1) * HD]).then_inc(S("new_k_stored"), 16)
            for u in range(q_u + 1, ma_u + 2):
                load_unit(sp, u)

        def heads_of(u):
            return HKV if u == kv_u else GQ

        def pe_qkv(pe):
            begin(pe, "pe", 2)
            pe.wait_ge(S("cache_landed"), 16 * 6)
            for g in range(HKV):
                for b in range(4):
                    m = pe.transpose(ps[:, (2 + g) * BANK + b * P:(2 + g) * BANK + (b + 1) * P], ck[:, g, b, :], ident[:, :])
            m.then_inc(S("cached_keys_turned"), 1)

            def turn(n):
                u, t = qkv_steps[n]
                pe.wait_ge(S("qk_turned_ready"), n + 1)
                if n >= 2:
                    pe.wait_ge(S("qk_turned_kept"), n - 1)
                for h in range(heads_of(u)):
                    src = rot[n % 2] if t >= T_CTX else nrm[n % 2]
                    m = pe.transpose(ps[:, (n % 2) * BANK + h * P:(n % 2) * BANK + (h + 1) * P], src[:, h * HD:(h + 1) * HD], ident[:, :])
                m.then_inc(S("qk_turned"), 1)

            for n, (u, t) in enumerate(qkv_steps):
                if t == 0:
                    pe.wait_ge(w_full[u % 2], w_ready[u])
                if n >= 4:
                    pe.wait_ge(S("qk_bank_free"), n - 3)
                m = gemm(pe, bank(4 + n % 4), lambda k: hT[:, k, t * P:(t + 1) * P], u % 2)
                m.then_inc(S("qk_projected"), 1)
                if t == NT - 1:
                    pe.wait_ge(S("qk_projected"), n + 1)
                    pe.sem_inc(w_free[u % 2], 1)
                if n >= 1:
                    turn(n - 1)
            turn(len(qkv_steps) - 1)
            end(pe, "pe")

        def act_qkv(act, ch):
            begin(act, "act", 2)
            act.wait_ge(S("cached_keys_turned"), 1)
            ch(act.activation(kT[:, 0, 0:N_PAST], bank(2), ACT.Copy))
            ch(act.activation(kT[:, 1, 0:N_PAST], bank(3), ACT.Copy))

            def keep_turned(n):
                u, t = qkv_steps[n]
                act.wait_ge(S("qk_turned"), n + 1)
                if u == kv_u:
                    m = act.activation(kT[:, :, key_at(t):key_at(t) + P], bank(n % 2, 2 * P).rearrange("p (g l) -> p g l", g=2), ACT.Copy)
                else:
                    o = (t * HQ + GQ * (u - q_u)) * P
                    m = act.activation(R2[:, o:o + GQ * P], bank(n % 2), ACT.Copy)
                m.then_inc(S("qk_turned_kept"), 1)
                act.wait_ge(S("qk_turned_kept"), n + 1)

            for n, (u, t) in enumerate(qkv_steps):
                act.wait_ge(S("qk_projected"), n + 1)
                b = 4 + n % 4
                w = heads_of(u) * HD
                if u == kv_u:
                    ch(act.activation(vv[:, val_at(t), :], ps[:, b * BANK + 256:b * BANK + 512], ACT.Copy))
                if n >= 1:
                    act.wait_ge(S("qk_bank_free"), n)
                act.activation(sqk[:, 0:w], bank(b, w), ACT.Square).then_inc(S("qk_squared"), 1)
                act.wait_ge(S("qk_squared"), n + 1)
                if n >= 1:
                    keep_turned(n - 1)
            keep_turned(len(qkv_steps) - 1)
            end(act, "act")

        def pool_qkv(pool, ch):
            begin(pool, "pool", 2)
            for n in range(len(qkv_steps)):
                pool.wait_ge(S("qk_var"), n + 1)
                pool.tensor_tensor(rsq, varq, mhalf[:, 0:4], ALU.pow).then_inc(S("qk_rstd"), 1)
            end(pool, "pool")

        def dve_qkv(dve, ch):
            begin(dve, "dve", 2)
            dve.wait_ge(S("cache_landed"), 16 * 6)
            ch(dve.memset(varq, 1.0))
            for n, (u, t) in enumerate(qkv_steps):
                H = heads_of(u)
                w = H * HD
                src = bank(4 + n % 4, w)
                dve.wait_ge(S("qk_squared"), n + 1)
                ch(dve.tensor_reduce(ssq[:, 0:H], sqk[:, 0:w].rearrange("p (h d) -> p h d", h=H), AX, ALU.add))
                if n >= 2:
                    dve.wait_ge(S("qk_turned"), n - 1)
                if n == 2:
                    dve.wait_ge(S("new_k_stored"), 16 * 2 * HKV * T_CTX)
                dve.tensor_scalar(varq[:, 0:H], ssq[:, 0:H], 1.0 / HD, EPS, ALU.mult, ALU.add).then_inc(S("qk_var"), 1)
                dve.wait_ge(S("qk_rstd"), n + 1)
                for h in range(H):
                    m = dve.scalar_tensor_tensor(nrm[n % 2][:, h * HD:(h + 1) * HD], src[:, h * HD:(h + 1) * HD], rsq[:, h:h + 1],
                                                 gqk[:, (1 if u == kv_u else 0), :], ALU.mult, ALU.mult)
                    if h < H - 1:
                        ch(m)
                m.then_inc(S("qk_bank_free"), 1)
                dve.wait_ge(S("qk_bank_free"), n + 1)
                if t >= T_CTX:
                    v = nrm[n % 2][:, 0:w].rearrange("p (h f e) -> p h f e", h=H, e=2)
                    r = rot[n % 2][:, 0:w].rearrange("p (h f e) -> p h f e", h=H, e=2)
                    t1 = rtmp[:, 0:H * 64].rearrange("p (h f) -> p h f", h=H)
                    t2 = rtmp2[:, 0:H * 64].rearrange("p (h f) -> p h f", h=H)
                    cs = cos_t[:, t - T_CTX, :].unsqueeze(1).broadcast_to([P, H, 64])
                    sn = sin_t[:, t - T_CTX, :].unsqueeze(1).broadcast_to([P, H, 64])
                    ch(dve.tensor_tensor(t1, v[:, :, :, 0], cs, ALU.mult))
                    ch(dve.tensor_tensor(t2, v[:, :, :, 1], sn, ALU.mult))
                    ch(dve.tensor_tensor(r[:, :, :, 0], t1, t2, ALU.subtract))
                    ch(dve.tensor_tensor(t1, v[:, :, :, 0], sn, ALU.mult))
                    ch(dve.tensor_tensor(t2, v[:, :, :, 1], cs, ALU.mult))
                    m = dve.tensor_tensor(r[:, :, :, 1], t1, t2, ALU.add)
                else:
                    m = dve.tensor_copy(rtmp[:, 0:1], ssq[:, 0:1])
                m.then_inc(S("qk_turned_ready"), 1)
                dve.wait_ge(S("qk_turned_ready"), n + 1)
            end(dve, "dve")

        Pb = [work(1536, at=v_end)] + [work(1536)]
        qst = [work(GQ * P) for _ in range(HKV)]
        pT = [R3[:, HKV * NK + s * 12 * 2 * P:HKV * NK + (s + 1) * 12 * 2 * P].rearrange("p (b n) -> p b n", b=12) for s in range(2)]
        mxa, nmx, sma, rsm = st[:, 44:46], st[:, 46:48], st[:, 48:50], st[:, 50:52]
        FIRST, LAST = 0, NT - 1

        def tile_plan(T):
            return (2, K_CTX, 12) if isinstance(T, int) and T < T_CTX else (12, 0, 0)

        def sset(s):
            return (s % 2) * 3 * BANK

        def over_tiles(eng, tile):
            for T in range(T_CTX + 1):
                tile(T)
            with eng.Fori(T_CTX + 1, LAST) as T:
                tile(T)
            tile(LAST)

        def ahead(T, k, by):
            if k + by < HQ:
                return T, k + by
            return None if isinstance(T, int) and T == LAST else (T + 1, k + by - HQ)

        def pool_attn(pool, ch):
            begin(pool, "pool", 3)

            def stage(T):
                for g in range(HKV):
                    if not (isinstance(T, int) and T == FIRST):
                        pool.wait_ge(S("scores_done"), T * HQ - HQ + GQ * (g + 1))
                    o = T * D + g * GQ * P
                    pool.tensor_copy(qst[g], R2[:, o:o + GQ * P] if isinstance(T, int) else R2[:, ds(o, GQ * P)]) \
                        .then_inc(S(f"queries_staged{g}"), 1)
            over_tiles(pool, stage)
            end(pool, "pool")

        def pe_attn(pe):
            begin(pe, "pe", 3)

            def scores(T, k):
                nk, k0, _ = tile_plan(T)
                g, j = k // GQ, k % GQ
                if j == 0:
                    pe.wait_ge(S(f"queries_staged{g}"), T + 1)
                if not (isinstance(T, int) and T == FIRST and k < 2):
                    pe.wait_ge(S("probsT_kept_act"), T * HQ + (k - 1))
                    pe.wait_ge(S("probsT_kept_dve"), T * HQ + (k - 1))
                for c0 in range(0, nk * P, BLK):
                    w = min(BLK, nk * P - c0)
                    m = pe.matmul(ps[:, sset(k) + c0:sset(k) + c0 + w], qst[g][:, j * P:(j + 1) * P],
                                  kT[:, g, k0 + c0:k0 + c0 + w], start=True, stop=True)
                m.then_inc(S("scores_done"), 1)

            def turn(T, k):
                nk = tile_plan(T)[0]
                pe.wait_ge(S("probs_scaled"), T * HQ + (k + 1))
                at = [0, 2 * BANK] if nk == 2 else [b * P for b in range(nk)]
                for b in range(nk):
                    m = pe.transpose(ps[:, sset(k) + at[b]:sset(k) + at[b] + P], Pb[k % 2][:, b * P:(b + 1) * P], ident[:, :])
                    if b == (0 if nk == 2 else 7):
                        m.then_inc(S("probsT_act"), 1)
                m.then_inc(S("probsT_dve"), 1)

            def weigh(T, q, part, plan):
                nk, _, v0 = plan
                g = q // 2
                if part == 0:
                    pe.wait_ge(S("probsT_kept_act"), T * HQ + (2 * q + 2))
                    pe.wait_ge(S("probsT_kept_dve"), T * HQ + (2 * q + 2))
                    if not (isinstance(T, int) and T == FIRST and q < 2):
                        pe.wait_ge(S("attn_kept"), T * GQ + (q - 1))
                for b in range(part * nk // 2, (part + 1) * nk // 2):
                    m = pe.matmul(bank(6 + q % 2, 2 * P), vv[:, v0 + b, g * HD:(g + 1) * HD], pT[q % 2][:, b, :], start=(b == 0), stop=(b == nk - 1))
                if part == 1:
                    m.then_inc(S("values_weighed"), 1)

            def tile(T):
                for k in range(HQ):
                    turn(T, k)
                    if k >= 2:
                        weigh(T, k // 2 - 1, k % 2, tile_plan(T))
                    elif not (isinstance(T, int) and T == FIRST):
                        weigh(T - 1, 3, k % 2, tile_plan(T - 1 if isinstance(T, int) else LAST))
                    nxt = ahead(T, k, 2)
                    if nxt:
                        scores(*nxt)

            scores(0, 0)
            scores(0, 1)
            over_tiles(pe, tile)
            for part in range(2):
                weigh(LAST, 3, part, tile_plan(LAST))
            end(pe, "pe")

        def dve_attn(dve, ch):
            begin(dve, "dve", 3)

            def top(T, k):
                b = k % 2
                dve.wait_ge(S("scores_done"), T * HQ + (k + 1))
                ch(dve.tensor_reduce(mxa[:, b:b + 1], ps[:, sset(k):sset(k) + tile_plan(T)[0] * P], AX, ALU.max))
                dve.tensor_scalar(nmx[:, b:b + 1], mxa[:, b:b + 1], -SCALE, None, ALU.mult).then_inc(S("max_ready"), 1)

            def norm(T, k):
                b = k % 2
                w = tile_plan(T)[0] * P
                dve.wait_ge(S("probs_ready"), T * HQ + (k + 1))
                ch(dve.reciprocal(rsm[:, b:b + 1], sma[:, b:b + 1]))
                dve.tensor_scalar(Pb[b][:, 0:w], Pb[b][:, 0:w], rsm[:, b:b + 1], None, ALU.mult).then_inc(S("probs_scaled"), 1)

            def keep_turned(T, k):
                j = k % 2
                dve.wait_ge(S("probsT_dve"), T * HQ + (k + 1))
                if j == 0 and not (isinstance(T, int) and T == FIRST and k < 4):
                    dve.wait_ge(S("values_weighed"), T * GQ + (k // 2 - 1))
                dst = pT[(k // 2) % 2]
                if tile_plan(T)[0] == 2:
                    m = dve.tensor_copy(dst[:, 1, j * P:(j + 1) * P], ps[:, sset(k) + 2 * BANK:sset(k) + 2 * BANK + P])
                else:
                    m = dve.tensor_copy(dst[:, 8:12, j * P:(j + 1) * P],
                                        ps[:, sset(k) + 2 * BANK:sset(k) + 3 * BANK].rearrange("p (b q) -> p b q", b=4))
                m.then_inc(S("probsT_kept_dve"), 1)

            def tile(T):
                inside = not isinstance(T, int)
                if inside:
                    ch.enter(T - (T_CTX + 1), 2 * HQ)
                for k in range(HQ):
                    nxt = ahead(T, k, 1)
                    if nxt:
                        top(*nxt)
                    keep_turned(T, k)
                    if nxt:
                        norm(*nxt)
                if inside:
                    ch.leave(LAST - (T_CTX + 1))

            top(0, 0)
            norm(0, 0)
            over_tiles(dve, tile)
            end(dve, "dve")

        def act_attn(act, ch):
            begin(act, "act", 3)

            def exps(T, k):
                b = k % 2
                w = tile_plan(T)[0] * P
                act.wait_ge(S("max_ready"), T * HQ + (k + 1))
                act.activation(Pb[b][:, 0:w], ps[:, sset(k):sset(k) + w], ACT.Exp, bias=nmx[:, b:b + 1],
                               scale=SCALE, accum_out=sma[:, b:b + 1]).then_inc(S("probs_ready"), 1)

            def keep_turned(T, k):
                j = k % 2
                act.wait_ge(S("probsT_act"), T * HQ + (k + 1))
                if j == 0 and not (isinstance(T, int) and T == FIRST and k < 4):
                    act.wait_ge(S("values_weighed"), T * GQ + (k // 2 - 1))
                dst = pT[(k // 2) % 2]
                if tile_plan(T)[0] == 2:
                    m = act.activation(dst[:, 0, j * P:(j + 1) * P], ps[:, sset(k):sset(k) + P], ACT.Copy)
                else:
                    m = act.activation(dst[:, 0:8, j * P:(j + 1) * P],
                                       ps[:, sset(k):sset(k) + 2 * BANK].rearrange("p (b q) -> p b q", b=8), ACT.Copy)
                m.then_inc(S("probsT_kept_act"), 1)

            def keep_out(T, q):
                act.wait_ge(S("values_weighed"), T * GQ + (q + 1))
                o = T * D + q * 2 * P
                dst = R2[:, o:o + 2 * P] if isinstance(T, int) else R2[:, ds(o, 2 * P)]
                act.activation(dst, bank(6 + q % 2, 2 * P), ACT.Copy).then_inc(S("attn_kept"), 1)

            def tile(T):
                for k in range(HQ):
                    keep_turned(T, k)
                    nxt = ahead(T, k, 1)
                    if nxt:
                        exps(*nxt)
                    if k % 2 == 1:
                        if k > 1:
                            keep_out(T, k // 2 - 1)
                        elif not (isinstance(T, int) and T == FIRST):
                            keep_out(T - 1, 3)

            exps(0, 0)
            over_tiles(act, tile)
            keep_out(LAST, 3)
            end(act, "act")

        def sp_attn(sp):
            pass

        mix = R3[:, :].rearrange("p (t n) -> p t n", t=NT)
        sig_at = WORK_N - NT * BLK
        sig = WK[:, sig_at:].rearrange("p (t n) -> p t n", t=NT)

        def merge(u0, branch, tag, k, add):
            gates, prods = f"gates_{tag}", f"merged_{tag}"

            def pe_merge(pe):
                begin(pe, "pe", k)
                for v in range(4):
                    u = u0 + v
                    pe.wait_ge(w_full[u % 2], w_ready[u])
                    for t in range(NT):
                        m = v * NT + t
                        if m >= 4:
                            pv, pt = (m - 4) // NT, (m - 4) % NT
                            pe.wait_ge(S(gates if pv % 2 == 0 else prods), (pv // 2) * NT + pt + 1)
                        if v % 2 == 0:
                            i = gemm(pe, bank(m % 4), lambda q: hT[:, q, t * P:(t + 1) * P], u % 2)
                        else:
                            i = gemm(pe, bank(m % 4), lambda q: branch(q, t), u % 2)
                        i.then_inc(S(f"tile_done_{tag}"), 1)
                    pe.wait_ge(S(f"tile_done_{tag}"), (v + 1) * NT)
                    pe.sem_inc(w_free[u % 2], 1)
                end(pe, "pe")

            def act_merge(act, ch):
                begin(act, "act", k)
                for cb in range(2):
                    for t in range(NT):
                        m = 2 * cb * NT + t
                        act.wait_ge(S(f"tile_done_{tag}"), m + 1)
                        if cb:
                            act.wait_ge(S(prods), t + 1)
                        act.activation(sig[:, t, :], bank(m % 4), ACT.Sigmoid).then_inc(S(gates), 1)
                        act.wait_ge(S(gates), cb * NT + t + 1)
                end(act, "act")

            def dve_merge(dve, ch):
                begin(dve, "dve", k)
                for cb in range(2):
                    for t in range(NT):
                        m = (2 * cb + 1) * NT + t
                        dve.wait_ge(S(gates), cb * NT + t + 1)
                        dve.wait_ge(S(f"tile_done_{tag}"), m + 1)
                        dst = mix[:, t, cb * BLK:(cb + 1) * BLK]
                        if add:
                            ch(dve.tensor_tensor(sig[:, t, :], sig[:, t, :], bank(m % 4), ALU.mult))
                            i = dve.tensor_tensor(dst, dst, sig[:, t, :], ALU.add)
                        else:
                            i = dve.tensor_tensor(dst, sig[:, t, :], bank(m % 4), ALU.mult)
                        i.then_inc(S(prods), 1)
                        dve.wait_ge(S(prods), cb * NT + t + 1)
                end(dve, "dve")
            return pe_merge, act_merge, dve_merge

        def pool_idle(k):
            def f(pool, ch):
                begin(pool, "pool", k)
                end(pool, "pool")
            return f

        pe_ma, act_ma, dve_ma = merge(ma_u, lambda h, t: R2[:, (t * HQ + h) * P:(t * HQ + h + 1) * P], "attn", 4, False)

        def sp_ma(sp):
            for u in range(ma_u + 2, ma_u + 4):
                load_unit(sp, u)
            for u in range(gla_u, gla_u + 2):
                load_unit(sp, u)

        gkT = work(N_TOK, at=0)[0:33, :]
        wg = work(2 * GH * DK)[0:33, :].rearrange("p (r n) -> p r n", r=2)
        qkv = work(NT * BLK).rearrange("p (t n) -> p t n", t=NT)
        ex = work(6 * DK).rearrange("p (a s n) -> p a s n", a=3, s=2)
        dec = [work(4).rearrange("p (d c) -> p d c", d=2) for _ in range(4)]
        qkd = [work(6 * DK).rearrange("p (a s n) -> p a s n", a=3, s=2) for _ in range(2)]
        qkT = [work(4 * P).rearrange("p (d a n) -> p d a n", d=2, a=2) for _ in range(2)]
        Sst = [[work(DV) for _ in range(3)] for _ in range(2)]
        ogT = R2[:, :].rearrange("p (k t) -> p k t", k=KD)
        spare = Wslot[(gla_u + 1) % 2][:, :, DV:2 * DV]
        lg = [spare[:, s, :].rearrange("p (d n) -> p d n", d=2) for s in range(2)]
        glt = spare[:, 2, :]
        on = [spare[:, 3 + s, :] for s in range(2)]
        am = spare[:, 5, :]
        rs = [spare[:, 6 + s, :] for s in range(2)]
        gst = st[:, 52:64]

        F_ORD = list(range(T_CTX, NT)) + list(range(T_CTX))
        B_ORD = list(range(NT - 1, T_CTX - 1, -1)) + list(range(T_CTX - 1, -1, -1))
        pairs = list(zip(F_ORD, B_ORD))
        NI = len(pairs)
        STEPS = NI + 3
        def tiles_of(i):
            lo, hi = min(pairs[i]), max(pairs[i])
            return slice(lo, hi + 1, hi - lo)

        def slot_of(i, d_):
            return int(pairs[i][d_] > pairs[i][1 - d_])
        chunks_of = ((0, 1), (1, 0))
        qkv_fill = {0: [2, 9], 1: [3, 8], 2: [4, 7], 3: [5, 6], 5: [0], 6: [1]}
        qkv_order = [t for j in sorted(qkv_fill) for t in qkv_fill[j]]
        r_fill = {8: [6, 5], 9: [7, 4], 10: [8, 3], 11: [9, 2], 12: [0, 1]}
        r_order = [t for j in sorted(r_fill) for t in r_fill[j]]
        done_by = {t: max(i for i in range(NI) if t in pairs[i]) for t in range(NT)}
        assert sorted(qkv_order) == sorted(r_order) == list(range(NT))

        def raw_out(h):
            return R2[:, ds(h * (2 * N_TOK), 2 * N_TOK)].rearrange("p (a t n) -> p t a n", a=2, t=NT)

        def sp_gla(sp):
            begin(sp, "sp", 5)
            sp.wait_ge(S("gate_weights_cleared"), 1)
            sp.dma_start(wg[0:RANK, 0, :], w_gk2_f[0]).then_inc(S("gate_weights_landed"), 16)
            sp.dma_start(wg[RANK:2 * RANK, 1, :], w_gk2_b[0]).then_inc(S("gate_weights_landed"), 16)
            sp.dma_start(wg[32:33, 0, :], b_gk_f[0:1, :]).then_inc(S("gate_weights_landed"), 16)
            sp.dma_start(wg[32:33, 1, :], b_gk_b[0:1, :]).then_inc(S("gate_weights_landed"), 16)
            for h in range(GH):
                if h:
                    sp.wait_ge(S("head_done"), h)
                    sp.wait_ge(S("ctx_state_stored"), 32 * h)
                for d_, src in ((0, state_gla_fwd), (1, state_gla_bwd)):
                    sp.dma_start(Sst[d_][0], src[0, 0, h]).then_inc(S("state_landed"), 16)
                if h + 1 < GH:
                    for u in (gla_u + 2 * h + 2, gla_u + 2 * h + 3):
                        load_unit(sp, u)
                else:
                    for u in (mb_u, mb_u + 1):
                        if u % 2 == (gla_u + 1) % 2:
                            sp.wait_ge(S("head_done"), GH)
                        load_unit(sp, u)
                sp.wait_ge(S("ctx_state_final"), h + 1)
                for d_, dst in ((0, new_sf), (1, new_sb)):
                    sp.dma_start(dst[0, 0, h], Sst[d_][(2 * NI) % 3]).then_inc(S("ctx_state_stored"), 16)

        def pe_gla(pe):
            begin(pe, "pe", 5)
            for n, (c0, w) in enumerate(((0, 512), (512, 512), (1024, 256))):
                for k in range(KD):
                    m = pe.matmul(ps[0:32, n * BANK:n * BANK + w], w_lr[:, k, :], hT[:, k, c0:c0 + w], start=(k == 0), stop=(k == KD - 1))
                m.then_inc(S("low_rank_done"), 1)
            pe.wait_ge(S("low_rank_kept"), 3)
            pe.wait_ge(S("gate_weights_landed"), 64)
            with pe.Fori(0, GH) as h:

                def gate(i):
                    if i >= 1:
                        pe.wait_ge(S("log_gates"), h * NI + i)
                    pe.sem_inc(S("gate_turns"), 1)
                    for d_ in range(2):
                        t = pairs[i][d_]
                        m = pe.matmul(ps[:, d_ * DK:(d_ + 1) * DK], gkT[0:33, t * P:(t + 1) * P], wg[0:33, d_, ds(h * DK, DK)], start=True, stop=True)
                    m.then_inc(S("gate_logits"), 1)

                def sums(i):
                    pe.wait_ge(S("log_gates"), h * NI + (i + 1))
                    if i >= 1:
                        pe.wait_ge(S("exps_done"), h * NI + i)
                    for a in range(2):
                        for d_ in range(2):
                            o = BANK + (2 * a + slot_of(i, d_)) * DK
                            m = pe.matmul(ps[:, o:o + DK], masks[:, (2 * d_ + a) * P:(2 * d_ + a + 1) * P], lg[i % 2][:, d_, :], start=True, stop=True)
                    m.then_inc(S("gate_sums"), 1)

                def totals(i):
                    if i >= 3:
                        pe.wait_ge(S("intra_masked"), h * NI + (i - 2))
                    for d_ in range(2):
                        o = 3 * BANK + (2 + d_) * P
                        m = pe.matmul(ps[:, o:o + P], lg[i % 2][:, d_, :], masks[:, 3 * P + 2:4 * P + 2], start=True, stop=True)
                    m.then_inc(S("gate_totals"), 1)

                def intra(i):
                    pe.wait_ge(S("gated_turned_kept"), h * NI + (i + 1))
                    pe.wait_ge(S("exps_done"), h * NI + min(i + 2, NI))
                    if i >= 1:
                        pe.wait_ge(S("intra_masked"), h * NI + i)
                    for d_ in range(2):
                        o = 3 * BANK + d_ * P
                        m = pe.matmul(ps[:, o:o + P], qkT[i % 2][:, d_, 1, :], qkT[i % 2][:, d_, 0, :], start=True, stop=True)
                    m.then_inc(S("intra_done"), 1)

                def turn(i):
                    pe.wait_ge(S("qk_gated"), h * NI + (i + 1))
                    if i >= 1:
                        pe.wait_ge(S("gated_turned_kept"), h * NI + i)
                    for d_ in range(2):
                        for a in range(2):
                            o = 2 * BANK + (2 * d_ + a) * P
                            m = pe.transpose(ps[:, o:o + P], qkd[i % 2][:, a, slot_of(i, d_), :], ident[:, :])
                    m.then_inc(S("gated_turned"), 1)

                def out(i):
                    if i == 0:
                        pe.wait_ge(S("state_landed"), h * 32 + 32)
                    pe.wait_ge(S("intra_masked"), h * NI + (i + 1))
                    if i >= 1:
                        pe.wait_ge(S("out_kept"), h * NI + i)
                    pe.wait_ge(S("state_moved"), h * (2 * NI) + (2 * i + 1))
                    for d_ in range(2):
                        t = pairs[i][d_]
                        o = 6 * BANK + slot_of(i, d_) * DV
                        pe.matmul(ps[:, o:o + DV], am[:, d_ * P:(d_ + 1) * P], qkv[:, t, 2 * DK:2 * DK + DV], start=True, stop=False, skip_group_check=True)
                        for x in range(2):
                            rows = slice(chunks_of[d_][x] * CHUNK, (chunks_of[d_][x] + 1) * CHUNK)
                            m = pe.matmul(ps[rows, o:o + DV], qkT[i % 2][:, d_, 0, rows], Sst[d_][(2 * i + x) % 3], start=False, stop=(x == 1),
                                          skip_group_check=True)
                    m.then_inc(S("tile_out"), 1)

                def chunk_kv(i):
                    if i >= 1:
                        pe.wait_ge(S("state_moved"), h * (2 * NI) + 2 * i)
                    for x in range(2):
                        for d_ in range(2):
                            t, c_ = pairs[i][d_], chunks_of[d_][x]
                            rows = slice(c_ * CHUNK, (c_ + 1) * CHUNK)
                            o = (4 + c_) * BANK + d_ * DV
                            m = pe.matmul(ps[:, o:o + DV], qkd[i % 2][rows, 2, slot_of(i, d_), :], qkv[rows, t, 2 * DK:2 * DK + DV], start=True, stop=True)
                            if x == 1:
                                m.then_inc(S(f"chunk_kv{c_}"), 1)

                def turn_out(m_):
                    pe.wait_ge(S("gated_out"), h * NT + (m_ + 1))
                    if m_ >= 1:
                        pe.wait_ge(S("gated_out_kept"), h * NT + m_)
                    for a in range(2):
                        o = 7 * BANK + (2 + a) * P
                        m = pe.transpose(ps[:, o:o + P], on[m_ % 2][:, a * P:(a + 1) * P], ident[:, :])
                    m.then_inc(S("gated_out_turned"), 1)

                def project(j, gap):
                    if gap < len(qkv_fill.get(j, [])):
                        t = qkv_fill[j][gap]
                        n = qkv_order.index(t)
                        if n == 0:
                            pe.wait_ge(w_full[gla_u % 2], h * 48 + w_ready[gla_u])
                        else:
                            pe.wait_ge(S("qkv_kept"), h * NT + n)
                        gemm(pe, bank(7), lambda q: hT[:, q, t * P:(t + 1) * P], gla_u % 2).then_inc(S("qkv_done"), 1)
                        if n == NT - 1:
                            pe.wait_ge(S("qkv_done"), h * NT + NT)
                            pe.sem_inc(w_free[gla_u % 2], 1)
                    if gap < len(r_fill.get(j, [])):
                        t = r_fill[j][gap]
                        n = r_order.index(t)
                        if n == 0:
                            pe.wait_ge(w_full[(gla_u + 1) % 2], h * 16 + w_ready[gla_u + 1])
                            pe.wait_ge(S("qkv_kept"), h * NT + NT)
                        else:
                            pe.wait_ge(S("r_used"), h * NT + n)
                            turn_out(n - 1)
                        gemm(pe, bank(7, DV), lambda q: hT[:, q, t * P:(t + 1) * P], (gla_u + 1) % 2, DV).then_inc(S("r_done"), 1)
                        if n == NT - 1:
                            pe.wait_ge(S("r_done"), h * NT + NT)
                            pe.sem_inc(w_free[(gla_u + 1) % 2], 1)

                for j in range(STEPS):
                    if j < NI:
                        gate(j)
                    if 0 <= j - 1 < NI:
                        sums(j - 1)
                        totals(j - 1)
                    if 0 <= j - 3 < NI:
                        intra(j - 3)
                    project(j, 0)
                    if 0 <= j - 2 < NI:
                        turn(j - 2)
                    if 0 <= j - 3 < NI:
                        out(j - 3)
                    project(j, 1)
                    if 0 <= j - 2 < NI:
                        chunk_kv(j - 2)
                turn_out(NT - 1)
                pe.wait_ge(S("gated_out_kept"), h * NT + NT)
            end(pe, "pe")

        def act_gla(act, ch):
            begin(act, "act", 5)
            for n, (c0, w) in enumerate(((0, 512), (512, 512), (1024, 256))):
                act.wait_ge(S("low_rank_done"), n + 1)
                act.activation(gkT[0:32, c0:c0 + w], ps[0:32, n * BANK:n * BANK + w], ACT.Copy).then_inc(S("low_rank_kept"), 1)
            with act.Fori(0, GH) as h:
                ch.enter(h, ACT_PER)

                def logs(i):
                    act.wait_ge(S("gate_logits"), h * NI + (i + 1))
                    if i >= 1:
                        act.wait_ge(S("log_gates"), h * NI + i)
                    ch(act.activation(glt, bank(0, 2 * DK), ACT.Abs))
                    ch(act.activation(glt, glt, ACT.Exp, scale=-1.0))
                    act.activation(glt, glt, ACT.Ln, bias=1.0).then_inc(S("softplus_done"), 1)
                    act.wait_ge(S("softplus_done"), h * NI + (i + 1))

                def exps(i):
                    act.wait_ge(S("gate_sums"), h * NI + (i + 1))
                    if i >= 1:
                        act.wait_ge(S("qk_gated"), h * NI + i)
                    if i >= 4:
                        act.wait_ge(S("state_moved"), h * (2 * NI) + 2 * (i - 3))
                    ch(act.activation(ex[:, 0:3:2, :, :], bank(1).rearrange("p (a s n) -> p a s n", a=2, s=2), ACT.Exp, scale=1.0 / GATE_NORM))
                    ch(act.activation(ex[:, 1, :, :], bank(1, 2 * DK).rearrange("p (s n) -> p s n", s=2), ACT.Exp, scale=-1.0 / GATE_NORM))
                    act.wait_ge(S("gate_totals"), h * NI + (i + 1))
                    if i >= 2:
                        act.wait_ge(S("intra_masked"), h * NI + (i - 1))
                    src = ps[:, 3 * BANK + 2 * P:4 * BANK].rearrange("p (d n) -> p d n", d=2)[:, :, P - 2:P]
                    act.activation(dec[i % 4], src, ACT.Exp, scale=1.0 / GATE_NORM).then_inc(S("exps_done"), 1)
                    act.wait_ge(S("exps_done"), h * NI + (i + 1))

                def keep_turned(i):
                    act.wait_ge(S("gated_turned"), h * NI + (i + 1))
                    if i >= 2:
                        act.wait_ge(S("tile_out"), h * NI + (i - 1))
                    act.activation(qkT[i % 2], bank(2).rearrange("p (d a n) -> p d a n", d=2, a=2), ACT.Copy).then_inc(S("gated_turned_kept"), 1)
                    act.wait_ge(S("gated_turned_kept"), h * NI + (i + 1))

                def projected(j, gap):
                    if gap < len(qkv_fill.get(j, [])):
                        t = qkv_fill[j][gap]
                        n = qkv_order.index(t)
                        act.wait_ge(S("qkv_done"), h * NT + (n + 1))
                        ch(act.activation(qkv[:, t, 0:DK], bank(7, DK), ACT.Copy, scale=GSCALE))
                        act.activation(qkv[:, t, DK:BLK], ps[:, 7 * BANK + DK:8 * BANK], ACT.Copy).then_inc(S("qkv_kept"), 1)
                    if gap < len(r_fill.get(j, [])):
                        t = r_fill[j][gap]
                        n = r_order.index(t)
                        act.wait_ge(S("r_done"), h * NT + (n + 1))
                        if n >= 2:
                            act.wait_ge(S("gated_out"), h * NT + (n - 1))
                        act.activation(rs[n % 2], bank(7, DV), ACT.Silu).then_inc(S("r_used"), 1)
                        act.wait_ge(S("out_kept"), h * NI + (done_by[t] + 1))
                        if n >= 2:
                            act.wait_ge(S("gated_out_turned"), h * NT + (n - 1))
                        act.activation(on[n % 2].rearrange("p (a n) -> p a n", a=2), raw_out(h)[:, t, :, :], ACT.Square,
                                       accum_out=gst[:, n % 2:n % 2 + 1]).then_inc(S("out_squared"), 1)
                        act.wait_ge(S("out_squared"), h * NT + (n + 1))

                for j in range(STEPS):
                    if j < NI:
                        logs(j)
                    if 0 <= j - 1 < NI:
                        exps(j - 1)
                    projected(j, 0)
                    if 0 <= j - 2 < NI:
                        keep_turned(j - 2)
                    projected(j, 1)
                act.wait_ge(S("gated_out_kept"), h * NT + NT)
                ch.leave(GH)
            end(act, "act")

        ACT_PER = 4 * NI + NT

        def pool_gla(pool, ch):
            begin(pool, "pool", 5)
            ch(pool.memset(gkT[32:33, :], 1.0))
            pool.memset(wg[:, :, :], 0.0).then_inc(S("gate_weights_cleared"), 1)
            with pool.Fori(0, GH) as h:
                ch.enter(h, NT)
                for n in range(NT):
                    pool.wait_ge(S("out_squared"), h * NT + (n + 1))
                    c = n % 2
                    if n >= 2:
                        pool.wait_ge(S("gated_out"), h * NT + (n - 1))
                    pool.sem_inc(S("rstd_turns"), 1)
                    ch(pool.tensor_scalar(gst[:, 2 + c:3 + c], gst[:, c:c + 1], 1.0 / DV, EPS, ALU.mult, ALU.add))
                    pool.tensor_tensor(gst[:, 4 + c:5 + c], gst[:, 2 + c:3 + c], mhalf[:, 0:1], ALU.pow).then_inc(S("out_rstd"), 1)
                ch.leave(GH)
            pool.wait_ge(S("ctx_state_stored"), 32 * GH)
            end(pool, "pool")

        def dve_gla(dve, ch):
            begin(dve, "dve", 5)
            ch(dve.memset(am, 0.0))
            with dve.Fori(0, GH) as h:
                ch.enter(h, DVE_PER)

                def loggate(i):
                    dve.wait_ge(S("softplus_done"), h * NI + (i + 1))
                    if i >= 2:
                        dve.wait_ge(S("gate_totals"), h * NI + (i - 1))
                    dve.scalar_tensor_tensor(lg[i % 2], bank(0, 2 * DK).rearrange("p (d n) -> p d n", d=2), 0.0,
                                             glt.rearrange("p (d n) -> p d n", d=2), ALU.min, ALU.subtract).then_inc(S("log_gates"), 1)

                def gated(i):
                    dve.wait_ge(S("exps_done"), h * NI + (i + 1))
                    last = max(qkv_order.index(t) for t in pairs[i])
                    dve.wait_ge(S("qkv_kept"), h * NT + (last + 1))
                    if i >= 2:
                        dve.wait_ge(S("chunk_kv0"), h * NI + (i - 1))
                        dve.wait_ge(S("chunk_kv1"), h * NI + (i - 1))
                    src = qkv[:, tiles_of(i), :]
                    o = qkd[i % 2]
                    ch(dve.tensor_tensor(o[:, 0:2, :, :].rearrange("p a s n -> p s a n"), src[:, :, 0:2 * DK].rearrange("p s (a n) -> p s a n", a=2),
                                         ex[:, 0:2, :, :].rearrange("p a s n -> p s a n"), ALU.mult))
                    dve.tensor_tensor(o[:, 2, :, :], src[:, :, DK:2 * DK], ex[:, 2, :, :], ALU.mult).then_inc(S("qk_gated"), 1)

                def masked(i):
                    dve.wait_ge(S("intra_done"), h * NI + (i + 1))
                    if i >= 1:
                        dve.wait_ge(S("tile_out"), h * NI + i)
                    dve.sem_inc(S("mask_turns"), 1)
                    dve.copy_predicated(am, keep[:, :], bank(3, 2 * P)).then_inc(S("intra_masked"), 1)

                def states(i):
                    if i == 0:
                        dve.wait_ge(S("state_landed"), h * 32 + 32)
                    else:
                        dve.wait_ge(S("tile_out"), h * NI + i)
                    dve.wait_ge(S("chunk_kv0"), h * NI + (i + 1))
                    dve.wait_ge(S("chunk_kv1"), h * NI + (i + 1))
                    for x in range(2):
                        if i + x >= 1:
                            dve.wait_ge(S("state_moved"), h * (2 * NI) + (2 * i + x))
                        for d_ in range(2):
                            s_, c_ = 2 * i + x, chunks_of[d_][x]
                            if i == T_LAT - 1 and x == 1:
                                m = dve.memset(Sst[d_][(s_ + 1) % 3], 0.0)
                            else:
                                m = dve.scalar_tensor_tensor(Sst[d_][(s_ + 1) % 3], Sst[d_][s_ % 3], dec[i % 4][:, d_, c_:c_ + 1],
                                                             ps[:, (4 + c_) * BANK + d_ * DV:(4 + c_) * BANK + (d_ + 1) * DV], ALU.mult, ALU.add)
                            if d_ == 0:
                                ch(m)
                        m.then_inc(S("state_moved"), 1)
                    if i == NI - 1:
                        dve.wait_ge(S("state_moved"), h * (2 * NI) + 2 * NI)
                        dve.sem_inc(S("ctx_state_final"), 1)

                def keep_out(i):
                    dve.wait_ge(S("tile_out"), h * NI + (i + 1))
                    dst = raw_out(h)[:, tiles_of(i), :, :]
                    src = bank(6).rearrange("p (s a n) -> p s a n", s=2, a=2)
                    if done_by[pairs[i][0]] == i:
                        dve.wait_ge(S("out_kept"), h * NI + i)
                        m = dve.tensor_tensor(dst, dst, src, ALU.add)
                    else:
                        m = dve.tensor_copy(dst, src)
                    m.then_inc(S("out_kept"), 1)

                def finish(n):
                    t = r_order[n]
                    dve.wait_ge(S("out_rstd"), h * NT + (n + 1))
                    c = n % 2
                    dve.scalar_tensor_tensor(on[c].rearrange("p (a n) -> p a n", a=2), raw_out(h)[:, t, :, :], gst[:, 4 + c:5 + c],
                                             rs[c].rearrange("p (a n) -> p a n", a=2), ALU.mult, ALU.mult).then_inc(S("gated_out"), 1)

                def keep_finished(n):
                    t = r_order[n]
                    dve.wait_ge(S("gated_out_turned"), h * NT + (n + 1))
                    if n + 1 < NT:
                        dve.wait_ge(S("r_used"), h * NT + (n + 2))
                    for a in range(2):
                        o = h * (2 * N_TOK) + (a * N_TOK + t * P)
                        m = dve.tensor_scalar(R2[:, ds(o, P)], ps[:, 7 * BANK + (2 + a) * P:7 * BANK + (3 + a) * P], ggT[:, a:a + 1], None, ALU.mult)
                        if a == 0:
                            ch(m)
                    m.then_inc(S("gated_out_kept"), 1)

                for j in range(STEPS):
                    fin = [r_order.index(t) for t in r_fill.get(j, [])]
                    if 0 <= j - 3 < NI:
                        masked(j - 3)
                    if j < NI:
                        loggate(j)
                    if 0 <= j - 1 < NI:
                        gated(j - 1)
                    if fin and fin[0] >= 1:
                        keep_finished(fin[0] - 1)
                    if fin and j < STEPS - 1:
                        finish(fin[0])
                    if 0 <= j - 3 < NI:
                        keep_out(j - 3)
                    if fin and j == STEPS - 1:
                        finish(fin[0])
                    if fin:
                        keep_finished(fin[1] - 1)
                    if 0 <= j - 2 < NI:
                        states(j - 2)
                    if fin:
                        finish(fin[1])
                keep_finished(NT - 1)
                dve.wait_ge(S("gated_out_kept"), h * NT + NT)
                ch.leave(GH)
                dve.sem_inc(S("head_done"), 1)
            end(dve, "dve")

        DVE_PER = NI + 2 * NI + NT

        pe_mb, act_mb, dve_mb = merge(mb_u, lambda q, t: ogT[:, q, t * P:(t + 1) * P], "gla", 6, True)

        def sp_mb(sp):
            for u in (mb_u + 2, mb_u + 3, out_u, out_u + 1):
                load_unit(sp, u)

        mixT = R1[:, :].rearrange("p (k t) -> p k t", k=KD)
        G1b = [work(D, at=0)] + [work(D)]
        xr = [work(D) for _ in range(2)]
        x1b = [work(D) for _ in range(2)]
        xh = [work(D) for _ in range(2)]
        sqo = work(D)
        h2T = [work(D).rearrange("p (k t) -> p k t", k=KD) for _ in range(2)]
        colb = R2[:, N_TOK:N_TOK + 2 * P].rearrange("p (a n) -> p a n", a=2)
        aff = R2[:, N_TOK + 2 * P:N_TOK + 2 * P + 2 * NE].rearrange("p (a n) -> p a n", a=2)
        ones = R2[:, N_TOK + 4 * P:N_TOK + 5 * P]
        so = st[:, 0:24]

        def bcast_cols(n):
            return n // KD, n % KD

        def pe_bcast(pe, n0, nb):
            for n in range(2 * KD):
                pe.wait_ge(S("columns_spread"), n0 + n + 1)
                if n >= 2:
                    pe.wait_ge(S("rows_kept"), n0 + n - 1)
                pe.matmul(bank(nb + n % 2, P), colb[:, n % 2, :], ident[:, :], start=True, stop=True).then_inc(S("rows_spread"), 1)

        def dve_bcast(dve, ch, n0, nb, G, dst):
            ch(dve.memset(ones, 1.0))

            def spread(n):
                j, k = bcast_cols(n)
                if n >= 2:
                    dve.wait_ge(S("rows_spread"), n0 + n - 1)
                dve.tensor_scalar(colb[:, n % 2, :], ones, G[:, k, j:j + 1], None, ALU.mult).then_inc(S("columns_spread"), 1)
            spread(0)
            for n in range(2 * KD):
                if n + 1 < 2 * KD:
                    spread(n + 1)
                j, k = bcast_cols(n)
                dve.wait_ge(S("rows_spread"), n0 + n + 1)
                dve.tensor_copy(dst[j][:, k * P:(k + 1) * P], bank(nb + n % 2, P)).then_inc(S("rows_kept"), 1)
                dve.wait_ge(S("rows_kept"), n0 + n + 1)

        def sp_out(sp):
            begin(sp, "sp", 7)
            for t in range(NT):
                if t >= 2:
                    sp.wait_ge(S("x1_made"), t - 1)
                sp.dma_start(xr[t % 2], x_rows(t)).then_inc(S(f"x_again{t % 2}"), 16)
                if t >= 1:
                    store_out(sp, t - 1)
            store_out(sp, NT - 1)

        def store_out(sp, t):
            sp.wait_ge(S("xhat_made"), t + 1)
            sp.dma_start(x1_dram[t * P:(t + 1) * P, :], x1b[t % 2]).then_inc(S(f"x1_stored{t % 2}"), 16)
            sp.dma_start(xhat_dram[t * P:(t + 1) * P, :], xh[t % 2]).then_inc(S(f"x1_stored{t % 2}"), 16)

        def pe_out(pe):
            begin(pe, "pe", 7)
            for t in range(NT):
                if t >= 2:
                    pe.wait_ge(S("mixT_act"), t - 1)
                    pe.wait_ge(S("mixT_dve"), t - 1)
                for k in range(KD):
                    o = (2 * (t % 2)) * BANK + k * P
                    m = pe.transpose(ps[:, o:o + P], mix[:, t, k * P:(k + 1) * P], ident[:, :])
                m.then_inc(S("mix_turned"), 1)
            pe_bcast(pe, 0, 6)
            for s in range(2):
                pe.wait_ge(w_full[(out_u + s) % 2], w_ready[out_u + s])
            pe.wait_ge(S("mixT_act"), NT)
            pe.wait_ge(S("mixT_dve"), NT)

            def project(t, cb):
                b = 2 * (t % 2) + cb
                if t >= 2 and cb == 0:
                    pe.wait_ge(S("out_banks_free"), t - 1)
                gemm(pe, bank(b), lambda q: mixT[:, q, t * P:(t + 1) * P], (out_u + cb) % 2).then_inc(S("out_done"), 1)

            def turn(t):
                pe.wait_ge(S("xhat_made"), t + 1)
                if t >= 1:
                    pe.wait_ge(S("h2_kept_act"), t)
                    pe.wait_ge(S("h2_kept_dve"), t)
                for k in range(KD):
                    m = pe.transpose(ps[:, 4 * BANK + k * P:4 * BANK + (k + 1) * P], xh[t % 2][:, k * P:(k + 1) * P], ident[:, :])
                m.then_inc(S("xhat_turned"), 1)

            def route(t):
                pe.wait_ge(S("h2_kept_act"), t + 1)
                pe.wait_ge(S("h2_kept_dve"), t + 1)
                if t >= 1:
                    pe.wait_ge(S("aff_made"), t)
                for k in range(KD):
                    m = pe.matmul(bank(6, NE), h2T[t % 2][:, k, :], wr[:, k, :], start=(k == 0), stop=(k == KD - 1))
                m.then_inc(S("routed"), 1)

            def turn_aff(t):
                pe.wait_ge(S("aff_made"), t + 1)
                if t >= 1:
                    pe.wait_ge(S("aff_kept"), t)
                pe.transpose(ps[0:NE, 7 * BANK:7 * BANK + P], aff[:, t % 2, :], ident[:, :]).then_inc(S("aff_turned"), 1)

            for t in range(NT + 2):
                if t < NT:
                    project(t, 0)
                if 0 <= t - 1 < NT:
                    turn(t - 1)
                if t < NT:
                    project(t, 1)
                if 0 <= t - 1 < NT:
                    route(t - 1)
                if 0 <= t - 2 < NT:
                    turn_aff(t - 2)
            end(pe, "pe")

        def act_out(act, ch):
            begin(act, "act", 7)
            for t in range(NT):
                act.wait_ge(S("mix_turned"), t + 1)
                b = 2 * (t % 2)
                act.activation(mixT[:, 0:4, t * P:(t + 1) * P], bank(b).rearrange("p (k t) -> p k t", k=4), ACT.Copy).then_inc(S("mixT_act"), 1)
                act.wait_ge(S("mixT_act"), t + 1)

            def square_mix(t):
                act.wait_ge(S("out_done"), 2 * t + 2)
                for cb in range(2):
                    ch(act.activation(sqo[:, cb * BLK:(cb + 1) * BLK], bank(2 * (t % 2) + cb), ACT.Square, accum_out=so[:, cb:cb + 1]))
                act.sem_inc(S("mix_squared"), 1)

            def square_x1(t):
                act.wait_ge(S("x1_made"), t + 1)
                act.activation(sqo[:, :], x1b[t % 2], ACT.Square, accum_out=so[:, 2:3]).then_inc(S("x1_squared"), 1)
                act.wait_ge(S("x1_squared"), t + 1)

            def keep_h2(t):
                j = kind_of(t)
                act.wait_ge(S("xhat_turned"), t + 1)
                if t >= 2:
                    act.wait_ge(S("routed"), t - 1)
                for k in range(4):
                    ch(act.activation(h2T[t % 2][:, k, :], ps[:, 4 * BANK + k * P:4 * BANK + (k + 1) * P], ACT.Identity,
                                      scale=A2[:, k, j:j + 1], bias=modT[:, 24 + k, j:j + 1]))
                act.sem_inc(S("h2_kept_act"), 1)

            def soft(t):
                act.wait_ge(S("router_max"), t + 1)
                act.activation(aff[:, t % 2, :], bank(6, NE), ACT.Exp, bias=so[:, 8:9], accum_out=so[:, 9:10]).then_inc(S("router_exp"), 1)
                act.wait_ge(S("router_exp"), t + 1)

            def keep_aff(t):
                act.wait_ge(S("aff_turned"), t + 1)
                act.activation(affT[:, t * P:(t + 1) * P], ps[0:NE, 7 * BANK:7 * BANK + P], ACT.Copy).then_inc(S("aff_kept"), 1)
                act.wait_ge(S("aff_kept"), t + 1)

            for t in range(NT + 2):
                if t < NT:
                    square_mix(t)
                if 0 <= t - 1 < NT:
                    keep_h2(t - 1)
                if t < NT:
                    square_x1(t)
                if 0 <= t - 1 < NT:
                    soft(t - 1)
                if 0 <= t - 2 < NT:
                    keep_aff(t - 2)
            end(act, "act")

        def pool_out(pool, ch):
            begin(pool, "pool", 7)
            for n in range(2 * NT):
                pool.wait_ge(S("out_vars"), n + 1)
                o = 4 + n % 2
                pool.tensor_tensor(so[:, o + 2:o + 3], so[:, o:o + 1], mhalf[:, 0:1], ALU.pow).then_inc(S("out_rstds"), 1)
            for t in range(2):
                pool.wait_ge(S(f"x1_stored{t}"), 32 * (NT // 2))
            end(pool, "pool")

        def dve_out(dve, ch):
            begin(dve, "dve", 7)
            for t in range(NT):
                dve.wait_ge(S("mix_turned"), t + 1)
                b = 2 * (t % 2) + 1
                dve.tensor_copy(mixT[:, 4:8, t * P:(t + 1) * P], bank(b).rearrange("p (k t) -> p k t", k=4)).then_inc(S("mixT_dve"), 1)
                dve.wait_ge(S("mixT_dve"), t + 1)
            dve_bcast(dve, ch, 0, 6, G1, G1b)

            def residual(t):
                j = kind_of(t)
                dve.wait_ge(S("mix_squared"), t + 1)
                ch(dve.tensor_tensor(so[:, 3:4], so[:, 0:1], so[:, 1:2], ALU.add))
                ch(dve.tensor_scalar(so[:, 4:5], so[:, 3:4], 1.0 / D, EPS, ALU.mult, ALU.add))
                dve.sem_inc(S("out_vars"), 1)
                dve.wait_ge(S("out_rstds"), 2 * t + 1)
                if t >= 2:
                    dve.wait_ge(S(f"x1_stored{t % 2}"), 32 * (t // 2))
                for cb in range(2):
                    ch(dve.scalar_tensor_tensor(x1b[t % 2][:, cb * BLK:(cb + 1) * BLK], bank(2 * (t % 2) + cb), so[:, 6:7],
                                                G1b[j][:, cb * BLK:(cb + 1) * BLK], ALU.mult, ALU.mult))
                dve.sem_inc(S("out_banks_free"), 1)
                dve.wait_ge(S(f"x_again{t % 2}"), 16 * (t // 2 + 1))
                dve.tensor_tensor(x1b[t % 2], x1b[t % 2], xr[t % 2], ALU.add).then_inc(S("x1_made"), 1)
                dve.wait_ge(S("x1_made"), t + 1)

            def normal(t):
                dve.wait_ge(S("x1_squared"), t + 1)
                ch(dve.tensor_scalar(so[:, 5:6], so[:, 2:3], 1.0 / D, EPS, ALU.mult, ALU.add))
                dve.sem_inc(S("out_vars"), 1)
                dve.wait_ge(S("out_rstds"), 2 * t + 2)
                if t >= 2:
                    dve.wait_ge(S("xhat_turned"), t - 1)
                dve.tensor_scalar(xh[t % 2], x1b[t % 2], so[:, 7:8], None, ALU.mult).then_inc(S("xhat_made"), 1)
                dve.wait_ge(S("xhat_made"), t + 1)

            def keep_h2(t):
                j = kind_of(t)
                dve.wait_ge(S("xhat_turned"), t + 1)
                if t >= 2:
                    dve.wait_ge(S("routed"), t - 1)
                for k in range(4, 8):
                    ch(dve.tensor_scalar(h2T[t % 2][:, k, :], ps[:, 4 * BANK + k * P:4 * BANK + (k + 1) * P],
                                         A2[:, k, j:j + 1], modT[:, 24 + k, j:j + 1], ALU.mult, ALU.add))
                dve.sem_inc(S("h2_kept_dve"), 1)

            def soft(t):
                dve.wait_ge(S("routed"), t + 1)
                ch(dve.tensor_reduce(so[:, 10:11], bank(6, NE), AX, ALU.max))
                if t >= 2:
                    dve.wait_ge(S("aff_turned"), t - 1)
                dve.tensor_scalar(so[:, 8:9], so[:, 10:11], -1.0, None, ALU.mult).then_inc(S("router_max"), 1)
                dve.wait_ge(S("router_exp"), t + 1)
                ch(dve.reciprocal(so[:, 11:12], so[:, 9:10]))
                ch(dve.tensor_scalar(aff[:, t % 2, :], aff[:, t % 2, :], so[:, 11:12], None, ALU.mult))
                dve.sem_inc(S("aff_made"), 1)

            for t in range(NT + 1):
                if t < NT:
                    residual(t)
                if t >= 1:
                    keep_h2(t - 1)
                if t < NT:
                    normal(t)
                if t >= 1:
                    soft(t - 1)
            end(dve, "dve")

        affw = RW[0:NE, 0:N_TOK]
        topv = RW[0:NE, N_TOK:N_TOK + CAP]
        topi = RW[0:NE, 2 * N_TOK:2 * N_TOK + CAP].bitcast(U32)
        topf = RW[0:NE, N_TOK + CAP:N_TOK + 2 * CAP]
        val = [st[:, 24:40], st[:, 40:56]]
        idxu = [WK[0:CAP_CTX, 0:NE].bitcast(U32), WK[0:CAP_LAT, NE:2 * NE].bitcast(U32)]
        zero = RW[:, 4 * D:5 * D]
        kinds = ((0, 0, N_CTX, 0, CAP_CTX), (1, N_CTX, N_TOK, CAP_CTX, CAP_LAT))

        def dve_topk(dve, ch):
            begin(dve, "dve", 8)
            dve.memset(zero, 0.0).then_inc(S("zero_made"), 1)
            dve.wait_ge(S("zero_made"), 1)
            for kind, lo, hi, at, cap in kinds:
                cur = affT[:, lo:hi]
                for r in range(cap // 8):
                    v = topv[:, at + 8 * r:at + 8 * r + 8]
                    ch(dve.max(v, cur))
                    ch(dve.max_index(topi[:, at + 8 * r:at + 8 * r + 8], v, cur))
                    if r + 1 < cap // 8:
                        ch(dve.match_replace(affw[:, lo:hi], v, cur, -1.0))
                        cur = affw[:, lo:hi]
            ch(dve.tensor_copy(topf, topi[:, :]))
            ch(dve.tensor_scalar(topf[:, CAP_CTX:CAP], topf[:, CAP_CTX:CAP], float(N_CTX), None, ALU.add))
            dve.sem_inc(S("chosen"), 1)
            dve.wait_ge(S("chosen_turned"), 1)
            for kind, lo, hi, at, cap in kinds:
                ch(dve.tensor_copy(val[kind][0:cap, :], ps[0:cap, 2 * kind * BANK:2 * kind * BANK + NE]))
                ch(dve.tensor_copy(idxu[kind][:, :], ps[0:cap, (2 * kind + 1) * BANK:(2 * kind + 1) * BANK + NE]))
            end(dve, "dve")

        def pe_topk(pe):
            begin(pe, "pe", 8)
            pe.wait_ge(S("chosen"), 1)
            for kind, lo, hi, at, cap in kinds:
                for a, src in enumerate((topv, topf)):
                    b = 2 * kind + a
                    m = pe.transpose(ps[0:cap, b * BANK:b * BANK + NE], src[:, at:at + cap], ident[0:NE, 0:NE])
            m.then_inc(S("chosen_turned"), 1)
            end(pe, "pe")

        def act_idle(k):
            def f(act, ch):
                begin(act, "act", k)
                end(act, "act")
            return f

        def sp_topk(sp):
            begin(sp, "sp", 8)
            for n in range(3):
                for half in range(2):
                    load_expert(sp, 0, n, half)
            sp.wait_ge(S("zero_made"), 1)
            for t in range(NT):
                sp.dma_start(ffn_dram[t * P:(t + 1) * P, :], zero).then_inc(S("ffn_cleared"), 16)

        We = [R1[:, 0:8 * D], R2[:, 2 * D:10 * D], R3[:, 0:8 * D]]
        We = [w.rearrange("p (k n) -> p k n", k=KD) for w in We]
        xg = [work(D, at=64), work(D)]
        xe = work(KD * CAP).rearrange("p (k c) -> p k c", k=KD)
        sl = [work(CAP) for _ in range(2)]
        hid = work(KD * CAP).rearrange("p (k c) -> p k c", k=KD)
        yT = work(KD * CAP).rearrange("p (k c) -> p k c", k=KD)
        yo = [work(D), work(D)]
        ist_g = [WK[0:CAP_CTX, 2 * NE:2 * NE + 1].bitcast(U32), WK[0:CAP_LAT, 2 * NE + 1:2 * NE + 2].bitcast(U32)]
        ist_a = [WK[0:CAP_CTX, 2 * NE + 2:2 * NE + 3].bitcast(U32), WK[0:CAP_LAT, 2 * NE + 3:2 * NE + 4].bitcast(U32)]
        vst = [st[:, 56:57], st[:, 57:58]]
        COL = (CAP_LAT, 0)
        CAPS = (CAP_CTX, CAP_LAT)
        we_dram = (w1[0], w3[0], w2[0])

        def load_expert(sp, e, n, half):
            src = we_dram[n][e] if isinstance(e, int) else we_dram[n][ds(e, 1)].rearrange("a k n -> (a k) n")
            cols = slice(half * BLK, (half + 1) * BLK)
            sp.dma_start(We[n][:, :, cols], src[:, cols].rearrange("(k p) n -> p k n", p=P)).then_inc(S(f"expert_landed{n}{half}"), 16)

        def sp_moe(sp):
            with sp.Fori(1, NE) as e:
                for half in range(2):
                    sp.wait_ge(S("up_half_used"), e * 2 - 1 + half)
                    load_expert(sp, e, 0, half)
                    load_expert(sp, e, 1, half)
                for half in range(2):
                    sp.wait_ge(S("down_half_used"), e * 2 - 1 + half)
                    load_expert(sp, e, 2, half)

        def pool_moe(pool, ch):
            begin(pool, "pool", 9)

            def gather(e):
                for kind in range(2):
                    ch(pool.tensor_copy(ist_g[kind][:, :], idxu[kind][:, ds(e, 1)]))
                pool.sem_inc(S("pool_turns"), 1)
                for kind in (1, 0):
                    pool.indirect_dma_start(xg[kind][0:CAPS[kind], :], None, xhat_dram,
                                            bass.IndirectOffsetOnAxis(ap=ist_g[kind][:, 0:1], axis=0)).then_inc(S("rows_gathered"), 16)

            def add_back(e):
                for kind in range(2):
                    ch(pool.tensor_copy(ist_a[kind][:, :], idxu[kind][:, ds(e, 1)]))
                ch(pool.tensor_copy(vst[1], val[1][:, ds(e, 1)]))
                pool.tensor_copy(vst[0][0:CAP_CTX, :], val[0][0:CAP_CTX, ds(e, 1)]).then_inc(S("scales_staged"), 1)
                pool.wait_ge(S("rows_scaled"), e + 1)
                pool.sem_inc(S("pool_turns"), 1)
                for kind in (1, 0):
                    pool.indirect_dma_start(ffn_dram, bass.IndirectOffsetOnAxis(ap=ist_a[kind][:, 0:1], axis=0),
                                            yo[kind][0:CAPS[kind], :], None, compute_op=ALU.add).then_inc(S("rows_added"), 16)
                pool.wait_ge(S("rows_added"), e * 32 + 32)

            gather(0)
            pool.wait_ge(S("ffn_cleared"), 16 * NT)
            with pool.Fori(1, NE) as e:
                ch.enter(e - 1, 5)
                pool.wait_ge(S("slots_turned"), e * 4)
                gather(e)
                add_back(e - 1)
                ch.leave(NE - 1)
            add_back(NE - 1)
            end(pool, "pool")

        def pe_moe(pe):
            begin(pe, "pe", 9)

            def turn_slots(e, q):
                if q == 0:
                    pe.wait_ge(S("rows_gathered"), e * 32 + 32)
                if q >= 2:
                    pe.wait_ge(S("slots_kept_act") if q % 2 == 0 else S("slots_kept_dve"), e * 2 + 1)
                for k in (2 * q, 2 * q + 1):
                    for kind in (1, 0):
                        cap = CAPS[kind]
                        o = (2 + q % 2) * BANK + (k % 2) * CAP + COL[kind]
                        m = pe.transpose(ps[:, o:o + cap], xg[kind][0:cap, k * P:(k + 1) * P], ident[0:cap, 0:cap])
                m.then_inc(S("slots_turned"), 1)

            def turn_rows(e, half):
                if half == 0:
                    pe.wait_ge(S("down_kept"), e * KD + KD)
                    pe.wait_ge(S("slots_kept_act"), e * 2 + 2)
                    pe.wait_ge(S("slots_kept_dve"), e * 2 + 2)
                else:
                    pe.wait_ge(S("rows_half_scaled"), e + 1)
                for k in range(4 * half, 4 * half + 4):
                    o = (k % 4) * P
                    pe.transpose(ps[:, 2 * BANK + o:2 * BANK + o + P], yT[:, k, 0:CAP_LAT], ident[:, :])
                    m = pe.transpose(ps[0:CAP_CTX, 3 * BANK + o:3 * BANK + o + P], yT[:, k, CAP_LAT:CAP], ident[:, :])
                m.then_inc(S("rows_turned"), 1)

            def up(e, rows):
                pe.wait_ge(S("slots_kept_act"), e * 2 + 2)
                pe.wait_ge(S("slots_kept_dve"), e * 2 + 2)
                for f in range(KD):
                    if f % 4 == 0:
                        for a in range(2):
                            pe.wait_ge(S(f"expert_landed{a}{f // 4}"), e * 16 + 16)
                    for a in range(2):
                        if rows or f >= 2:
                            pe.wait_ge(S("hidden_made"), e * KD + (f - 1))
                        for k in range(KD):
                            m = pe.matmul(bank(4 + 2 * a + f % 2, CAP), We[a][:, k, f * P:(f + 1) * P], xe[:, k, :], start=(k == 0), stop=(k == KD - 1))
                        m.then_inc(S(f"up_done{a}"), 1)
                    if f % 4 == 3:
                        pe.wait_ge(S("up_done1"), e * KD + (f + 1))
                        pe.sem_inc(S("up_half_used"), 1)
                    if rows and f < 2:
                        turn_rows(e - 1, f)

            def down(e, slots_too):
                pe.wait_ge(S("hidden_made"), e * KD + KD)
                for d in range(KD):
                    if d % 4 == 0:
                        pe.wait_ge(S(f"expert_landed2{d // 4}"), e * 16 + 16)
                    if d >= 2:
                        pe.wait_ge(S("down_kept"), e * KD + (d - 1))
                    for k in range(KD):
                        m = pe.matmul(bank(d % 2, CAP), We[2][:, k, d * P:(d + 1) * P], hid[:, k, :], start=(k == 0), stop=(k == KD - 1))
                    m.then_inc(S("down_done"), 1)
                    if d % 4 == 3:
                        pe.wait_ge(S("down_done"), e * KD + (d + 1))
                        pe.sem_inc(S("down_half_used"), 1)
                    if slots_too and d < 4:
                        turn_slots(e + 1, d)

            for q in range(4):
                turn_slots(0, q)
            up(0, False)
            with pe.Fori(1, NE) as e:
                down(e - 1, True)
                up(e, True)
            down(NE - 1, False)
            for half in range(2):
                turn_rows(NE - 1, half)
            end(pe, "pe")

        def slots(q):
            for k in (2 * q, 2 * q + 1):
                for kind in (1, 0):
                    o = (2 + q % 2) * BANK + (k % 2) * CAP + COL[kind]
                    yield xe[:, k, COL[kind]:COL[kind] + CAPS[kind]], ps[:, o:o + CAPS[kind]], k, kind

        def act_moe(act, ch):
            begin(act, "act", 9)

            def keep_slots(e, q):
                act.wait_ge(S("slots_turned"), e * 4 + (q + 1))
                for dst, src, k, kind in slots(q):
                    ch(act.activation(dst, src, ACT.Identity, scale=A2[:, k, kind:kind + 1], bias=modT[:, 24 + k, kind:kind + 1]))
                act.sem_inc(S("slots_kept_act"), 1)

            def gates(e):
                for f in range(KD):
                    act.wait_ge(S("up_done0"), e * KD + (f + 1))
                    if f >= 2:
                        act.wait_ge(S("hidden_made"), e * KD + (f - 1))
                    act.activation(sl[f % 2], bank(4 + f % 2, CAP), ACT.Silu).then_inc(S("silu_made"), 1)
                    act.wait_ge(S("silu_made"), e * KD + (f + 1))

            def keep_down(e, slots_too):
                for d in range(KD):
                    act.wait_ge(S("down_done"), e * KD + (d + 1))
                    act.activation(yT[:, d, :], bank(d % 2, CAP), ACT.Copy).then_inc(S("down_kept"), 1)
                    act.wait_ge(S("down_kept"), e * KD + (d + 1))
                    if slots_too and d in (0, 2):
                        keep_slots(e + 1, d)

            keep_slots(0, 0)
            keep_slots(0, 2)
            gates(0)
            with act.Fori(1, NE) as e:
                ch.enter(e - 1, 8)
                keep_down(e - 1, True)
                gates(e)
                ch.leave(NE - 1)
            keep_down(NE - 1, False)
            end(act, "act")

        def dve_moe(dve, ch):
            begin(dve, "dve", 9)

            def keep_slots(e, q):
                dve.wait_ge(S("slots_turned"), e * 4 + (q + 1))
                for dst, src, k, kind in slots(q):
                    ch(dve.tensor_scalar(dst, src, A2[:, k, kind:kind + 1], modT[:, 24 + k, kind:kind + 1], ALU.mult, ALU.add))
                dve.sem_inc(S("slots_kept_dve"), 1)

            def scale_rows(e, half):
                if half == 0:
                    dve.wait_ge(S("scales_staged"), e + 1)
                dve.wait_ge(S("rows_turned"), e * 2 + (half + 1))
                o = slice(half * BLK, (half + 1) * BLK)
                ch(dve.tensor_scalar(yo[1][:, o], bank(2), vst[1], None, ALU.mult))
                ch(dve.tensor_scalar(yo[0][0:CAP_CTX, o], bank(3, BANK, CAP_CTX), vst[0][0:CAP_CTX, :], None, ALU.mult))
                dve.sem_inc(S("rows_half_scaled" if half == 0 else "rows_scaled"), 1)

            def hidden(e, rows):
                for f in range(KD):
                    dve.wait_ge(S("silu_made"), e * KD + (f + 1))
                    dve.wait_ge(S("up_done1"), e * KD + (f + 1))
                    dve.tensor_tensor(hid[:, f, :], sl[f % 2], bank(6 + f % 2, CAP), ALU.mult).then_inc(S("hidden_made"), 1)
                    dve.wait_ge(S("hidden_made"), e * KD + (f + 1))
                    if rows and f < 2:
                        scale_rows(e - 1, f)

            keep_slots(0, 1)
            keep_slots(0, 3)
            hidden(0, False)
            with dve.Fori(1, NE) as e:
                ch.enter(e - 1, 8 + 4)
                keep_slots(e, 1)
                keep_slots(e, 3)
                hidden(e, True)
                ch.leave(NE - 1)
            for half in range(2):
                scale_rows(NE - 1, half)
            end(dve, "dve")

        G2b = [work(D, at=64)] + [work(D)]
        ff = [work(D) for _ in range(3)]
        x1r = [work(D) for _ in range(3)]
        sqf = work(D)
        sf_ = st[:, 0:12]

        def sp_final(sp):
            begin(sp, "sp", 10)

            def load(t):
                if t >= 3:
                    sp.wait_ge(S(f"y_stored{t % 3}"), 16 * (t // 3))
                sp.dma_start(ff[t % 3], ffn_dram[t * P:(t + 1) * P, :]).then_inc(S(f"ffn_back{t % 3}"), 16)
                sp.dma_start(x1r[t % 3], x1_dram[t * P:(t + 1) * P, :]).then_inc(S(f"ffn_back{t % 3}"), 16)
            load(0)
            load(1)
            load(2)
            for t in range(NT):
                sp.wait_ge(S("y_made"), t + 1)
                sp.dma_start(y_rows(t), ff[t % 3]).then_inc(S(f"y_stored{t % 3}"), 16)
                if t + 3 < NT:
                    load(t + 3)
            for r in range(3):
                sp.wait_ge(S(f"y_stored{r}"), 16 * len(range(r, NT, 3)))
            sp.wait_ge(S("ctx_state_stored"), 32 * GH)
            sp.wait_ge(S("new_k_stored"), 16 * 2 * HKV * T_CTX)

        def pe_final(pe):
            begin(pe, "pe", 10)
            pe_bcast(pe, 2 * KD, 6)
            end(pe, "pe")

        def act_final(act, ch):
            begin(act, "act", 10)
            for t in range(NT):
                act.wait_ge(S(f"ffn_back{t % 3}"), 32 * (t // 3 + 1))
                if t >= 1:
                    act.wait_ge(S("x_var"), NT + t)
                act.activation(sqf, ff[t % 3], ACT.Square, accum_out=sf_[:, 0:1]).then_inc(S("x_sumsq"), 1)
                act.wait_ge(S("x_sumsq"), NT + t + 1)
            end(act, "act")

        def pool_final(pool, ch):
            begin(pool, "pool", 10)
            for t in range(NT):
                pool.wait_ge(S("x_var"), NT + t + 1)
                pool.tensor_tensor(sf_[:, 2:3], sf_[:, 1:2], mhalf[:, 0:1], ALU.pow).then_inc(S("x_rstd"), 1)
            end(pool, "pool")

        def dve_final(dve, ch):
            begin(dve, "dve", 10)
            dve_bcast(dve, ch, 2 * KD, 6, G2, G2b)
            for t in range(NT):
                j = kind_of(t)
                dve.wait_ge(S("x_sumsq"), NT + t + 1)
                dve.tensor_scalar(sf_[:, 1:2], sf_[:, 0:1], 1.0 / D, EPS, ALU.mult, ALU.add).then_inc(S("x_var"), 1)
                dve.wait_ge(S("x_rstd"), NT + t + 1)
                ch(dve.scalar_tensor_tensor(ff[t % 3], ff[t % 3], sf_[:, 2:3], G2b[j], ALU.mult, ALU.mult))
                dve.tensor_tensor(ff[t % 3], ff[t % 3], x1r[t % 3], ALU.add).then_inc(S("y_made"), 1)
                dve.wait_ge(S("y_made"), t + 1)
            end(dve, "dve")

        STAGES_SP = [sp_mod, sp_norm, sp_qkv, sp_attn, sp_ma, sp_gla, sp_mb, sp_out, sp_topk, sp_moe, sp_final]
        STAGES_PE = [pe_mod, pe_norm, pe_qkv, pe_attn, pe_ma, pe_gla, pe_mb, pe_out, pe_topk, pe_moe, pe_final]
        STAGES_ACT = [act_mod, act_norm, act_qkv, act_attn, act_ma, act_gla, act_mb, act_out, act_idle(8), act_moe, act_final]
        STAGES_DVE = [dve_mod, dve_norm, dve_qkv, dve_attn, dve_ma, dve_gla, dve_mb, dve_out, dve_topk, dve_moe, dve_final]
        STAGES_POOL = [pool_mod, pool_norm, pool_qkv, pool_attn, pool_idle(4), pool_gla, pool_idle(6), pool_out,
                       pool_idle(8), pool_moe, pool_final]

        @block.sync
        def _(sp):
            for f in STAGES_SP:
                f(sp)

        @block.tensor
        def _(pe):
            for f in STAGES_PE:
                f(pe)

        @block.scalar
        def _(act):
            ch = Chain(act, S("act_chain"))
            for f in STAGES_ACT:
                f(act, ch)

        @block.vector
        def _(dve):
            ch = Chain(dve, S("dve_chain"))
            for f in STAGES_DVE:
                f(dve, ch)

        @block.gpsimd
        def _(pool):
            ch = Chain(pool, S("pool_chain"))
            for f in STAGES_POOL:
                f(pool, ch)


_INS = ["x_prompt", "x_sample", "cache_k", "cache_v", "state_gla_fwd", "state_gla_bwd", "c", "c_ctx",
        "g_pre_mix", "g_post_mix", "g_pre_ffn", "g_post_ffn", "w_mod", "b_mod", "w_in", "g_q", "g_k",
        "w_gk2_f", "b_gk_f", "w_gk2_b", "b_gk_b", "g_gla", "w_pa", "w_pg", "w_out", "w_router", "w1", "w3", "w2"]
_OUTS = [(1, N_CTX, D), (1, N_LAT, D), (1, 1, HKV, N_CTX, HD), (1, 1, HKV, N_CTX, HD), (1, 1, GH, DK, DV), (1, 1, GH, DK, DV)]


def host_consts():
    import numpy as np
    i = np.arange(128)
    same = (i[:, None] // 64) == (i[None, :] // 64)
    upto, after = i[:, None] <= i[None, :], i[:, None] > i[None, :]
    since, before = i[:, None] >= i[None, :], i[:, None] < i[None, :]
    chunk = (i[:, None] // 64) == np.arange(2)[None, :]
    masks = np.concatenate([same & upto, same & after, same & since, same & before, chunk], axis=1).astype(np.float32)
    keep = np.concatenate([same & upto, same & since], axis=1).astype(np.int32)
    freqs = np.float32(10000.0) ** (-np.arange(32, dtype=np.float32) / np.float32(32))
    r = np.repeat(np.arange(16), 64).astype(np.float32)
    col = np.tile(np.arange(64), 16).astype(np.float32)
    ang = np.concatenate([r[:, None] * freqs, col[:, None] * freqs], axis=-1).astype(np.float32)
    rope = np.stack([np.cos(ang), np.sin(ang)]).astype(np.float32)
    return {"k_ident": np.eye(128, dtype=np.float32), "k_masks": masks, "k_keep": keep, "k_rope": rope}


def kernel(**inputs):
    import numpy as _np
    import concourse.bacc as _bacc
    from concourse import mybir as _mybir
    from concourse.bass_utils import run_bass_kernel_spmd as _run

    nc = _bacc.Bacc("TRN2", target_bir_lowering=False, num_devices=1)
    arrays, args = {}, []
    given = {name: _np.ascontiguousarray(inputs[name]) for name in _INS}
    given.update(host_consts())
    for name, a in given.items():
        arrays[f"in_{name}_dram"] = a
        args.append(nc.dram_tensor(f"in_{name}_dram", a.shape, _mybir.dt.from_np(a.dtype), kind="ExternalInput").ap())
    for i, shape in enumerate(_OUTS):
        args.append(nc.dram_tensor(f"out_{i}_dram", shape, F32, kind="ExternalOutput").ap())
    build_program(nc, *args)
    r = _run(nc, [arrays], core_ids=[0])
    return tuple(r.results[0][f"out_{i}_dram"] for i in range(len(_OUTS)))
```

```python
from contextlib import ExitStack

import concourse.bass as bass
from concourse import mybir

F32 = mybir.dt.float32
F32R = mybir.dt.float32r
U32 = mybir.dt.uint32
I32 = mybir.dt.int32
ALU = mybir.AluOpType
ACT = mybir.ActivationFunctionType
AX = mybir.AxisListType.X
ds = bass.ds

P = 128
D = 1024
KD = D // P
N_CTX, N_LAT, N_PAST = 256, 1024, 512
T_CTX, T_LAT = N_CTX // P, N_LAT // P
NT = T_CTX + T_LAT
N_TOK = N_CTX + N_LAT
HQ, HKV, HD = 8, 2, 128
GQ = HQ // HKV
GH, DK, DV, RANK, CHUNK = 4, 128, 256, 16, 64
GATE_NORM = 16.0
NE = 16
CAP_CTX, CAP_LAT = 2 * N_CTX // NE, 2 * N_LAT // NE
CAP = CAP_CTX + CAP_LAT
EPS = 1e-6
SCALE = float(HD) ** -0.5
GSCALE = float(DK) ** -0.5
BLK = 512
BANK = 512
C_Q, C_K, C_V = 0, 1024, 1280
C_QG, C_KG, C_VG, C_RG = 1536, 2048, 2560, 3584
C_LR = 4608
C_GA, C_GB = 4640, 5664


def kind_of(t):
    return 0 if t < T_CTX else 1


class Chain:

    def __init__(self, eng, sem):
        self.eng, self.sem, self.n, self.off = eng, sem, 0, None

    def at(self, n):
        return n if self.off is None else self.off + n

    def __call__(self, ins):
        self.n += 1
        ins.then_inc(self.sem, 1)
        self.eng.wait_ge(self.sem, self.at(self.n))

    def enter(self, i, per):
        self.off, self.start, self.per = i * per, self.n, per

    def leave(self, turns):
        assert self.n - self.start == self.per, (self.n - self.start, self.per)
        self.n = self.start + turns * self.per
        self.off = None


def build_program(nc, x_prompt, x_sample, cache_k, cache_v, state_gla_fwd, state_gla_bwd, c, c_ctx,
                  g_pre_mix, g_post_mix, g_pre_ffn, g_post_ffn, w_mod, b_mod, w_in, g_q, g_k,
                  w_gk2_f, b_gk_f, w_gk2_b, b_gk_b, g_gla, w_pa, w_pg, w_out, w_router, w1, w3, w2,
                  k_ident, k_masks, k_keep, k_rope,
                  y_prompt, y_sample, new_k, new_v, new_sf, new_sb):
    ctx = ExitStack()
    with ctx:
        sems = {}

        def S(name):
            if name not in sems:
                sems[name] = ctx.enter_context(nc.semaphore(name))
            return sems[name]

        def sb(name, shape, dt=F32):
            return ctx.enter_context(nc.sbuf_tensor(name, shape, dt))

        ps = ctx.enter_context(nc.psum_tensor("ps", [P, 8 * BANK], F32))
        R1 = sb("R1", [P, NT * D])
        R2 = sb("R2", [P, NT * D])
        R3 = sb("R3", [P, NT * D])
        RW = sb("RW", [P, 2 * KD * BLK])
        WORK_N = 12304
        ident = sb("ident", [P, P])
        masks = sb("masks", [P, 4 * P + 2])
        keep = sb("keep", [P, 2 * P], I32)
        modT = sb("modT", [P, 48, 2])
        gv = sb("gv", [P, 4, KD])
        A1 = sb("A1", [P, KD, 2])
        G1 = sb("G1", [P, KD, 2])
        A2 = sb("A2", [P, KD, 2])
        G2 = sb("G2", [P, KD, 2])
        cS = sb("cS", [P, KD, 2])
        bg = sb("bg", [P, KD])
        gqk = sb("gqk", [P, 2, HD])
        ggT = sb("ggT", [P, 2])
        st = sb("st", [P, 64])
        mhalf = sb("mhalf", [P, 16])
        w_lr = sb("w_lr", [P, KD, 2 * RANK])
        wr = sb("wr", [P, KD * NE + P - NE])
        with nc.sbuf_tensor("WK", [P, WORK_N], F32) as WK:
            pass
        Wsplit = [sb(f"W_{n}", [P, KD, BLK], F32R) for n in ("high", "low")]
        Tsplit = [sb(f"tile_{n}", [P, 2, KD, P], F32R) for n in ("high", "low")]
        assert 2 * KD * BLK + 4 * D <= WORK_N
        affT = R2[0:NE, 0:N_TOK]
        xhat_dram = nc.dram_tensor("xhat_scratch", (N_TOK, D), F32, kind="Internal").ap()
        x1_dram = nc.dram_tensor("x1_scratch", (N_TOK, D), F32, kind="Internal").ap()
        ffn_dram = nc.dram_tensor("ffn_scratch", (N_TOK, D), F32, kind="Internal").ap()

        hT = R1[:, :].rearrange("p (k t) -> p k t", k=KD)
        Wslot = [RW[:, s * KD * BLK:(s + 1) * KD * BLK].rearrange("p (k n) -> p k n", k=KD) for s in range(2)]

        def bank(b, n=BANK, parts=P):
            return ps[0:parts, b * BANK:b * BANK + n]

        used = [0]

        def work(n, at=None):
            if at is not None:
                used[0] = at
            o = used[0]
            used[0] += n
            assert used[0] <= WORK_N, used[0]
            return WK[:, o:o + n]

        xp = x_prompt.rearrange("a t d -> (a t) d")
        xs_ = x_sample.rearrange("a t d -> (a t) d")
        yp = y_prompt.rearrange("a t d -> (a t) d")
        ys = y_sample.rearrange("a t d -> (a t) d")

        def x_rows(t):
            return xp[t * P:(t + 1) * P, :] if t < T_CTX else xs_[(t - T_CTX) * P:(t - T_CTX + 1) * P, :]

        def y_rows(t):
            return yp[t * P:(t + 1) * P, :] if t < T_CTX else ys[(t - T_CTX) * P:(t - T_CTX + 1) * P, :]

        wmod, win = w_mod[0], w_in[0]
        wpa, wpg, wout = w_pa[0], w_pg[0], w_out[0]

        units = []
        mod_u = len(units)
        units += [[(wmod, u * BLK, BLK, 0)] for u in range(10)]
        kv_u = len(units)
        units += [[(win, C_K, BLK, 0)]]
        q_u = len(units)
        units += [[(win, C_Q + cb * BLK, BLK, 0)] for cb in range(2)]
        ma_u = len(units)
        for cb in range(2):
            units += [[(win, C_GA + cb * BLK, BLK, 0)], [(wpa, cb * BLK, BLK, 0)]]
        gla_u = len(units)
        for h in range(GH):
            units += [[(win, C_QG + h * DK, DK, 0), (win, C_KG + h * DK, DK, DK), (win, C_VG + h * DV, DV, 2 * DK)],
                      [(win, C_RG + h * DV, DV, 0)]]
        mb_u = len(units)
        for cb in range(2):
            units += [[(win, C_GB + cb * BLK, BLK, 0)], [(wpg, cb * BLK, BLK, 0)]]
        out_u = len(units)
        units += [[(wout, cb * BLK, BLK, 0)] for cb in range(2)]
        g2_u = len(units)
        units += [[(wmod, 5 * D + u * BLK, BLK, 0)] for u in range(2)]
        w_ready, uses, tot = [], [], [0, 0]
        cnt = [0, 0]
        slot = [mb_u % 2 if mb_u <= u < mb_u + 4 else u % 2 for u in range(len(units))]
        for u, dmas in enumerate(units):
            s = slot[u]
            tot[s] += 16 * len(dmas)
            w_ready.append(tot[s])
            uses.append(cnt[s])
            cnt[s] += 1
        w_full = [S("weights_landed_slot0"), S("weights_landed_slot1")]
        w_free = [S("weights_used_slot0"), S("weights_used_slot1")]

        def load_unit(sp, u):
            s = slot[u]
            if uses[u] > 0:
                sp.wait_ge(w_free[s], uses[u])
            for src, c0, n, o in units[u]:
                sp.dma_start(Wslot[s][:, :, o:o + n], src[:, c0:c0 + n].rearrange("(k p) n -> p k n", p=P)) \
                    .then_inc(w_full[s], 16)

        stage_done = {e: S("stage_done_" + e) for e in ("pe", "act", "dve", "pool")}

        def begin(eng, me, k):
            for e in ("pe", "act", "dve", "pool"):
                if e != me:
                    eng.wait_ge(stage_done[e], k)

        def end(eng, me, stages=1):
            eng.drain().then_inc(stage_done[me], stages)

        def gemm(pe, out, lhs, slot, width=BLK, off=0):
            for k in range(KD):
                m = pe.matmul(out, lhs(k), Wslot[slot][:, k, off:off + width], start=(k == 0), stop=(k == KD - 1))
            return m


        block = ctx.enter_context(nc.Block())

        cT = work(16, at=0).rearrange("p (k j) -> p k j", j=2)
        modrow = R3[0:2, 0:6 * D]
        brow = R2[0:2, 0:6 * D]
        x_t = [work(D, at=64)] + [work(D) for _ in range(2)]
        xn_t = [work(D) for _ in range(2)]
        sq_t = work(D)
        vv = work(14 * 256).rearrange("p (b n) -> p b n", b=14)
        cos_t = work(T_LAT * 64).rearrange("p (t f) -> p t f", t=T_LAT)
        sin_t = work(T_LAT * 64).rearrange("p (t f) -> p t f", t=T_LAT)
        ck = work(HKV * 4 * HD).rearrange("p (g b d) -> p g b d", g=HKV, b=4)
        ss1, var1, rstd1 = st[:, 0:10], st[:, 10:20], st[:, 20:30]
        NU = 5 * D // BLK
        PRE = 2 * D // BLK
        x_behind = {PRE + n: tl for n, tl in enumerate([[0, 1], [2], [3, 4], [5, 6], [7, 8], [9]])}
        N_CONST = 13 * 16

        def sp_mod(sp):
            for u in range(PRE):
                load_unit(sp, u)
                if u == 0:
                    sp.wait_ge(w_full[0], w_ready[0])
            n = 0
            for dst, src in (
                (ident[:, :], k_ident),
                (gv[:, 0, :], g_pre_mix[0].rearrange("(k p) -> p k", p=P)),
                (gv[:, 1, :], g_post_mix[0].rearrange("(k p) -> p k", p=P)),
                (gv[:, 2, :], g_pre_ffn[0].rearrange("(k p) -> p k", p=P)),
                (gv[:, 3, :], g_post_ffn[0].rearrange("(k p) -> p k", p=P)),
                (bg[:, :], b_mod[0, 5 * D:6 * D].rearrange("(k p) -> p k", p=P)),
                (masks[:, :], k_masks), (keep[:, :], k_keep),
                (gqk[:, 0, :], g_q[0:1, :].broadcast_to([P, HD])),
                (gqk[:, 1, :], g_k[0:1, :].broadcast_to([P, HD])),
                (ggT[:, :], g_gla[0].rearrange("(k p) -> p k", p=P)),
                (w_lr[:, :, :], win[:, C_LR:C_LR + 2 * RANK].rearrange("(k p) n -> p k n", p=P)),
                (wr[:, 0:KD * NE].rearrange("p (k n) -> p k n", k=KD), w_router[0].rearrange("(k p) n -> p k n", p=P)),
            ):
                sp.dma_start(dst, src, allow_slow_non_contiguous=True).then_inc(S("consts_landed"), 16)
                n += 16
            assert n == N_CONST
            for u in range(PRE, NU):
                load_unit(sp, u)
                if u == PRE + 1:
                    for g in range(HKV):
                        sp.dma_start(ck[:, g, :, :], cache_k[0, 0, g].rearrange("(b p) d -> p b d", p=P)).then_inc(S("cache_landed"), 16)
                        sp.dma_start(vv[:, 0:4, g * HD:(g + 1) * HD], cache_v[0, 0, g].rearrange("(b p) d -> p b d", p=P)).then_inc(S("cache_landed"), 16)
                    sp.dma_start(cos_t, k_rope[0].rearrange("(t p) f -> p t f", p=P)).then_inc(S("cache_landed"), 16)
                    sp.dma_start(sin_t, k_rope[1].rearrange("(t p) f -> p t f", p=P)).then_inc(S("cache_landed"), 16)
            load_unit(sp, kv_u)
            load_unit(sp, q_u)


        def pe_mod(pe):
            pe.wait_ge(S("cond_ready"), 1)

            def unit(u):
                s = u % 2
                pe.wait_ge(w_full[s], w_ready[u])
                if u >= 2:
                    pe.wait_ge(S("mod_row_kept"), u - 1)
                for k in range(KD):
                    m = pe.matmul(bank(s, BLK, 2), cS[:, k, :], Wslot[s][:, k, :], start=(k == 0), stop=(k == KD - 1))
                m.then_inc(S("mod_row"), 1)
                pe.wait_ge(S("mod_row"), u + 1)
                pe.sem_inc(w_free[s], 1)

            def columns(lo, hi):
                pe.wait_ge(S("mod_row_kept"), hi)
                pe.wait_ge(S("consts_landed"), N_CONST)
                for n in range(4 * lo, 4 * hi):
                    m = pe.transpose(ps[:, 2 * BANK + 2 * n:2 * BANK + 2 * n + 2], modrow[:, n * P:(n + 1) * P], ident[0:2, 0:2])
                m.then_inc(S("mod_columns"), 1)

            def turn(t):
                pe.wait_ge(S("x_scaled"), t + 1)
                if t >= 2:
                    pe.wait_ge(S("h_kept_act"), t - 1)
                    pe.wait_ge(S("h_kept_dve"), t - 1)
                for k in range(KD):
                    o = (4 + 2 * (t % 2)) * BANK + k * P
                    m = pe.transpose(ps[:, o:o + P], xn_t[t % 2][:, k * P:(k + 1) * P], ident[:, :])
                m.then_inc(S("x_turned"), 1)

            for u in range(PRE):
                unit(u)
            columns(0, PRE)
            for u in range(PRE, NU):
                unit(u)
                for t in x_behind[u]:
                    turn(t)
            pe.wait_ge(S("pre_scale_ready"), 1)
            columns(PRE, NU)
            end(pe, "pe", 2)

        def act_mod(act, ch):
            for dst, src in ((cT[:, :, 0], c_ctx.rearrange("(k p) -> p k", p=P)), (cT[:, :, 1], c[0].rearrange("(k p) -> p k", p=P))):
                act.dma_start(dst, src, allow_slow_non_contiguous=True).then_inc(S("cond_landed"), 16)
            for r in range(2):
                act.dma_start(brow[r:r + 1, :], b_mod[0:1, :]).then_inc(S("bias_landed"), 16)
            act.wait_ge(S("cond_landed"), 32)
            act.activation(cS[:, :, :], cT, ACT.Silu).then_inc(S("cond_ready"), 1)

            def square(t):
                act.wait_ge(S(f"x_landed{t % 3}"), 16 * (t // 3 + 1))
                if t >= 1:
                    act.wait_ge(S("x_sumsq"), t)
                act.activation(sq_t, x_t[t % 3], ACT.Square, accum_out=ss1[:, t:t + 1]).then_inc(S("x_sumsq"), 1)

            square(0)
            square(1)
            for t in range(NT):
                if t + 2 < NT:
                    square(t + 2)
                act.wait_ge(S("x_turned"), t + 1)
                act.wait_ge(S("pre_scale_ready"), 1)
                j = kind_of(t)
                for k in range(4):
                    o = (4 + 2 * (t % 2)) * BANK + k * P
                    m = act.activation(hT[:, k, t * P:(t + 1) * P], ps[:, o:o + P], ACT.Identity, scale=A1[:, k, j:j + 1], bias=modT[:, k, j:j + 1])
                    if k < 3:
                        ch(m)
                m.then_inc(S("h_kept_act"), 1)
                act.wait_ge(S("h_kept_act"), t + 1)
            end(act, "act", 2)

        def dve_mod(dve, ch):
            dve.wait_ge(S("bias_landed"), 32)

            def row(u):
                dve.wait_ge(S("mod_row"), u + 1)
                o = slice(u * BLK, (u + 1) * BLK)
                dve.tensor_tensor(modrow[:, o], bank(u % 2, BLK, 2), brow[:, o], ALU.add).then_inc(S("mod_row_kept"), 1)

            def scale(t):
                dve.wait_ge(S("x_rstd"), t + 1)
                if t >= 2:
                    dve.wait_ge(S("x_turned"), t - 1)
                dve.tensor_scalar(xn_t[t % 2], x_t[t % 3], rstd1[:, t:t + 1], None, ALU.mult).then_inc(S("x_scaled"), 1)

            def g(n):
                return gv[:, n, :].unsqueeze(2).broadcast_to([P, KD, 2])

            def columns(lo, hi):
                return dve.tensor_copy(modT[:, 4 * lo:4 * hi, :], ps[:, 2 * BANK + 8 * lo:2 * BANK + 8 * hi].rearrange("p (a b) -> p a b", b=2))

            scale(0)
            scale(1)
            for u in range(PRE):
                row(u)
            dve.wait_ge(S("mod_columns"), 1)
            dve.wait_ge(S("consts_landed"), N_CONST)
            ch(columns(0, PRE))
            ch(dve.scalar_tensor_tensor(A1[:, :, :], modT[:, 8:16, :], 1.0, g(0), ALU.add, ALU.mult))
            dve.sem_inc(S("pre_scale_ready"), 1)
            for u in range(PRE, NU):
                row(u)
                for t in x_behind[u]:
                    if t + 2 < NT:
                        scale(t + 2)
                    dve.wait_ge(S("x_turned"), t + 1)
                    j = kind_of(t)
                    for k in range(4, 8):
                        o = (4 + 2 * (t % 2)) * BANK + k * P
                        m = dve.tensor_scalar(hT[:, k, t * P:(t + 1) * P], ps[:, o:o + P], A1[:, k, j:j + 1], modT[:, k, j:j + 1], ALU.mult, ALU.add)
                        if k < 7:
                            ch(m)
                    m.then_inc(S("h_kept_dve"), 1)
                    dve.wait_ge(S("h_kept_dve"), t + 1)
            dve.wait_ge(S("mod_columns"), 2)
            ch(columns(PRE, NU))
            ch(dve.tensor_tensor(G1[:, :, :], modT[:, 16:24, :], g(1), ALU.mult))
            ch(dve.scalar_tensor_tensor(A2[:, :, :], modT[:, 32:40, :], 1.0, g(2), ALU.add, ALU.mult))
            ch(dve.tensor_tensor(bg[:, :], bg[:, :], gv[:, 3, :], ALU.mult))
            end(dve, "dve", 2)

        def pool_mod(pool, ch):
            ch(pool.memset(mhalf[:, :], -0.5))
            ch(pool.memset(wr[:, KD * NE:], 0.0))

            def load(t):
                if t >= 3:
                    pool.wait_ge(S("x_scaled"), t - 2)
                pool.dma_start(x_t[t % 3], x_rows(t)).then_inc(S(f"x_landed{t % 3}"), 16)
            pool.wait_ge(w_full[0], w_ready[0])
            for t in range(3):
                load(t)
            for t in range(NT):
                pool.wait_ge(S("x_sumsq"), t + 1)
                ch(pool.tensor_scalar(var1[:, t:t + 1], ss1[:, t:t + 1], 1.0 / D, EPS, ALU.mult, ALU.add))
                pool.tensor_tensor(rstd1[:, t:t + 1], var1[:, t:t + 1], mhalf[:, 0:1], ALU.pow).then_inc(S("x_rstd"), 1)
                if t + 3 < NT:
                    load(t + 3)
            end(pool, "pool", 2)

        sqk = work(BLK, at=0)
        nrm = [work(BLK) for _ in range(2)]
        rot = [work(BLK) for _ in range(2)]
        rtmp = work(256)
        rtmp2 = work(256)
        ssq, varq, rsq = st[:, 32:36], st[:, 36:40], st[:, 40:44]
        NK = N_PAST + N_LAT + N_CTX
        kT = R3[:, 0:HKV * NK].rearrange("p (g l) -> p g l", g=HKV)
        assert HKV * NK + 12 * BLK <= NT * D
        K_CTX = N_PAST + N_LAT

        def key_at(t):
            return K_CTX + t * P if t < T_CTX else N_PAST + (t - T_CTX) * P

        def val_at(t):
            return 12 + t if t < T_CTX else 4 + t - T_CTX
        qkv_steps = [(kv_u, t) for t in range(NT)] + [(q_u + cb, t) for cb in range(2) for t in range(NT)]

        def sp_qkv(sp):
            for t in range(T_CTX):
                sp.wait_ge(S("qk_turned_ready"), t + 1)
                for g in range(HKV):
                    rows = slice(t * P, (t + 1) * P)
                    sp.dma_start(new_k[0, 0, g, rows, :], nrm[t % 2][:, g * HD:(g + 1) * HD]).then_inc(S("new_k_stored"), 16)
                    sp.dma_start(new_v[0, 0, g, rows, :], vv[:, 12 + t, g * HD:(g + 1) * HD]).then_inc(S("new_k_stored"), 16)
            for u in range(q_u + 1, ma_u + 2):
                load_unit(sp, u)

        def heads_of(u):
            return HKV if u == kv_u else GQ

        def pe_qkv(pe):
            begin(pe, "pe", 2)
            pe.wait_ge(S("cache_landed"), 16 * 6)
            for g in range(HKV):
                for b in range(4):
                    m = pe.transpose(ps[:, (2 + g) * BANK + b * P:(2 + g) * BANK + (b + 1) * P], ck[:, g, b, :], ident[:, :])
            m.then_inc(S("cached_keys_turned"), 1)

            def turn(n):
                u, t = qkv_steps[n]
                pe.wait_ge(S("qk_turned_ready"), n + 1)
                if n >= 2:
                    pe.wait_ge(S("qk_turned_kept"), n - 1)
                for h in range(heads_of(u)):
                    src = rot[n % 2] if t >= T_CTX else nrm[n % 2]
                    m = pe.transpose(ps[:, (n % 2) * BANK + h * P:(n % 2) * BANK + (h + 1) * P], src[:, h * HD:(h + 1) * HD], ident[:, :])
                m.then_inc(S("qk_turned"), 1)

            for n, (u, t) in enumerate(qkv_steps):
                if t == 0:
                    pe.wait_ge(w_full[u % 2], w_ready[u])
                if n >= 4:
                    pe.wait_ge(S("qk_bank_free"), n - 3)
                m = gemm(pe, bank(4 + n % 4), lambda k: hT[:, k, t * P:(t + 1) * P], u % 2)
                m.then_inc(S("qk_projected"), 1)
                if t == NT - 1:
                    pe.wait_ge(S("qk_projected"), n + 1)
                    pe.sem_inc(w_free[u % 2], 1)
                if n >= 1:
                    turn(n - 1)
            turn(len(qkv_steps) - 1)
            end(pe, "pe")

        def act_qkv(act, ch):
            begin(act, "act", 2)
            act.wait_ge(S("cached_keys_turned"), 1)
            ch(act.activation(kT[:, 0, 0:N_PAST], bank(2), ACT.Copy))
            ch(act.activation(kT[:, 1, 0:N_PAST], bank(3), ACT.Copy))

            def keep_turned(n):
                u, t = qkv_steps[n]
                act.wait_ge(S("qk_turned"), n + 1)
                if u == kv_u:
                    m = act.activation(kT[:, :, key_at(t):key_at(t) + P], bank(n % 2, 2 * P).rearrange("p (g l) -> p g l", g=2), ACT.Copy)
                else:
                    o = (t * HQ + GQ * (u - q_u)) * P
                    m = act.activation(R2[:, o:o + GQ * P], bank(n % 2), ACT.Copy)
                m.then_inc(S("qk_turned_kept"), 1)
                act.wait_ge(S("qk_turned_kept"), n + 1)

            for n, (u, t) in enumerate(qkv_steps):
                act.wait_ge(S("qk_projected"), n + 1)
                b = 4 + n % 4
                w = heads_of(u) * HD
                if u == kv_u:
                    ch(act.activation(vv[:, val_at(t), :], ps[:, b * BANK + 256:b * BANK + 512], ACT.Copy))
                if n >= 1:
                    act.wait_ge(S("qk_bank_free"), n)
                act.activation(sqk[:, 0:w], bank(b, w), ACT.Square).then_inc(S("qk_squared"), 1)
                act.wait_ge(S("qk_squared"), n + 1)
                if n >= 1:
                    keep_turned(n - 1)
            keep_turned(len(qkv_steps) - 1)
            end(act, "act")

        def pool_qkv(pool, ch):
            begin(pool, "pool", 2)
            for n in range(len(qkv_steps)):
                pool.wait_ge(S("qk_var"), n + 1)
                pool.tensor_tensor(rsq, varq, mhalf[:, 0:4], ALU.pow).then_inc(S("qk_rstd"), 1)
            end(pool, "pool")

        def dve_qkv(dve, ch):
            begin(dve, "dve", 2)
            dve.wait_ge(S("cache_landed"), 16 * 6)
            ch(dve.memset(varq, 1.0))
            for n, (u, t) in enumerate(qkv_steps):
                H = heads_of(u)
                w = H * HD
                src = bank(4 + n % 4, w)
                dve.wait_ge(S("qk_squared"), n + 1)
                ch(dve.tensor_reduce(ssq[:, 0:H], sqk[:, 0:w].rearrange("p (h d) -> p h d", h=H), AX, ALU.add))
                if n >= 2:
                    dve.wait_ge(S("qk_turned"), n - 1)
                if n == 2:
                    dve.wait_ge(S("new_k_stored"), 16 * 2 * HKV * T_CTX)
                dve.tensor_scalar(varq[:, 0:H], ssq[:, 0:H], 1.0 / HD, EPS, ALU.mult, ALU.add).then_inc(S("qk_var"), 1)
                dve.wait_ge(S("qk_rstd"), n + 1)
                for h in range(H):
                    m = dve.scalar_tensor_tensor(nrm[n % 2][:, h * HD:(h + 1) * HD], src[:, h * HD:(h + 1) * HD], rsq[:, h:h + 1],
                                                 gqk[:, (1 if u == kv_u else 0), :], ALU.mult, ALU.mult)
                    if h < H - 1:
                        ch(m)
                m.then_inc(S("qk_bank_free"), 1)
                dve.wait_ge(S("qk_bank_free"), n + 1)
                if t >= T_CTX:
                    v = nrm[n % 2][:, 0:w].rearrange("p (h f e) -> p h f e", h=H, e=2)
                    r = rot[n % 2][:, 0:w].rearrange("p (h f e) -> p h f e", h=H, e=2)
                    t1 = rtmp[:, 0:H * 64].rearrange("p (h f) -> p h f", h=H)
                    t2 = rtmp2[:, 0:H * 64].rearrange("p (h f) -> p h f", h=H)
                    cs = cos_t[:, t - T_CTX, :].unsqueeze(1).broadcast_to([P, H, 64])
                    sn = sin_t[:, t - T_CTX, :].unsqueeze(1).broadcast_to([P, H, 64])
                    ch(dve.tensor_tensor(t1, v[:, :, :, 0], cs, ALU.mult))
                    ch(dve.tensor_tensor(t2, v[:, :, :, 1], sn, ALU.mult))
                    ch(dve.tensor_tensor(r[:, :, :, 0], t1, t2, ALU.subtract))
                    ch(dve.tensor_tensor(t1, v[:, :, :, 0], sn, ALU.mult))
                    ch(dve.tensor_tensor(t2, v[:, :, :, 1], cs, ALU.mult))
                    m = dve.tensor_tensor(r[:, :, :, 1], t1, t2, ALU.add)
                else:
                    m = dve.tensor_copy(rtmp[:, 0:1], ssq[:, 0:1])
                m.then_inc(S("qk_turned_ready"), 1)
                dve.wait_ge(S("qk_turned_ready"), n + 1)
            end(dve, "dve")

        Pb = [work(1536, at=0)] + [work(1536)]
        qst = [work(GQ * P) for _ in range(HKV)]
        pT = [R3[:, HKV * NK + s * 12 * 2 * P:HKV * NK + (s + 1) * 12 * 2 * P].rearrange("p (b n) -> p b n", b=12) for s in range(2)]
        mxa, nmx, sma, rsm = st[:, 44:46], st[:, 46:48], st[:, 48:50], st[:, 50:52]
        FIRST, LAST = 0, NT - 1

        def tile_plan(T):
            return (2, K_CTX, 12) if isinstance(T, int) and T < T_CTX else (12, 0, 0)

        def sset(s):
            return (s % 2) * 3 * BANK

        def over_tiles(eng, tile):
            for T in range(T_CTX + 1):
                tile(T)
            with eng.Fori(T_CTX + 1, LAST) as T:
                tile(T)
            tile(LAST)

        def ahead(T, k, by):
            if k + by < HQ:
                return T, k + by
            return None if isinstance(T, int) and T == LAST else (T + 1, k + by - HQ)

        def pool_attn(pool, ch):
            begin(pool, "pool", 3)

            def stage(T):
                for g in range(HKV):
                    if not (isinstance(T, int) and T == FIRST):
                        pool.wait_ge(S("scores_done"), T * HQ - HQ + GQ * (g + 1))
                    o = T * D + g * GQ * P
                    pool.tensor_copy(qst[g], R2[:, o:o + GQ * P] if isinstance(T, int) else R2[:, ds(o, GQ * P)]) \
                        .then_inc(S(f"queries_staged{g}"), 1)
            over_tiles(pool, stage)
            end(pool, "pool")

        def pe_attn(pe):
            begin(pe, "pe", 3)

            def scores(T, k):
                nk, k0, _ = tile_plan(T)
                g, j = k // GQ, k % GQ
                if j == 0:
                    pe.wait_ge(S(f"queries_staged{g}"), T + 1)
                if not (isinstance(T, int) and T == FIRST and k < 2):
                    pe.wait_ge(S("probsT_kept_act"), T * HQ + (k - 1))
                    pe.wait_ge(S("probsT_kept_dve"), T * HQ + (k - 1))
                for c0 in range(0, nk * P, BLK):
                    w = min(BLK, nk * P - c0)
                    m = pe.matmul(ps[:, sset(k) + c0:sset(k) + c0 + w], qst[g][:, j * P:(j + 1) * P],
                                  kT[:, g, k0 + c0:k0 + c0 + w], start=True, stop=True)
                m.then_inc(S("scores_done"), 1)

            def turn(T, k):
                nk = tile_plan(T)[0]
                pe.wait_ge(S("probs_scaled"), T * HQ + (k + 1))
                at = [0, 2 * BANK] if nk == 2 else [b * P for b in range(nk)]
                for b in range(nk):
                    m = pe.transpose(ps[:, sset(k) + at[b]:sset(k) + at[b] + P], Pb[k % 2][:, b * P:(b + 1) * P], ident[:, :])
                    if b == (0 if nk == 2 else 7):
                        m.then_inc(S("probsT_act"), 1)
                m.then_inc(S("probsT_dve"), 1)

            def weigh(T, q, part, plan):
                nk, _, v0 = plan
                g = q // 2
                if part == 0:
                    pe.wait_ge(S("probsT_kept_act"), T * HQ + (2 * q + 2))
                    pe.wait_ge(S("probsT_kept_dve"), T * HQ + (2 * q + 2))
                    if not (isinstance(T, int) and T == FIRST and q < 2):
                        pe.wait_ge(S("attn_kept"), T * GQ + (q - 1))
                for b in range(part * nk // 2, (part + 1) * nk // 2):
                    m = pe.matmul(bank(6 + q % 2, 2 * P), vv[:, v0 + b, g * HD:(g + 1) * HD], pT[q % 2][:, b, :], start=(b == 0), stop=(b == nk - 1))
                if part == 1:
                    m.then_inc(S("values_weighed"), 1)

            def tile(T):
                for k in range(HQ):
                    turn(T, k)
                    if k >= 2:
                        weigh(T, k // 2 - 1, k % 2, tile_plan(T))
                    elif not (isinstance(T, int) and T == FIRST):
                        weigh(T - 1, 3, k % 2, tile_plan(T - 1 if isinstance(T, int) else LAST))
                    nxt = ahead(T, k, 2)
                    if nxt:
                        scores(*nxt)

            scores(0, 0)
            scores(0, 1)
            over_tiles(pe, tile)
            for part in range(2):
                weigh(LAST, 3, part, tile_plan(LAST))
            end(pe, "pe")

        def dve_attn(dve, ch):
            begin(dve, "dve", 3)

            def top(T, k):
                b = k % 2
                dve.wait_ge(S("scores_done"), T * HQ + (k + 1))
                ch(dve.tensor_reduce(mxa[:, b:b + 1], ps[:, sset(k):sset(k) + tile_plan(T)[0] * P], AX, ALU.max))
                dve.tensor_scalar(nmx[:, b:b + 1], mxa[:, b:b + 1], -SCALE, None, ALU.mult).then_inc(S("max_ready"), 1)

            def norm(T, k):
                b = k % 2
                w = tile_plan(T)[0] * P
                dve.wait_ge(S("probs_ready"), T * HQ + (k + 1))
                ch(dve.reciprocal(rsm[:, b:b + 1], sma[:, b:b + 1]))
                dve.tensor_scalar(Pb[b][:, 0:w], Pb[b][:, 0:w], rsm[:, b:b + 1], None, ALU.mult).then_inc(S("probs_scaled"), 1)

            def keep_turned(T, k):
                j = k % 2
                dve.wait_ge(S("probsT_dve"), T * HQ + (k + 1))
                if j == 0 and not (isinstance(T, int) and T == FIRST and k < 4):
                    dve.wait_ge(S("values_weighed"), T * GQ + (k // 2 - 1))
                dst = pT[(k // 2) % 2]
                if tile_plan(T)[0] == 2:
                    m = dve.tensor_copy(dst[:, 1, j * P:(j + 1) * P], ps[:, sset(k) + 2 * BANK:sset(k) + 2 * BANK + P])
                else:
                    m = dve.tensor_copy(dst[:, 8:12, j * P:(j + 1) * P],
                                        ps[:, sset(k) + 2 * BANK:sset(k) + 3 * BANK].rearrange("p (b q) -> p b q", b=4))
                m.then_inc(S("probsT_kept_dve"), 1)

            def tile(T):
                inside = not isinstance(T, int)
                if inside:
                    ch.enter(T - (T_CTX + 1), 2 * HQ)
                for k in range(HQ):
                    nxt = ahead(T, k, 1)
                    if nxt:
                        top(*nxt)
                    keep_turned(T, k)
                    if nxt:
                        norm(*nxt)
                if inside:
                    ch.leave(LAST - (T_CTX + 1))

            top(0, 0)
            norm(0, 0)
            over_tiles(dve, tile)
            end(dve, "dve")

        def act_attn(act, ch):
            begin(act, "act", 3)

            def exps(T, k):
                b = k % 2
                w = tile_plan(T)[0] * P
                act.wait_ge(S("max_ready"), T * HQ + (k + 1))
                act.activation(Pb[b][:, 0:w], ps[:, sset(k):sset(k) + w], ACT.Exp, bias=nmx[:, b:b + 1],
                               scale=SCALE, accum_out=sma[:, b:b + 1]).then_inc(S("probs_ready"), 1)

            def keep_turned(T, k):
                j = k % 2
                act.wait_ge(S("probsT_act"), T * HQ + (k + 1))
                if j == 0 and not (isinstance(T, int) and T == FIRST and k < 4):
                    act.wait_ge(S("values_weighed"), T * GQ + (k // 2 - 1))
                dst = pT[(k // 2) % 2]
                if tile_plan(T)[0] == 2:
                    m = act.activation(dst[:, 0, j * P:(j + 1) * P], ps[:, sset(k):sset(k) + P], ACT.Copy)
                else:
                    m = act.activation(dst[:, 0:8, j * P:(j + 1) * P],
                                       ps[:, sset(k):sset(k) + 2 * BANK].rearrange("p (b q) -> p b q", b=8), ACT.Copy)
                m.then_inc(S("probsT_kept_act"), 1)

            def keep_out(T, q):
                act.wait_ge(S("values_weighed"), T * GQ + (q + 1))
                o = T * D + q * 2 * P
                dst = R2[:, o:o + 2 * P] if isinstance(T, int) else R2[:, ds(o, 2 * P)]
                act.activation(dst, bank(6 + q % 2, 2 * P), ACT.Copy).then_inc(S("attn_kept"), 1)

            def tile(T):
                for k in range(HQ):
                    keep_turned(T, k)
                    nxt = ahead(T, k, 1)
                    if nxt:
                        exps(*nxt)
                    if k % 2 == 1:
                        if k > 1:
                            keep_out(T, k // 2 - 1)
                        elif not (isinstance(T, int) and T == FIRST):
                            keep_out(T - 1, 3)

            exps(0, 0)
            over_tiles(act, tile)
            keep_out(LAST, 3)
            end(act, "act")

        def sp_attn(sp):
            pass

        mix = R3[:, :].rearrange("p (t n) -> p t n", t=NT)
        steps_m = [(v, t) for v in range(4) for t in range(NT)]
        sig_slot = 1 - mb_u % 2
        assert sig_slot == slot[gla_u + 1]

        def merge(u0, branch, tag, k_stage, add):
            n0, m0 = 2 * NT * tag, 4 * NT * tag
            w0, c0 = 4 * KD * tag, 4 * (KD - 1) * tag

            def stationary(m):
                v, t = steps_m[m]
                return hT[:, :, t * P:(t + 1) * P] if v % 2 == 0 else branch(t)

            def gate_tile(t, cb):
                if not add:
                    return mix[:, t, cb * BLK:(cb + 1) * BLK]
                return Wslot[sig_slot][:, t % KD, :]

            def pe_merge(pe):
                begin(pe, "pe", k_stage)
                high, low = 0, 1
                for m, (v, t) in enumerate(steps_m):
                    pe.wait_ge(S("tile_split"), m0 + m + 1)
                    if m >= 4:
                        pv, pt = steps_m[m - 4]
                        pe.wait_ge(S("gates_made" if pv % 2 == 0 else "tiles_merged"), n0 + (pv // 2) * NT + pt + 1)
                    for k in range(KD):
                        if t == 0:
                            pe.wait_ge(S("weights_split"), w0 + v * KD + k + 1)
                        for n, (a, b) in enumerate(((high, high), (high, low), (low, high))):
                            i = pe.matmul(bank(m % 4), Tsplit[a][:, m % 2, k, :], Wsplit[b][:, k, :], start=(k == 0 and n == 0), stop=(k == KD - 1 and n == 2))
                        if t == NT - 1 and k < KD - 1:
                            i.then_inc(S("weights_chunk_used"), 1)
                    i.then_inc(S("merge_tile_done"), 1)
                    if t == 0:
                        pe.sem_inc(w_free[slot[u0 + v]], 1)
                end(pe, "pe")

            def chunk_free(eng, v, k):
                if v >= 1:
                    if k < KD - 1:
                        eng.wait_ge(S("weights_chunk_used"), c0 + (v - 1) * (KD - 1) + k + 1)
                    else:
                        eng.wait_ge(S("merge_tile_done"), m0 + v * NT)

            def act_merge(act, ch):
                begin(act, "act", k_stage)

                def tile_high(m):
                    if m >= 2:
                        act.wait_ge(S("merge_tile_done"), m0 + m - 1)
                    act.activation(Tsplit[0][:, m % 2, :, :], stationary(m), ACT.Copy).then_inc(S("tile_high"), 1)

                def weights_high(v):
                    u = u0 + v
                    act.wait_ge(w_full[slot[u]], w_ready[u])
                    for k in range(KD):
                        chunk_free(act, v, k)
                        act.activation(Wsplit[0][:, k, :], Wslot[slot[u]][:, k, :], ACT.Copy).then_inc(S("weights_high"), 1)

                tile_high(0)
                weights_high(0)
                for m, (v, t) in enumerate(steps_m):
                    if m + 1 < len(steps_m):
                        tile_high(m + 1)
                    if t == NT - 1 and v < 3:
                        weights_high(v + 1)
                    if v % 2 == 0:
                        act.wait_ge(S("merge_tile_done"), m0 + m + 1)
                        if add and v:
                            act.wait_ge(S("tiles_merged"), n0 + NT)
                        dst = bank(4 + t - KD) if add and t >= KD else gate_tile(t, v // 2)
                        act.activation(dst, bank(m % 4), ACT.Sigmoid).then_inc(S("gates_made"), 1)
                    elif add and t in (3, 4):
                        act.wait_ge(S("tiles_merged"), n0 + (v // 2) * NT + (t - 2))
                        act.wait_ge(S("gates_made"), n0 + (v // 2 + 1) * NT)
                        act.activation(gate_tile(KD + t - 3, v // 2), bank(4 + t - 3), ACT.Copy).then_inc(S("gates_moved"), 1)
                end(act, "act")

            def dve_merge(dve, ch):
                begin(dve, "dve", k_stage)

                def tile_low(m):
                    if m >= 2:
                        dve.wait_ge(S("merge_tile_done"), m0 + m - 1)
                    dve.wait_ge(S("tile_high"), m0 + m + 1)
                    dve.tensor_tensor(Tsplit[1][:, m % 2, :, :], stationary(m), Tsplit[0][:, m % 2, :, :].bitcast(F32), ALU.subtract).then_inc(S("tile_split"), 1)

                def weights_low(v):
                    u = u0 + v
                    dve.wait_ge(w_full[slot[u]], w_ready[u])
                    for k in range(KD):
                        chunk_free(dve, v, k)
                        dve.wait_ge(S("weights_high"), w0 + v * KD + k + 1)
                        dve.tensor_tensor(Wsplit[1][:, k, :], Wslot[slot[u]][:, k, :], Wsplit[0][:, k, :].bitcast(F32), ALU.subtract).then_inc(S("weights_split"), 1)

                tile_low(0)
                weights_low(0)
                for m, (v, t) in enumerate(steps_m):
                    if m + 1 < len(steps_m):
                        tile_low(m + 1)
                    if t == NT - 1 and v < 3:
                        weights_low(v + 1)
                    if v % 2 == 1:
                        cb = v // 2
                        dve.wait_ge(S("gates_made"), n0 + cb * NT + t + 1)
                        dve.wait_ge(S("merge_tile_done"), m0 + m + 1)
                        if add and t >= KD:
                            dve.wait_ge(S("gates_moved"), 2 * cb + t - KD + 1)
                        dst, gate = mix[:, t, cb * BLK:(cb + 1) * BLK], gate_tile(t, cb)
                        if add:
                            ch(dve.tensor_tensor(gate, gate, bank(m % 4), ALU.mult))
                            i = dve.tensor_tensor(dst, dst, gate, ALU.add)
                        else:
                            i = dve.tensor_tensor(dst, gate, bank(m % 4), ALU.mult)
                        i.then_inc(S("tiles_merged"), 1)
                end(dve, "dve")
            return pe_merge, act_merge, dve_merge

        def pool_idle(k):
            def f(pool, ch):
                begin(pool, "pool", k)
                end(pool, "pool")
            return f

        attn_out = R2[:, :].rearrange("p (t h n) -> p t h n", t=NT, h=HQ)
        pe_ma, act_ma, dve_ma = merge(ma_u, lambda t: attn_out[:, t, :, :], 0, 4, False)

        def sp_ma(sp):
            for u in range(ma_u + 2, ma_u + 4):
                load_unit(sp, u)
            for u in range(gla_u, gla_u + 2):
                load_unit(sp, u)

        gkT = work(N_TOK, at=0)[0:33, :]
        wg = work(2 * GH * DK)[0:33, :].rearrange("p (r n) -> p r n", r=2)
        qkv = work(NT * BLK).rearrange("p (t n) -> p t n", t=NT)
        ex = work(6 * DK).rearrange("p (a s n) -> p a s n", a=3, s=2)
        dec = [work(4).rearrange("p (d c) -> p d c", d=2) for _ in range(4)]
        qkd = [work(6 * DK).rearrange("p (a s n) -> p a s n", a=3, s=2) for _ in range(2)]
        qkT = [work(4 * P).rearrange("p (d a n) -> p d a n", d=2, a=2) for _ in range(2)]
        Sst = [[work(DV) for _ in range(3)] for _ in range(2)]
        ogT = R2[:, :].rearrange("p (k t) -> p k t", k=KD)
        spare = Wslot[(gla_u + 1) % 2][:, :, DV:2 * DV]
        lg = [spare[:, s, :].rearrange("p (d n) -> p d n", d=2) for s in range(2)]
        glt = spare[:, 2, :]
        on = [spare[:, 3 + s, :] for s in range(2)]
        am = spare[:, 5, :]
        rs = [spare[:, 6 + s, :] for s in range(2)]
        gst = st[:, 52:64]

        F_ORD = list(range(T_CTX, NT)) + list(range(T_CTX))
        B_ORD = list(range(NT - 1, T_CTX - 1, -1)) + list(range(T_CTX - 1, -1, -1))
        pairs = list(zip(F_ORD, B_ORD))
        NI = len(pairs)
        STEPS = NI + 3
        def tiles_of(i):
            lo, hi = min(pairs[i]), max(pairs[i])
            return slice(lo, hi + 1, hi - lo)

        def slot_of(i, d_):
            return int(pairs[i][d_] > pairs[i][1 - d_])
        chunks_of = ((0, 1), (1, 0))
        qkv_fill = {(0, 0): 2, (0, 1): 9, (1, 0): 3, (1, 1): 8, (2, 0): 4, (2, 1): 7, (3, 0): 5, (3, 1): 6, (4, 0): 0, (5, 0): 1}
        qkv_order = [qkv_fill[g] for g in sorted(qkv_fill)]
        r_fill = {(6, 0): 6, (7, 0): 5, (8, 1): 7, (9, 0): 4, (9, 1): 8, (10, 0): 3, (10, 1): 9, (11, 0): 2, (12, 0): 0, (12, 1): 1}
        r_order = [r_fill[g] for g in sorted(r_fill)]
        done_by = {t: max(i for i in range(NI) if t in pairs[i]) for t in range(NT)}
        finished_in = {j: [n for n, t in enumerate(r_order) if min(done_by[t] + 4, STEPS - 1) == j] for j in range(STEPS)}
        assert sorted(qkv_order) == sorted(r_order) == list(range(NT))

        def raw_out(h):
            return R2[:, ds(h * (2 * N_TOK), 2 * N_TOK)].rearrange("p (a t n) -> p t a n", a=2, t=NT)

        def sp_gla(sp):
            begin(sp, "sp", 5)
            sp.wait_ge(S("gate_weights_cleared"), 1)
            sp.dma_start(wg[0:RANK, 0, :], w_gk2_f[0]).then_inc(S("gate_weights_landed"), 16)
            sp.dma_start(wg[RANK:2 * RANK, 1, :], w_gk2_b[0]).then_inc(S("gate_weights_landed"), 16)
            sp.dma_start(wg[32:33, 0, :], b_gk_f[0:1, :]).then_inc(S("gate_weights_landed"), 16)
            sp.dma_start(wg[32:33, 1, :], b_gk_b[0:1, :]).then_inc(S("gate_weights_landed"), 16)
            for h in range(GH):
                if h:
                    sp.wait_ge(S("head_done"), h)
                    sp.wait_ge(S("ctx_state_stored"), 32 * h)
                for d_, src in ((0, state_gla_fwd), (1, state_gla_bwd)):
                    sp.dma_start(Sst[d_][0], src[0, 0, h]).then_inc(S("state_landed"), 16)
                if h + 1 < GH:
                    for u in (gla_u + 2 * h + 2, gla_u + 2 * h + 3):
                        load_unit(sp, u)
                else:
                    load_unit(sp, mb_u)
                sp.wait_ge(S("ctx_state_final"), h + 1)
                for d_, dst in ((0, new_sf), (1, new_sb)):
                    sp.dma_start(dst[0, 0, h], Sst[d_][(2 * NI) % 3]).then_inc(S("ctx_state_stored"), 16)

        def pe_gla(pe):
            begin(pe, "pe", 5)
            for n, (c0, w) in enumerate(((0, 512), (512, 512), (1024, 256))):
                for k in range(KD):
                    m = pe.matmul(ps[0:32, n * BANK:n * BANK + w], w_lr[:, k, :], hT[:, k, c0:c0 + w], start=(k == 0), stop=(k == KD - 1))
                m.then_inc(S("low_rank_done"), 1)
            pe.wait_ge(S("low_rank_kept"), 3)
            pe.wait_ge(S("gate_weights_landed"), 64)
            with pe.Fori(0, GH) as h:

                def gate(i):
                    if i >= 1:
                        pe.wait_ge(S("log_gates"), h * NI + i)
                    pe.sem_inc(S("gate_turns"), 1)
                    for d_ in range(2):
                        t = pairs[i][d_]
                        m = pe.matmul(ps[:, d_ * DK:(d_ + 1) * DK], gkT[0:33, t * P:(t + 1) * P], wg[0:33, d_, ds(h * DK, DK)], start=True, stop=True)
                    m.then_inc(S("gate_logits"), 1)

                def sums(i):
                    pe.wait_ge(S("log_gates"), h * NI + (i + 1))
                    if i >= 1:
                        pe.wait_ge(S("exps_done"), h * NI + i)
                    for a in range(2):
                        for d_ in range(2):
                            o = BANK + (2 * a + slot_of(i, d_)) * DK
                            m = pe.matmul(ps[:, o:o + DK], masks[:, (2 * d_ + a) * P:(2 * d_ + a + 1) * P], lg[i % 2][:, d_, :], start=True, stop=True)
                    m.then_inc(S("gate_sums"), 1)

                def totals(i):
                    if i >= 3:
                        pe.wait_ge(S("intra_masked"), h * NI + (i - 2))
                    for d_ in range(2):
                        o = 3 * BANK + (2 + d_) * P
                        m = pe.matmul(ps[:, o:o + P], lg[i % 2][:, d_, :], masks[:, 3 * P + 2:4 * P + 2], start=True, stop=True)
                    m.then_inc(S("gate_totals"), 1)

                def intra(i):
                    pe.wait_ge(S("gated_turned_kept"), h * NI + (i + 1))
                    pe.wait_ge(S("exps_done"), h * NI + min(i + 2, NI))
                    if i >= 1:
                        pe.wait_ge(S("intra_masked"), h * NI + i)
                    for d_ in range(2):
                        o = 3 * BANK + d_ * P
                        m = pe.matmul(ps[:, o:o + P], qkT[i % 2][:, d_, 1, :], qkT[i % 2][:, d_, 0, :], start=True, stop=True)
                    m.then_inc(S("intra_done"), 1)

                def turn(i):
                    pe.wait_ge(S("qk_gated"), h * NI + (i + 1))
                    if i >= 1:
                        pe.wait_ge(S("gated_turned_kept"), h * NI + i)
                    for d_ in range(2):
                        for a in range(2):
                            o = 2 * BANK + (2 * d_ + a) * P
                            m = pe.transpose(ps[:, o:o + P], qkd[i % 2][:, a, slot_of(i, d_), :], ident[:, :])
                    m.then_inc(S("gated_turned"), 1)

                def out(i):
                    if i == 0:
                        pe.wait_ge(S("state_landed"), h * 32 + 32)
                    pe.wait_ge(S("intra_masked"), h * NI + (i + 1))
                    if i >= 1:
                        pe.wait_ge(S("out_kept"), h * NI + i)
                    pe.wait_ge(S("state_moved"), h * (2 * NI) + (2 * i + 1))
                    for d_ in range(2):
                        t = pairs[i][d_]
                        o = 6 * BANK + slot_of(i, d_) * DV
                        pe.matmul(ps[:, o:o + DV], am[:, d_ * P:(d_ + 1) * P], qkv[:, t, 2 * DK:2 * DK + DV], start=True, stop=False, skip_group_check=True)
                        for x in range(2):
                            rows = slice(chunks_of[d_][x] * CHUNK, (chunks_of[d_][x] + 1) * CHUNK)
                            m = pe.matmul(ps[rows, o:o + DV], qkT[i % 2][:, d_, 0, rows], Sst[d_][(2 * i + x) % 3], start=False, stop=(x == 1),
                                          skip_group_check=True)
                    m.then_inc(S("tile_out"), 1)

                def chunk_kv(i):
                    if i >= 1:
                        pe.wait_ge(S("state_moved"), h * (2 * NI) + 2 * i)
                    for x in range(2):
                        for d_ in range(2):
                            t, c_ = pairs[i][d_], chunks_of[d_][x]
                            rows = slice(c_ * CHUNK, (c_ + 1) * CHUNK)
                            o = (4 + c_) * BANK + d_ * DV
                            m = pe.matmul(ps[:, o:o + DV], qkd[i % 2][rows, 2, slot_of(i, d_), :], qkv[rows, t, 2 * DK:2 * DK + DV], start=True, stop=True)
                            if x == 1:
                                m.then_inc(S(f"chunk_kv{c_}"), 1)

                def turn_out(m_):
                    pe.wait_ge(S("gated_out"), h * NT + (m_ + 1))
                    if m_ >= 1:
                        pe.wait_ge(S("gated_out_kept"), h * NT + m_)
                    for a in range(2):
                        o = 7 * BANK + (2 + a) * P
                        m = pe.transpose(ps[:, o:o + P], on[m_ % 2][:, a * P:(a + 1) * P], ident[:, :])
                    m.then_inc(S("gated_out_turned"), 1)

                def project(j, gap):
                    if (j, gap) in qkv_fill:
                        t = qkv_fill[j, gap]
                        n = qkv_order.index(t)
                        if n == 0:
                            pe.wait_ge(w_full[gla_u % 2], h * 48 + w_ready[gla_u])
                        else:
                            pe.wait_ge(S("qkv_kept"), h * NT + n)
                        gemm(pe, bank(7), lambda q: hT[:, q, t * P:(t + 1) * P], gla_u % 2).then_inc(S("qkv_done"), 1)
                        if n == NT - 1:
                            pe.wait_ge(S("qkv_done"), h * NT + NT)
                            pe.sem_inc(w_free[gla_u % 2], 1)
                    if (j, gap) in r_fill:
                        t = r_fill[j, gap]
                        n = r_order.index(t)
                        if n == 0:
                            pe.wait_ge(w_full[(gla_u + 1) % 2], h * 16 + w_ready[gla_u + 1])
                            pe.wait_ge(S("qkv_kept"), h * NT + NT)
                        else:
                            pe.wait_ge(S("r_used"), h * NT + n)
                        if n >= 2:
                            turn_out(n - 2)
                        gemm(pe, bank(7, DV), lambda q: hT[:, q, t * P:(t + 1) * P], (gla_u + 1) % 2, DV).then_inc(S("r_done"), 1)
                        if n == NT - 1:
                            pe.wait_ge(S("r_done"), h * NT + NT)
                            pe.sem_inc(w_free[(gla_u + 1) % 2], 1)

                for j in range(STEPS):
                    if j < NI:
                        gate(j)
                    if 0 <= j - 1 < NI:
                        sums(j - 1)
                        totals(j - 1)
                    if 0 <= j - 3 < NI:
                        intra(j - 3)
                    project(j, 0)
                    if 0 <= j - 2 < NI:
                        turn(j - 2)
                    if 0 <= j - 3 < NI:
                        out(j - 3)
                    project(j, 1)
                    if 0 <= j - 2 < NI:
                        chunk_kv(j - 2)
                turn_out(NT - 2)
                turn_out(NT - 1)
                pe.wait_ge(S("gated_out_kept"), h * NT + NT)
            end(pe, "pe")

        def act_gla(act, ch):
            begin(act, "act", 5)
            for n, (c0, w) in enumerate(((0, 512), (512, 512), (1024, 256))):
                act.wait_ge(S("low_rank_done"), n + 1)
                act.activation(gkT[0:32, c0:c0 + w], ps[0:32, n * BANK:n * BANK + w], ACT.Copy).then_inc(S("low_rank_kept"), 1)
            act.preload_act_table_set("natural_log_exp_and_others")
            with act.Fori(0, GH) as h:
                ch.enter(h, ACT_PER)

                def logs(i):
                    act.wait_ge(S("gate_logits"), h * NI + (i + 1))
                    if i >= 1:
                        act.wait_ge(S("log_gates"), h * NI + i)
                    ch(act.activation(glt, bank(0, 2 * DK), ACT.Abs))
                    ch(act.activation(glt, glt, ACT.Exp, scale=-1.0))
                    act.activation(glt, glt, ACT.Ln, bias=1.0).then_inc(S("softplus_done"), 1)
                    act.wait_ge(S("softplus_done"), h * NI + (i + 1))

                def exps(i):
                    act.wait_ge(S("gate_sums"), h * NI + (i + 1))
                    if i >= 1:
                        act.wait_ge(S("qk_gated"), h * NI + i)
                    if i >= 4:
                        act.wait_ge(S("state_moved"), h * (2 * NI) + 2 * (i - 3))
                    ch(act.activation(ex[:, 0:3:2, :, :], bank(1).rearrange("p (a s n) -> p a s n", a=2, s=2), ACT.Exp, scale=1.0 / GATE_NORM))
                    ch(act.activation(ex[:, 1, :, :], bank(1, 2 * DK).rearrange("p (s n) -> p s n", s=2), ACT.Exp, scale=-1.0 / GATE_NORM))
                    act.wait_ge(S("gate_totals"), h * NI + (i + 1))
                    if i >= 2:
                        act.wait_ge(S("intra_masked"), h * NI + (i - 1))
                    src = ps[:, 3 * BANK + 2 * P:4 * BANK].rearrange("p (d n) -> p d n", d=2)[:, :, P - 2:P]
                    act.activation(dec[i % 4], src, ACT.Exp, scale=1.0 / GATE_NORM).then_inc(S("exps_done"), 1)
                    act.wait_ge(S("exps_done"), h * NI + (i + 1))

                def keep_turned(i):
                    act.wait_ge(S("gated_turned"), h * NI + (i + 1))
                    if i >= 2:
                        act.wait_ge(S("tile_out"), h * NI + (i - 1))
                    act.activation(qkT[i % 2], bank(2).rearrange("p (d a n) -> p d a n", d=2, a=2), ACT.Copy).then_inc(S("gated_turned_kept"), 1)
                    act.wait_ge(S("gated_turned_kept"), h * NI + (i + 1))

                def projected(j, gap):
                    if (j, gap) in qkv_fill:
                        t = qkv_fill[j, gap]
                        n = qkv_order.index(t)
                        act.wait_ge(S("qkv_done"), h * NT + (n + 1))
                        ch(act.activation(qkv[:, t, 0:DK], bank(7, DK), ACT.Copy, scale=GSCALE))
                        act.activation(qkv[:, t, DK:BLK], ps[:, 7 * BANK + DK:8 * BANK], ACT.Copy).then_inc(S("qkv_kept"), 1)

                def gates_of(j, gap):
                    if (j, gap) in r_fill:
                        n = r_order.index(r_fill[j, gap])
                        act.wait_ge(S("r_done"), h * NT + (n + 1))
                        if n >= 2:
                            act.wait_ge(S("gated_out"), h * NT + (n - 1))
                        ch(act.activation(rs[n % 2], bank(7, DV), ACT.Exp, scale=-1.0))
                        ch(act.activation(rs[n % 2], rs[n % 2], ACT.Ln, bias=1.0))
                        act.activation(rs[n % 2], rs[n % 2], ACT.Exp, scale=-1.0).then_inc(S("r_gated"), 1)

                def square(n):
                    t = r_order[n]
                    act.wait_ge(S("out_kept"), h * NI + (done_by[t] + 1))
                    if n >= 2:
                        act.wait_ge(S("gated_out_turned"), h * NT + (n - 1))
                    act.activation(on[n % 2].rearrange("p (a n) -> p a n", a=2), raw_out(h)[:, t, :, :], ACT.Square,
                                   accum_out=gst[:, n % 2:n % 2 + 1]).then_inc(S("out_squared"), 1)

                for j in range(STEPS):
                    if j < NI:
                        logs(j)
                    if j < STEPS - 1:
                        for n in finished_in[j]:
                            square(n)
                    if 0 <= j - 1 < NI:
                        exps(j - 1)
                    projected(j, 0)
                    gates_of(j, 0)
                    if 0 <= j - 2 < NI:
                        keep_turned(j - 2)
                    projected(j, 1)
                    gates_of(j, 1)
                for n in finished_in[STEPS - 1]:
                    square(n)
                act.wait_ge(S("gated_out_kept"), h * NT + NT)
                ch.leave(GH)
            end(act, "act")

        ACT_PER = 4 * NI + 3 * NT

        def pool_gla(pool, ch):
            begin(pool, "pool", 5)
            ch(pool.memset(gkT[32:33, :], 1.0))
            pool.memset(wg[:, :, :], 0.0).then_inc(S("gate_weights_cleared"), 1)
            with pool.Fori(0, GH) as h:
                ch.enter(h, NT)
                for n in range(NT):
                    pool.wait_ge(S("out_squared"), h * NT + (n + 1))
                    c = n % 2
                    if n >= 2:
                        pool.wait_ge(S("gated_out"), h * NT + (n - 1))
                    pool.sem_inc(S("pool_turns"), 1)
                    ch(pool.tensor_scalar(gst[:, 2 + c:3 + c], gst[:, c:c + 1], 1.0 / DV, EPS, ALU.mult, ALU.add))
                    pool.tensor_tensor(gst[:, 4 + c:5 + c], gst[:, 2 + c:3 + c], mhalf[:, 0:1], ALU.pow).then_inc(S("out_rstd"), 1)
                ch.leave(GH)
            pool.wait_ge(S("ctx_state_stored"), 32 * GH)
            end(pool, "pool")

        def dve_gla(dve, ch):
            begin(dve, "dve", 5)
            ch(dve.memset(am, 0.0))
            with dve.Fori(0, GH) as h:
                ch.enter(h, DVE_PER)

                def loggate(i):
                    dve.wait_ge(S("softplus_done"), h * NI + (i + 1))
                    if i >= 2:
                        dve.wait_ge(S("gate_totals"), h * NI + (i - 1))
                    dve.scalar_tensor_tensor(lg[i % 2], bank(0, 2 * DK).rearrange("p (d n) -> p d n", d=2), 0.0,
                                             glt.rearrange("p (d n) -> p d n", d=2), ALU.min, ALU.subtract).then_inc(S("log_gates"), 1)

                def gated(i):
                    dve.wait_ge(S("exps_done"), h * NI + (i + 1))
                    last = max(qkv_order.index(t) for t in pairs[i])
                    dve.wait_ge(S("qkv_kept"), h * NT + (last + 1))
                    if i >= 2:
                        dve.wait_ge(S("chunk_kv0"), h * NI + (i - 1))
                        dve.wait_ge(S("chunk_kv1"), h * NI + (i - 1))
                    src = qkv[:, tiles_of(i), :]
                    o = qkd[i % 2]
                    ch(dve.tensor_tensor(o[:, 0:2, :, :].rearrange("p a s n -> p s a n"), src[:, :, 0:2 * DK].rearrange("p s (a n) -> p s a n", a=2),
                                         ex[:, 0:2, :, :].rearrange("p a s n -> p s a n"), ALU.mult))
                    dve.tensor_tensor(o[:, 2, :, :], src[:, :, DK:2 * DK], ex[:, 2, :, :], ALU.mult).then_inc(S("qk_gated"), 1)

                def masked(i):
                    dve.wait_ge(S("intra_done"), h * NI + (i + 1))
                    if i >= 1:
                        dve.wait_ge(S("tile_out"), h * NI + i)
                    dve.sem_inc(S("mask_turns"), 1)
                    dve.copy_predicated(am, keep[:, :], bank(3, 2 * P)).then_inc(S("intra_masked"), 1)

                def states(i):
                    if i == 0:
                        dve.wait_ge(S("state_landed"), h * 32 + 32)
                    else:
                        dve.wait_ge(S("tile_out"), h * NI + i)
                    dve.wait_ge(S("chunk_kv0"), h * NI + (i + 1))
                    dve.wait_ge(S("chunk_kv1"), h * NI + (i + 1))
                    for x in range(2):
                        if i + x >= 1:
                            dve.wait_ge(S("state_moved"), h * (2 * NI) + (2 * i + x))
                        for d_ in range(2):
                            s_, c_ = 2 * i + x, chunks_of[d_][x]
                            if i == T_LAT - 1 and x == 1:
                                m = dve.memset(Sst[d_][(s_ + 1) % 3], 0.0)
                            else:
                                m = dve.scalar_tensor_tensor(Sst[d_][(s_ + 1) % 3], Sst[d_][s_ % 3], dec[i % 4][:, d_, c_:c_ + 1],
                                                             ps[:, (4 + c_) * BANK + d_ * DV:(4 + c_) * BANK + (d_ + 1) * DV], ALU.mult, ALU.add)
                            if d_ == 0:
                                ch(m)
                        m.then_inc(S("state_moved"), 1)
                    if i == NI - 1:
                        dve.wait_ge(S("state_moved"), h * (2 * NI) + 2 * NI)
                        dve.sem_inc(S("ctx_state_final"), 1)

                def keep_out(i):
                    dve.wait_ge(S("tile_out"), h * NI + (i + 1))
                    dst = raw_out(h)[:, tiles_of(i), :, :]
                    src = bank(6).rearrange("p (s a n) -> p s a n", s=2, a=2)
                    if done_by[pairs[i][0]] == i:
                        dve.wait_ge(S("out_kept"), h * NI + i)
                        m = dve.tensor_tensor(dst, dst, src, ALU.add)
                    else:
                        m = dve.tensor_copy(dst, src)
                    m.then_inc(S("out_kept"), 1)

                def swish(n):
                    dve.wait_ge(S("r_gated"), h * NT + (n + 1))
                    dve.tensor_tensor(rs[n % 2], rs[n % 2], bank(7, DV), ALU.mult).then_inc(S("r_used"), 1)

                def finish(n):
                    t = r_order[n]
                    dve.wait_ge(S("out_rstd"), h * NT + (n + 1))
                    dve.wait_ge(S("r_used"), h * NT + (n + 1))
                    c = n % 2
                    dve.scalar_tensor_tensor(on[c].rearrange("p (a n) -> p a n", a=2), raw_out(h)[:, t, :, :], gst[:, 4 + c:5 + c],
                                             rs[c].rearrange("p (a n) -> p a n", a=2), ALU.mult, ALU.mult).then_inc(S("gated_out"), 1)

                def keep_finished(n):
                    t = r_order[n]
                    dve.wait_ge(S("gated_out_turned"), h * NT + (n + 1))
                    if n + 2 < NT:
                        dve.wait_ge(S("r_used"), h * NT + (n + 3))
                    for a in range(2):
                        o = h * (2 * N_TOK) + (a * N_TOK + t * P)
                        m = dve.tensor_scalar(R2[:, ds(o, P)], ps[:, 7 * BANK + (2 + a) * P:7 * BANK + (3 + a) * P], ggT[:, a:a + 1], None, ALU.mult)
                        if a == 0:
                            ch(m)
                    m.then_inc(S("gated_out_kept"), 1)

                gate_step = [j + gap for j, gap in sorted(r_fill)]
                early = {j + 1: r_order.index(t) for (j, gap), t in r_fill.items() if gap == 1}

                def gates_of(j, gap):
                    if (j, gap) in r_fill:
                        n = r_order.index(r_fill[j, gap])
                        swish(n)
                        if n >= 2:
                            keep_finished(n - 2)
                        if gap == 0 and j < STEPS - 1 and n in finished_in[j]:
                            finish(n)

                for j in range(STEPS):
                    if 0 <= j - 3 < NI:
                        masked(j - 3)
                    if j < NI:
                        loggate(j)
                    if 0 <= j - 1 < NI:
                        gated(j - 1)
                    if j < STEPS - 1:
                        for n in finished_in[j]:
                            if gate_step[n] < j or n == early.get(j):
                                finish(n)
                    gates_of(j, 0)
                    if 0 <= j - 3 < NI:
                        keep_out(j - 3)
                    gates_of(j, 1)
                    if 0 <= j - 2 < NI:
                        states(j - 2)
                for n in finished_in[STEPS - 1]:
                    finish(n)
                keep_finished(NT - 2)
                keep_finished(NT - 1)
                dve.wait_ge(S("gated_out_kept"), h * NT + NT)
                ch.leave(GH)
                dve.sem_inc(S("head_done"), 1)
            end(dve, "dve")

        DVE_PER = NI + 2 * NI + NT

        pe_mb, act_mb, dve_mb = merge(mb_u, lambda t: ogT[:, :, t * P:(t + 1) * P], 1, 6, True)

        def sp_mb(sp):
            for u in (mb_u + 1, mb_u + 2, mb_u + 3, out_u, out_u + 1):
                if slot[u] == sig_slot:
                    sp.wait_ge(S("tiles_merged"), 4 * NT)
                load_unit(sp, u)

        mixT = R1[:, :].rearrange("p (k t) -> p k t", k=KD)
        G1b = [work(D, at=0)] + [work(D)]
        xr = [work(D) for _ in range(2)]
        x1b = [work(D) for _ in range(2)]
        xh = [work(D) for _ in range(2)]
        sqo = work(D)
        h2T = [work(D).rearrange("p (k t) -> p k t", k=KD) for _ in range(2)]
        colb = R2[:, N_TOK:N_TOK + BLK].rearrange("p (k n) -> p k n", k=4)
        aff = R2[:, N_TOK + BLK:N_TOK + BLK + 2 * NE].rearrange("p (a n) -> p a n", a=2)
        G2b = [RW[:, j * D:(j + 1) * D] for j in range(2)]
        so = st[:, 0:24]

        def pe_bcast(pe, n, b):
            pe.wait_ge(S("columns_spread"), n + 1)
            if n >= 1:
                pe.wait_ge(S("rows_kept"), n)
            for k in range(4):
                m = pe.matmul(ps[:, b * BANK + k * P:b * BANK + (k + 1) * P], colb[:, k, :], ident[:, :], start=True, stop=True)
            m.then_inc(S("rows_spread"), 1)

        def kind_part(n):
            return (n % 4) // 2, 4 * (n % 2)

        def sp_out(sp):
            begin(sp, "sp", 7)
            for t in range(NT):
                if t >= 2:
                    sp.wait_ge(S("x1_made"), t - 1)
                sp.dma_start(xr[t % 2], x_rows(t)).then_inc(S(f"rows_landed{3 + t % 2}"), 16)
                if t >= 1:
                    store_out(sp, t - 1)
                if t == 1:
                    sp.wait_ge(S("zero_made"), 1)
                    for r in range(NT):
                        sp.dma_start(ffn_dram[r * P:(r + 1) * P, :], zero).then_inc(S("ffn_cleared"), 16)
            store_out(sp, NT - 1)

        def store_out(sp, t):
            sp.wait_ge(S("xhat_made"), t + 1)
            sp.dma_start(x1_dram[t * P:(t + 1) * P, :], x1b[t % 2]).then_inc(S(f"x1_stored{t % 2}"), 16)
            sp.dma_start(xhat_dram[t * P:(t + 1) * P, :], xh[t % 2]).then_inc(S(f"x1_stored{t % 2}"), 16)

        def pe_out(pe):
            begin(pe, "pe", 7)
            for t in range(NT):
                if t >= 2:
                    pe.wait_ge(S("mixT_act"), t - 1)
                    pe.wait_ge(S("mixT_dve"), t - 1)
                for k in range(KD):
                    o = (2 * (t % 2)) * BANK + k * P
                    m = pe.transpose(ps[:, o:o + P], mix[:, t, k * P:(k + 1) * P], ident[:, :])
                m.then_inc(S("mix_turned"), 1)
                if t % 2 == 1 and t < 8:
                    pe_bcast(pe, t // 2, 6)
            for s in range(2):
                pe.wait_ge(w_full[(out_u + s) % 2], w_ready[out_u + s])
            pe.wait_ge(S("mixT_act"), NT)
            pe.wait_ge(S("mixT_dve"), NT)

            def project(t, cb):
                b = 2 * (t % 2) + cb
                if t >= 2 and cb == 0:
                    pe.wait_ge(S("out_banks_free"), t - 1)
                gemm(pe, bank(b), lambda q: mixT[:, q, t * P:(t + 1) * P], (out_u + cb) % 2).then_inc(S("out_done"), 1)
                if t == NT - 1:
                    pe.wait_ge(S("out_done"), 2 * t + cb + 1)
                    pe.sem_inc(w_free[(out_u + cb) % 2], 1)

            def turn(t):
                pe.wait_ge(S("xhat_made"), t + 1)
                if t >= 1:
                    pe.wait_ge(S("h2_kept_act"), t)
                    pe.wait_ge(S("h2_kept_dve"), t)
                for k in range(KD):
                    m = pe.transpose(ps[:, 4 * BANK + k * P:4 * BANK + (k + 1) * P], xh[t % 2][:, k * P:(k + 1) * P], ident[:, :])
                m.then_inc(S("xhat_turned"), 1)

            def route(t):
                pe.wait_ge(S("h2_kept_act"), t + 1)
                pe.wait_ge(S("h2_kept_dve"), t + 1)
                if t >= 1:
                    pe.wait_ge(S("aff_made"), t)
                for k in range(KD):
                    m = pe.matmul(bank(6, P), h2T[t % 2][:, k, :], wr[:, k * NE:k * NE + P], start=(k == 0), stop=(k == KD - 1))
                m.then_inc(S("routed"), 1)

            def turn_aff(t):
                pe.wait_ge(S("aff_made"), t + 1)
                if t >= 1:
                    pe.wait_ge(S("aff_kept"), t)
                pe.transpose(ps[0:NE, 7 * BANK:7 * BANK + P], aff[:, t % 2, :], ident[:, :]).then_inc(S("aff_turned"), 1)

            for t in range(NT + 3):
                if t < NT:
                    project(t, 0)
                if 0 <= t - 2 < NT:
                    route(t - 2)
                if 0 <= t - 3 < NT:
                    turn_aff(t - 3)
                if t < NT:
                    project(t, 1)
                if 0 <= t - 1 < NT:
                    turn(t - 1)
            end(pe, "pe")

        def act_out(act, ch):
            begin(act, "act", 7)
            for t in range(NT):
                act.wait_ge(S("mix_turned"), t + 1)
                b = 2 * (t % 2)
                act.activation(mixT[:, 0:4, t * P:(t + 1) * P], bank(b).rearrange("p (k t) -> p k t", k=4), ACT.Copy).then_inc(S("mixT_act"), 1)
                act.wait_ge(S("mixT_act"), t + 1)

            def square_mix(t):
                act.wait_ge(S("out_done"), 2 * t + 2)
                for cb in range(2):
                    ch(act.activation(sqo[:, cb * BLK:(cb + 1) * BLK], bank(2 * (t % 2) + cb), ACT.Square, accum_out=so[:, cb:cb + 1]))
                act.sem_inc(S("mix_squared"), 1)

            def square_x1(t):
                act.wait_ge(S("x1_made"), t + 1)
                act.activation(sqo[:, :], x1b[t % 2], ACT.Square, accum_out=so[:, 2:3]).then_inc(S("x1_squared"), 1)
                act.wait_ge(S("x1_squared"), t + 1)

            def keep_h2(t):
                j = kind_of(t)
                act.wait_ge(S("xhat_turned"), t + 1)
                if t >= 2:
                    act.wait_ge(S("routed"), t - 1)
                for k in range(4):
                    ch(act.activation(h2T[t % 2][:, k, :], ps[:, 4 * BANK + k * P:4 * BANK + (k + 1) * P], ACT.Identity,
                                      scale=A2[:, k, j:j + 1], bias=modT[:, 24 + k, j:j + 1]))
                act.sem_inc(S("h2_kept_act"), 1)

            def soft(t):
                act.wait_ge(S("router_max"), t + 1)
                act.activation(aff[:, t % 2, :], bank(6, NE), ACT.Exp, bias=so[:, 8:9], accum_out=so[:, 9:10]).then_inc(S("router_exp"), 1)
                act.wait_ge(S("router_exp"), t + 1)

            def keep_aff(t):
                act.wait_ge(S("aff_turned"), t + 1)
                act.activation(affT[:, t * P:(t + 1) * P], ps[0:NE, 7 * BANK:7 * BANK + P], ACT.Copy).then_inc(S("aff_kept"), 1)
                act.wait_ge(S("aff_kept"), t + 1)

            for t in range(NT + 3):
                if 0 <= t - 2 < NT:
                    soft(t - 2)
                if 0 <= t - 3 < NT:
                    keep_aff(t - 3)
                if t < NT:
                    square_mix(t)
                if 0 <= t - 1 < NT:
                    keep_h2(t - 1)
                if t < NT:
                    square_x1(t)
            end(act, "act")

        def pool_out(pool, ch):
            begin(pool, "pool", 7)
            pool.memset(zero, 0.0).then_inc(S("zero_made"), 1)
            for n in range(2 * NT):
                pool.wait_ge(S("out_vars"), n + 1)
                o = 4 + n % 2
                pool.tensor_tensor(so[:, o + 2:o + 3], so[:, o:o + 1], mhalf[:, 0:1], ALU.pow).then_inc(S("out_rstds"), 1)
            end(pool, "pool")

        def dve_out(dve, ch):
            begin(dve, "dve", 7)

            def spread(n):
                j, k = kind_part(n)
                dve.tensor_copy(colb, G1[:, k:k + 4, j:j + 1].broadcast_to([P, 4, P])).then_inc(S("columns_spread"), 1)
            spread(0)
            for t in range(NT):
                dve.wait_ge(S("mix_turned"), t + 1)
                b = 2 * (t % 2) + 1
                dve.tensor_copy(mixT[:, 4:8, t * P:(t + 1) * P], bank(b).rearrange("p (k t) -> p k t", k=4)).then_inc(S("mixT_dve"), 1)
                dve.wait_ge(S("mixT_dve"), t + 1)
                if t % 2 == 1 and t < 8:
                    n = t // 2
                    j, k = kind_part(n)
                    dve.wait_ge(S("rows_spread"), n + 1)
                    dve.tensor_copy(G1b[j][:, k * P:(k + 4) * P], bank(6)).then_inc(S("rows_kept"), 1)
                    dve.wait_ge(S("rows_kept"), n + 1)
                    if n + 1 < 4:
                        spread(n + 1)

            def residual(t):
                j = kind_of(t)
                dve.wait_ge(S("mix_squared"), t + 1)
                ch(dve.tensor_tensor(so[:, 3:4], so[:, 0:1], so[:, 1:2], ALU.add))
                ch(dve.tensor_scalar(so[:, 4:5], so[:, 3:4], 1.0 / D, EPS, ALU.mult, ALU.add))
                dve.sem_inc(S("out_vars"), 1)
                dve.wait_ge(S("out_rstds"), 2 * t + 1)
                if t >= 2:
                    dve.wait_ge(S(f"x1_stored{t % 2}"), 32 * (t // 2))
                for cb in range(2):
                    ch(dve.scalar_tensor_tensor(x1b[t % 2][:, cb * BLK:(cb + 1) * BLK], bank(2 * (t % 2) + cb), so[:, 6:7],
                                                G1b[j][:, cb * BLK:(cb + 1) * BLK], ALU.mult, ALU.mult))
                dve.sem_inc(S("out_banks_free"), 1)
                dve.wait_ge(S(f"rows_landed{3 + t % 2}"), 16 * (t // 2 + 1))
                dve.tensor_tensor(x1b[t % 2], x1b[t % 2], xr[t % 2], ALU.add).then_inc(S("x1_made"), 1)
                dve.wait_ge(S("x1_made"), t + 1)

            def normal(t):
                dve.wait_ge(S("x1_squared"), t + 1)
                ch(dve.tensor_scalar(so[:, 5:6], so[:, 2:3], 1.0 / D, EPS, ALU.mult, ALU.add))
                dve.sem_inc(S("out_vars"), 1)
                dve.wait_ge(S("out_rstds"), 2 * t + 2)
                if t >= 2:
                    dve.wait_ge(S("xhat_turned"), t - 1)
                dve.tensor_scalar(xh[t % 2], x1b[t % 2], so[:, 7:8], None, ALU.mult).then_inc(S("xhat_made"), 1)
                dve.wait_ge(S("xhat_made"), t + 1)

            def keep_h2(t):
                j = kind_of(t)
                dve.wait_ge(S("xhat_turned"), t + 1)
                if t >= 2:
                    dve.wait_ge(S("routed"), t - 1)
                for k in range(4, 8):
                    ch(dve.tensor_scalar(h2T[t % 2][:, k, :], ps[:, 4 * BANK + k * P:4 * BANK + (k + 1) * P],
                                         A2[:, k, j:j + 1], modT[:, 24 + k, j:j + 1], ALU.mult, ALU.add))
                dve.sem_inc(S("h2_kept_dve"), 1)

            def soft(t):
                dve.wait_ge(S("routed"), t + 1)
                ch(dve.tensor_reduce(so[:, 10:11], bank(6, NE), AX, ALU.max))
                if t >= 2:
                    dve.wait_ge(S("aff_turned"), t - 1)
                dve.tensor_scalar(so[:, 8:9], so[:, 10:11], -1.0, None, ALU.mult).then_inc(S("router_max"), 1)
                dve.wait_ge(S("router_exp"), t + 1)
                ch(dve.reciprocal(so[:, 11:12], so[:, 9:10]))
                ch(dve.tensor_scalar(aff[:, t % 2, :], aff[:, t % 2, :], so[:, 11:12], None, ALU.mult))
                dve.sem_inc(S("aff_made"), 1)

            for t in range(NT + 2):
                if 0 <= t - 2 < NT:
                    soft(t - 2)
                if 0 <= t - 1 < NT:
                    keep_h2(t - 1)
                if t < NT:
                    residual(t)
                    normal(t)
                if t == T_CTX + 3:
                    dve.wait_ge(S("aff_kept"), T_CTX)
                    best(dve, ch, 0)
            end(dve, "dve")

        o_ = 8 * D
        affw = R3[0:NE, o_:o_ + N_TOK]
        topv, topi, topf = (R3[0:NE, o_ + N_TOK + n * CAP:o_ + N_TOK + (n + 1) * CAP] for n in range(3))
        topi = topi.bitcast(U32)
        val = [st[:, 24:40], st[:, 40:56]]
        idxu = [WK[0:CAP_CTX, 0:NE].bitcast(U32), WK[0:CAP_LAT, NE:2 * NE].bitcast(U32)]
        zero = work(D, at=11 * D)
        grow = R1[0:2, 8 * D:9 * D]
        kinds = ((0, 0, N_CTX, 0, CAP_CTX), (1, N_CTX, N_TOK, CAP_CTX, CAP_LAT))

        def best(dve, ch, kind):
            _, lo, hi, at, cap = kinds[kind]
            cur = affT[:, lo:hi]
            for r in range(cap // 8):
                v = topv[:, at + 8 * r:at + 8 * r + 8]
                ch(dve.max(v, cur))
                ch(dve.max_index(topi[:, at + 8 * r:at + 8 * r + 8], v, cur))
                if r + 1 < cap // 8:
                    ch(dve.match_replace(affw[:, lo:hi], v, cur, -1.0))
                    cur = affw[:, lo:hi]

        def dve_topk(dve, ch):
            begin(dve, "dve", 8)
            best(dve, ch, 1)
            ch(dve.tensor_copy(topf, topi[:, :]))
            ch(dve.tensor_scalar(topf[:, CAP_CTX:CAP], topf[:, CAP_CTX:CAP], float(N_CTX), None, ALU.add))
            dve.sem_inc(S("chosen"), 1)
            dve.wait_ge(S("chosen_turned"), 1)
            for kind, lo, hi, at, cap in kinds:
                ch(dve.tensor_copy(val[kind][0:cap, :], ps[0:cap, 2 * kind * BANK:2 * kind * BANK + NE]))
                ch(dve.tensor_copy(idxu[kind][:, :], ps[0:cap, (2 * kind + 1) * BANK:(2 * kind + 1) * BANK + NE]))
            end(dve, "dve")

        def pe_topk(pe):
            begin(pe, "pe", 8)
            for n in range(2):
                s_ = (g2_u + n) % 2
                pe.wait_ge(w_full[s_], w_ready[g2_u + n])
                for k in range(KD):
                    m = pe.matmul(bank(4 + n, BLK, 2), cS[:, k, :], Wslot[s_][:, k, :], start=(k == 0), stop=(k == KD - 1))
                m.then_inc(S("mod_row"), 1)
            pe.wait_ge(S("gates_moved"), 4 + 2)
            for k in range(KD):
                m = pe.transpose(ps[:, 7 * BANK + 2 * k:7 * BANK + 2 * k + 2], grow[:, k * P:(k + 1) * P], ident[0:2, 0:2])
            m.then_inc(S("mod_columns"), 1)
            for n in range(4, 8):
                pe_bcast(pe, n, 6)
            pe.wait_ge(S("chosen"), 1)
            for kind, lo, hi, at, cap in kinds:
                for a, src in enumerate((topv, topf)):
                    b = 2 * kind + a
                    m = pe.transpose(ps[0:cap, b * BANK:b * BANK + NE], src[:, at:at + cap], ident[0:NE, 0:NE])
            m.then_inc(S("chosen_turned"), 1)
            end(pe, "pe")

        def act_topk(act, ch):
            begin(act, "act", 8)
            act.wait_ge(S("zero_made"), 1)
            for n in range(2):
                act.wait_ge(S("mod_row"), NU + n + 1)
                act.activation(grow[:, n * BLK:(n + 1) * BLK], bank(4 + n, BLK, 2), ACT.Copy).then_inc(S("gates_moved"), 1)
            act.wait_ge(S("mod_columns"), 3)
            for k in range(KD):
                ch(act.activation(G2[:, k, :], ps[:, 7 * BANK + 2 * k:7 * BANK + 2 * k + 2], ACT.Identity, scale=gv[:, 3, k:k + 1], bias=bg[:, k:k + 1]))
            for n in range(4, 8):
                j, k = kind_part(n)
                for q in range(4):
                    m = act.activation(colb[:, q, :], zero[:, 0:P], ACT.Identity, bias=G2[:, k + q, j:j + 1])
                    if q < 3:
                        ch(m)
                m.then_inc(S("columns_spread"), 1)
                act.wait_ge(S("rows_spread"), n + 1)
                act.activation(G2b[j][:, k * P:(k + 4) * P], bank(6), ACT.Copy).then_inc(S("rows_kept"), 1)
                act.wait_ge(S("rows_kept"), n + 1)
            end(act, "act")

        def sp_topk(sp):
            begin(sp, "sp", 8)
            for u in (g2_u, g2_u + 1):
                load_unit(sp, u)
            for n in range(3):
                for half in range(2):
                    load_expert(sp, 0, n, half)

        We = [R1[:, 0:8 * D], R2[:, 2 * D:10 * D], R3[:, 0:8 * D]]
        We = [w.rearrange("p (k n) -> p k n", k=KD) for w in We]
        xg = [work(D, at=64), work(D)]
        xe = work(KD * CAP).rearrange("p (k c) -> p k c", k=KD)
        sl = [work(CAP) for _ in range(2)]
        hid = work(KD * CAP).rearrange("p (k c) -> p k c", k=KD)
        yT = work(KD * CAP).rearrange("p (k c) -> p k c", k=KD)
        yo = [work(D), work(D)]
        ist_g = [WK[0:CAP_CTX, 2 * NE:2 * NE + 1].bitcast(U32), WK[0:CAP_LAT, 2 * NE + 1:2 * NE + 2].bitcast(U32)]
        ist_a = [WK[0:CAP_CTX, 2 * NE + 2:2 * NE + 3].bitcast(U32), WK[0:CAP_LAT, 2 * NE + 3:2 * NE + 4].bitcast(U32)]
        vst = [st[:, 56:57], st[:, 57:58]]
        COL = (CAP_LAT, 0)
        CAPS = (CAP_CTX, CAP_LAT)
        x1r = R1[:, :].rearrange("p (t d) -> p t d", t=NT)
        we_dram = (w1[0], w3[0], w2[0])

        def load_expert(sp, e, n, half):
            src = we_dram[n][e] if isinstance(e, int) else we_dram[n][ds(e, 1)].rearrange("a k n -> (a k) n")
            cols = slice(half * BLK, (half + 1) * BLK)
            sp.dma_start(We[n][:, :, cols], src[:, cols].rearrange("(k p) n -> p k n", p=P)).then_inc(S(f"expert_landed{n}{half}"), 16)

        def sp_moe(sp):
            with sp.Fori(1, NE) as e:
                for half in range(2):
                    sp.wait_ge(S("up_done0"), e * KD - (4 - 4 * half))
                    sp.wait_ge(S("up_done1"), e * KD - (4 - 4 * half))
                    load_expert(sp, e, 0, half)
                    load_expert(sp, e, 1, half)
                for half in range(2):
                    sp.wait_ge(S("down_done"), e * KD - (4 - 4 * half))
                    load_expert(sp, e, 2, half)
            sp.wait_ge(S("up_done0"), KD * NE)
            sp.wait_ge(S("up_done1"), KD * NE)
            sp.dma_start(x1r[:, :, :], x1_dram.rearrange("(t p) d -> p t d", p=P)).then_inc(S("x1_back"), 16)

        def pool_moe(pool, ch):
            begin(pool, "pool", 9)

            def gather(e):
                for kind in range(2):
                    ch(pool.tensor_copy(ist_g[kind][:, :], idxu[kind][:, ds(e, 1)]))
                pool.sem_inc(S("pool_turns"), 1)
                for kind in (1, 0):
                    pool.indirect_dma_start(xg[kind][0:CAPS[kind], :], None, xhat_dram,
                                            bass.IndirectOffsetOnAxis(ap=ist_g[kind][:, 0:1], axis=0)).then_inc(S("rows_gathered"), 16)

            def add_back(e):
                for kind in range(2):
                    ch(pool.tensor_copy(ist_a[kind][:, :], idxu[kind][:, ds(e, 1)]))
                ch(pool.tensor_copy(vst[1], val[1][:, ds(e, 1)]))
                pool.tensor_copy(vst[0][0:CAP_CTX, :], val[0][0:CAP_CTX, ds(e, 1)]).then_inc(S("scales_staged"), 1)
                pool.wait_ge(S("rows_scaled"), e + 1)
                pool.sem_inc(S("pool_turns"), 1)
                for kind in (1, 0):
                    pool.indirect_dma_start(ffn_dram, bass.IndirectOffsetOnAxis(ap=ist_a[kind][:, 0:1], axis=0),
                                            yo[kind][0:CAPS[kind], :], None, compute_op=ALU.add).then_inc(S("rows_added"), 16)
                pool.wait_ge(S("rows_added"), e * 32 + 32)

            for t in range(2):
                pool.wait_ge(S(f"x1_stored{t}"), 32 * (NT // 2))
            gather(0)
            pool.wait_ge(S("ffn_cleared"), 16 * NT)
            with pool.Fori(1, NE) as e:
                ch.enter(e - 1, 5)
                pool.wait_ge(S("slots_turned"), e * 4)
                gather(e)
                add_back(e - 1)
                ch.leave(NE - 1)
            add_back(NE - 1)
            end(pool, "pool")

        def pe_moe(pe):
            begin(pe, "pe", 9)

            def turn_slots(e, q):
                if q == 0:
                    pe.wait_ge(S("rows_gathered"), e * 32 + 32)
                if q >= 2:
                    pe.wait_ge(S("slots_kept_act") if q % 2 == 0 else S("slots_kept_dve"), e * 2 + 1)
                for k in (2 * q, 2 * q + 1):
                    for kind in (1, 0):
                        cap = CAPS[kind]
                        o = (2 + q % 2) * BANK + (k % 2) * CAP + COL[kind]
                        m = pe.transpose(ps[:, o:o + cap], xg[kind][0:cap, k * P:(k + 1) * P], ident[0:cap, 0:cap])
                m.then_inc(S("slots_turned"), 1)

            def turn_rows(e, half):
                if half == 0:
                    pe.wait_ge(S("down_kept"), e * KD + KD)
                    pe.wait_ge(S("slots_kept_act"), e * 2 + 2)
                    pe.wait_ge(S("slots_kept_dve"), e * 2 + 2)
                else:
                    pe.wait_ge(S("rows_half_scaled"), e + 1)
                for k in range(4 * half, 4 * half + 4):
                    o = (k % 4) * P
                    pe.transpose(ps[:, 2 * BANK + o:2 * BANK + o + P], yT[:, k, 0:CAP_LAT], ident[:, :])
                    m = pe.transpose(ps[0:CAP_CTX, 3 * BANK + o:3 * BANK + o + P], yT[:, k, CAP_LAT:CAP], ident[:, :])
                m.then_inc(S("rows_turned"), 1)

            def up(e, rows):
                pe.wait_ge(S("slots_kept_act"), e * 2 + 2)
                pe.wait_ge(S("slots_kept_dve"), e * 2 + 2)
                for f in range(KD):
                    if f % 4 == 0:
                        for a in range(2):
                            pe.wait_ge(S(f"expert_landed{a}{f // 4}"), e * 16 + 16)
                    for a in range(2):
                        if a == 0 and (rows or f >= 2):
                            pe.wait_ge(S("hidden_made"), e * KD + (f - 1))
                        for k in range(KD):
                            m = pe.matmul(bank(4 + 2 * a + f % 2, CAP), We[a][:, k, f * P:(f + 1) * P], xe[:, k, :], start=(k == 0), stop=(k == KD - 1))
                        m.then_inc(S(f"up_done{a}"), 1)
                    if rows and f < 2:
                        turn_rows(e - 1, f)

            def down(e, slots_too):
                pe.wait_ge(S("hidden_made"), e * KD + (KD - 1))
                for d in range(KD):
                    if d % 4 == 0:
                        pe.wait_ge(S(f"expert_landed2{d // 4}"), e * 16 + 16)
                    if d >= 2:
                        pe.wait_ge(S("down_kept"), e * KD + (d - 1))
                    for k in range(KD):
                        if d == 0 and k == KD - 1:
                            pe.wait_ge(S("hidden_made"), e * KD + KD)
                        m = pe.matmul(bank(d % 2, CAP), We[2][:, k, d * P:(d + 1) * P], hid[:, k, :], start=(k == 0), stop=(k == KD - 1))
                    m.then_inc(S("down_done"), 1)
                    if slots_too and d < 4:
                        turn_slots(e + 1, d)

            for q in range(4):
                turn_slots(0, q)
            up(0, False)
            with pe.Fori(1, NE) as e:
                down(e - 1, True)
                up(e, True)
            down(NE - 1, False)
            for half in range(2):
                turn_rows(NE - 1, half)
            end(pe, "pe")

        def slots(q):
            for k in (2 * q, 2 * q + 1):
                for kind in (1, 0):
                    o = (2 + q % 2) * BANK + (k % 2) * CAP + COL[kind]
                    yield xe[:, k, COL[kind]:COL[kind] + CAPS[kind]], ps[:, o:o + CAPS[kind]], k, kind

        def act_moe(act, ch):
            begin(act, "act", 9)

            def keep_slots(e, q):
                act.wait_ge(S("slots_turned"), e * 4 + (q + 1))
                for dst, src, k, kind in slots(q):
                    ch(act.activation(dst, src, ACT.Identity, scale=A2[:, k, kind:kind + 1], bias=modT[:, 24 + k, kind:kind + 1]))
                act.sem_inc(S("slots_kept_act"), 1)

            def gates(e):
                for f in range(KD):
                    act.wait_ge(S("up_done0"), e * KD + (f + 1))
                    if f >= 2:
                        act.wait_ge(S("hidden_made"), e * KD + (f - 1))
                    act.activation(sl[f % 2], bank(4 + f % 2, CAP), ACT.Silu).then_inc(S("silu_made"), 1)
                    act.wait_ge(S("silu_made"), e * KD + (f + 1))

            def keep_down(e, slots_too):
                for d in range(KD):
                    act.wait_ge(S("down_done"), e * KD + (d + 1))
                    act.activation(yT[:, d, :], bank(d % 2, CAP), ACT.Copy).then_inc(S("down_kept"), 1)
                    act.wait_ge(S("down_kept"), e * KD + (d + 1))
                    if slots_too and d in (0, 2):
                        keep_slots(e + 1, d)

            keep_slots(0, 0)
            keep_slots(0, 2)
            gates(0)
            with act.Fori(1, NE) as e:
                ch.enter(e - 1, 8)
                keep_down(e - 1, True)
                gates(e)
                ch.leave(NE - 1)
            keep_down(NE - 1, False)
            end(act, "act")

        def dve_moe(dve, ch):
            begin(dve, "dve", 9)

            def keep_slots(e, q):
                dve.wait_ge(S("slots_turned"), e * 4 + (q + 1))
                for dst, src, k, kind in slots(q):
                    ch(dve.tensor_scalar(dst, src, A2[:, k, kind:kind + 1], modT[:, 24 + k, kind:kind + 1], ALU.mult, ALU.add))
                dve.sem_inc(S("slots_kept_dve"), 1)

            def scale_rows(e, half):
                if half == 0:
                    dve.wait_ge(S("scales_staged"), e + 1)
                dve.wait_ge(S("rows_turned"), e * 2 + (half + 1))
                o = slice(half * BLK, (half + 1) * BLK)
                ch(dve.tensor_scalar(yo[1][:, o], bank(2), vst[1], None, ALU.mult))
                ch(dve.tensor_scalar(yo[0][0:CAP_CTX, o], bank(3, BANK, CAP_CTX), vst[0][0:CAP_CTX, :], None, ALU.mult))
                dve.sem_inc(S("rows_half_scaled" if half == 0 else "rows_scaled"), 1)

            def hidden(e, rows):
                for f in range(KD):
                    dve.wait_ge(S("silu_made"), e * KD + (f + 1))
                    dve.wait_ge(S("up_done1"), e * KD + (f + 1))
                    dve.tensor_tensor(hid[:, f, :], sl[f % 2], bank(6 + f % 2, CAP), ALU.mult).then_inc(S("hidden_made"), 1)
                    dve.wait_ge(S("hidden_made"), e * KD + (f + 1))
                    if rows and f < 2:
                        scale_rows(e - 1, f)

            keep_slots(0, 1)
            keep_slots(0, 3)
            hidden(0, False)
            with dve.Fori(1, NE) as e:
                ch.enter(e - 1, 8 + 4)
                keep_slots(e, 1)
                keep_slots(e, 3)
                hidden(e, True)
                ch.leave(NE - 1)
            for half in range(2):
                scale_rows(NE - 1, half)
            end(dve, "dve")

        ff = R2[:, :].rearrange("p (t d) -> p t d", t=NT)
        sqf = work(D, at=64)
        landed_before = [0] * 3 + [NT // 2] * 2
        sf_, vf, rf = st[:, 0:10], st[:, 10:20], st[:, 20:30]

        def sp_final(sp):
            begin(sp, "sp", 10)

            for a in range(0, NT, 2):
                sp.dma_start(ff[:, a:a + 2, :], ffn_dram[a * P:(a + 2) * P, :].rearrange("(t p) d -> p t d", p=P)).then_inc(S(f"rows_landed{a // 2}"), 16)
            for t in range(NT):
                sp.wait_ge(S(f"y_made{t % 2}"), t // 2 + 1)
                sp.dma_start(y_rows(t), ff[:, t, :]).then_inc(S("y_stored"), 16)
            sp.wait_ge(S("y_stored"), 16 * NT)
            sp.wait_ge(S("ctx_state_stored"), 32 * GH)
            sp.wait_ge(S("new_k_stored"), 16 * 2 * HKV * T_CTX)

        def pe_final(pe):
            begin(pe, "pe", 10)
            end(pe, "pe")

        def act_final(act, ch):
            begin(act, "act", 10)
            for t in range(NT):
                act.wait_ge(S(f"rows_landed{t // 2}"), 16 * (landed_before[t // 2] + 1))
                act.activation(sqf, ff[:, t, :], ACT.Square, accum_out=sf_[:, t:t + 1]).then_inc(S("x_sumsq"), 1)
                act.wait_ge(S("x_sumsq"), NT + t + 1)
            end(act, "act")

        def pool_final(pool, ch):
            begin(pool, "pool", 10)
            pool.wait_ge(S("x1_back"), 16)

            def add(t):
                pool.wait_ge(S("ffn_scaled"), t // 2 + 1)
                pool.tensor_tensor(ff[:, t, :], ff[:, t, :], x1r[:, t, :], ALU.add).then_inc(S("y_made0"), 1)
            for t in range(NT):
                pool.wait_ge(S("x_sumsq"), NT + t + 1)
                ch(pool.tensor_scalar(vf[:, t:t + 1], sf_[:, t:t + 1], 1.0 / D, EPS, ALU.mult, ALU.add))
                pool.tensor_tensor(rf[:, t:t + 1], vf[:, t:t + 1], mhalf[:, 0:1], ALU.pow).then_inc(S("x_rstd"), 1)
                if t % 2 == 1:
                    add(t - 1)
            end(pool, "pool")

        def dve_final(dve, ch):
            begin(dve, "dve", 10)
            dve.wait_ge(S("x1_back"), 16)
            for t in range(NT):
                j = kind_of(t)
                dve.wait_ge(S("x_rstd"), NT + t + 1)
                m = dve.scalar_tensor_tensor(ff[:, t, :], ff[:, t, :], rf[:, t:t + 1], G2b[j], ALU.mult, ALU.mult)
                if t % 2 == 0:
                    m.then_inc(S("ffn_scaled"), 1)
                else:
                    ch(m)
                    dve.tensor_tensor(ff[:, t, :], ff[:, t, :], x1r[:, t, :], ALU.add).then_inc(S("y_made1"), 1)
            end(dve, "dve")

        STAGES_SP = [sp_mod, sp_qkv, sp_attn, sp_ma, sp_gla, sp_mb, sp_out, sp_topk, sp_moe, sp_final]
        STAGES_PE = [pe_mod, pe_qkv, pe_attn, pe_ma, pe_gla, pe_mb, pe_out, pe_topk, pe_moe, pe_final]
        STAGES_ACT = [act_mod, act_qkv, act_attn, act_ma, act_gla, act_mb, act_out, act_topk, act_moe, act_final]
        STAGES_DVE = [dve_mod, dve_qkv, dve_attn, dve_ma, dve_gla, dve_mb, dve_out, dve_topk, dve_moe, dve_final]
        STAGES_POOL = [pool_mod, pool_qkv, pool_attn, pool_idle(4), pool_gla, pool_idle(6), pool_out,
                       pool_idle(8), pool_moe, pool_final]

        @block.sync
        def _(sp):
            for f in STAGES_SP:
                f(sp)

        @block.tensor
        def _(pe):
            for f in STAGES_PE:
                f(pe)

        @block.scalar
        def _(act):
            ch = Chain(act, S("act_chain"))
            for f in STAGES_ACT:
                f(act, ch)

        @block.vector
        def _(dve):
            ch = Chain(dve, S("dve_chain"))
            for f in STAGES_DVE:
                f(dve, ch)

        @block.gpsimd
        def _(pool):
            ch = Chain(pool, S("pool_chain"))
            for f in STAGES_POOL:
                f(pool, ch)


_INS = ["x_prompt", "x_sample", "cache_k", "cache_v", "state_gla_fwd", "state_gla_bwd", "c", "c_ctx",
        "g_pre_mix", "g_post_mix", "g_pre_ffn", "g_post_ffn", "w_mod", "b_mod", "w_in", "g_q", "g_k",
        "w_gk2_f", "b_gk_f", "w_gk2_b", "b_gk_b", "g_gla", "w_pa", "w_pg", "w_out", "w_router", "w1", "w3", "w2"]
_OUTS = [(1, N_CTX, D), (1, N_LAT, D), (1, 1, HKV, N_CTX, HD), (1, 1, HKV, N_CTX, HD), (1, 1, GH, DK, DV), (1, 1, GH, DK, DV)]


def host_consts():
    import numpy as np
    i = np.arange(128)
    same = (i[:, None] // 64) == (i[None, :] // 64)
    upto, after = i[:, None] <= i[None, :], i[:, None] > i[None, :]
    since, before = i[:, None] >= i[None, :], i[:, None] < i[None, :]
    chunk = (i[:, None] // 64) == np.arange(2)[None, :]
    masks = np.concatenate([same & upto, same & after, same & since, same & before, chunk], axis=1).astype(np.float32)
    keep = np.concatenate([same & upto, same & since], axis=1).astype(np.int32)
    freqs = np.float32(10000.0) ** (-np.arange(32, dtype=np.float32) / np.float32(32))
    r = np.repeat(np.arange(16), 64).astype(np.float32)
    col = np.tile(np.arange(64), 16).astype(np.float32)
    ang = np.concatenate([r[:, None] * freqs, col[:, None] * freqs], axis=-1).astype(np.float32)
    rope = np.stack([np.cos(ang), np.sin(ang)]).astype(np.float32)
    return {"k_ident": np.eye(128, dtype=np.float32), "k_masks": masks, "k_keep": keep, "k_rope": rope}


def kernel(**inputs):
    import numpy as _np
    import concourse.bacc as _bacc
    from concourse import mybir as _mybir
    from concourse.bass_utils import run_bass_kernel_spmd as _run

    nc = _bacc.Bacc("TRN2", target_bir_lowering=False, num_devices=1)
    arrays, args = {}, []
    given = {name: _np.ascontiguousarray(inputs[name]) for name in _INS}
    given.update(host_consts())
    for name, a in given.items():
        arrays[f"in_{name}_dram"] = a
        args.append(nc.dram_tensor(f"in_{name}_dram", a.shape, _mybir.dt.from_np(a.dtype), kind="ExternalInput").ap())
    for i, shape in enumerate(_OUTS):
        args.append(nc.dram_tensor(f"out_{i}_dram", shape, F32, kind="ExternalOutput").ap())
    build_program(nc, *args)
    r = _run(nc, [arrays], core_ids=[0])
    return tuple(r.results[0][f"out_{i}_dram"] for i in range(len(_OUTS)))
```
